# Optimizing a Trainium2 kernel written in Bass

```python
import jax, jax.numpy as jnp
from jax import lax
import numpy as np

D_MODEL = 1024
BATCH = 1
SEQ = 256
DEPTH = 2

MLA_HEADS = 8
MLA_NOPE_DIM = 64
MLA_ROPE_DIM = 32
MLA_V_DIM = 64
MLA_Q_RANK = 384
MLA_KV_RANK = 256
MLA_QK_DIM = MLA_NOPE_DIM + MLA_ROPE_DIM
MOBA_HEADS = 8
MOBA_HEAD_DIM = 64
MOBA_WIDTH = MOBA_HEADS * MOBA_HEAD_DIM
MOBA_BLOCK = 256
MOBA_TOPK = 3
MOBA_Q_CHUNK = 16
CONV_CH = 512
CONV_WIDTH = 31
D_FF = 2816
FFN_CONV_WIDTH = 3
ATTN_Q_BLOCK = 128
ROPE_THETA = 10000.0
NORM_EPS = 1e-6
N_BRANCH = 3
D_IN = MLA_Q_RANK + MLA_KV_RANK + MLA_ROPE_DIM + 3 * MOBA_WIDTH + 2 * CONV_CH + N_BRANCH * D_MODEL


def rms_norm(x, g):
    xf = x.astype(jnp.float32)
    y = xf * lax.rsqrt(jnp.mean(xf * xf, axis=-1, keepdims=True) + NORM_EPS)
    return (y * g.astype(jnp.float32)).astype(x.dtype)

def layer_norm(x, g, b):
    xf = x.astype(jnp.float32)
    mu = jnp.mean(xf, axis=-1, keepdims=True)
    var = jnp.mean(jnp.square(xf - mu), axis=-1, keepdims=True)
    y = (xf - mu) * lax.rsqrt(var + NORM_EPS) * g.astype(jnp.float32) + b.astype(jnp.float32)
    return y.astype(x.dtype)

def rope_tables(positions, dim):
    inv_freq = 1.0 / (ROPE_THETA ** (jnp.arange(0, dim, 2, dtype=jnp.float32) / dim))
    ang = positions.astype(jnp.float32)[..., None] * inv_freq
    return jnp.cos(ang), jnp.sin(ang)

def apply_rope(x, cos, sin):
    xf = x.astype(jnp.float32)
    x1, x2 = jnp.split(xf, 2, axis=-1)
    c, s = cos[:, None], sin[:, None]
    return jnp.concatenate([x1 * c - x2 * s, x2 * c + x1 * s], axis=-1).astype(x.dtype)

def causal_depthwise_conv(x, w, b):
    width = w.shape[0]
    y = lax.conv_general_dilated(
        x, w[:, None, :].astype(x.dtype), window_strides=(1,), padding=[(width - 1, 0)],
        dimension_numbers=('NWC', 'WIO', 'NWC'), feature_group_count=x.shape[-1])
    return y + b

def modulate(h, shift, scale):
    return h * (1.0 + scale[:, None, :]) + shift[:, None, :]

def causal_attention(q, k, v):
    B, H, S, dqk = q.shape
    dv = v.shape[-1]
    nqb = S // ATTN_Q_BLOCK
    scale = dqk ** -0.5
    q_blocks = q.reshape(B, H, nqb, ATTN_Q_BLOCK, dqk).transpose(2, 0, 1, 3, 4)
    kpos = jnp.arange(S)

    def one_block(args):
        qb, bi = args
        s = jnp.einsum('bhqd,bhkd->bhqk', qb, k).astype(jnp.float32) * scale
        qpos = bi * ATTN_Q_BLOCK + jnp.arange(ATTN_Q_BLOCK)
        s = jnp.where(kpos[None, :] <= qpos[:, None], s, -jnp.inf)
        p = jax.nn.softmax(s, axis=-1).astype(v.dtype)
        return jnp.einsum('bhqk,bhkd->bhqd', p, v)

    o = lax.map(one_block, (q_blocks, jnp.arange(nqb)))
    return o.transpose(1, 2, 0, 3, 4).reshape(B, H, S, dv)

def moba_attention(q, k, v):
    B, H, S, d = q.shape
    nb = -(-S // MOBA_BLOCK)
    s_pad = nb * MOBA_BLOCK
    pad = [(0, 0), (0, 0), (0, s_pad - S), (0, 0)]
    q, k, v = jnp.pad(q, pad), jnp.pad(k, pad), jnp.pad(v, pad)
    k_blocks = k.reshape(B, H, nb, MOBA_BLOCK, d)
    v_blocks = v.reshape(B, H, nb, MOBA_BLOCK, d)
    k_mean = jnp.mean(k_blocks.astype(jnp.float32), axis=3)
    block_score = jnp.einsum('bhsd,bhnd->bhsn', q.astype(jnp.float32), k_mean)
    q_blk = jnp.arange(s_pad) // MOBA_BLOCK
    fully_past = jnp.arange(nb)[None, :] < q_blk[:, None]
    block_score = jnp.where(fully_past[None, None], block_score, -jnp.inf)
    topk = min(MOBA_TOPK, nb)
    _, sel = lax.top_k(block_score, topk)

    nc = s_pad // MOBA_Q_CHUNK
    q_c = q.reshape(B, H, nc, MOBA_Q_CHUNK, d).transpose(2, 0, 1, 3, 4)
    sel_c = sel.reshape(B, H, nc, MOBA_Q_CHUNK, topk).transpose(2, 0, 1, 3, 4)
    b_idx = jnp.arange(B)[:, None, None, None]
    h_idx = jnp.arange(H)[None, :, None, None]
    jpos = jnp.arange(MOBA_BLOCK)
    scale = d ** -0.5

    def one_chunk(args):
        qc, sc, ci = args
        qpos = ci * MOBA_Q_CHUNK + jnp.arange(MOBA_Q_CHUNK)
        own = (ci * MOBA_Q_CHUNK) // MOBA_BLOCK
        k_sel = k_blocks[b_idx, h_idx, sc]
        v_sel = v_blocks[b_idx, h_idx, sc]
        s_sel = jnp.einsum('bhqd,bhqnjd->bhqnj', qc, k_sel).astype(jnp.float32) * scale
        valid = jnp.arange(topk)[None, :] < (qpos // MOBA_BLOCK)[:, None]
        s_sel = jnp.where(valid[None, None, :, :, None], s_sel, -jnp.inf)
        k_own = lax.dynamic_index_in_dim(k_blocks, own, axis=2, keepdims=False)
        v_own = lax.dynamic_index_in_dim(v_blocks, own, axis=2, keepdims=False)
        s_own = jnp.einsum('bhqd,bhjd->bhqj', qc, k_own).astype(jnp.float32) * scale
        causal = own * MOBA_BLOCK + jpos[None, :] <= qpos[:, None]
        s_own = jnp.where(causal[None, None], s_own, -jnp.inf)
        s_all = jnp.concatenate([s_sel.reshape(B, H, MOBA_Q_CHUNK, topk * MOBA_BLOCK), s_own], axis=-1)
        p = jax.nn.softmax(s_all, axis=-1).astype(v.dtype)
        p_sel = p[..., :topk * MOBA_BLOCK].reshape(B, H, MOBA_Q_CHUNK, topk, MOBA_BLOCK)
        p_own = p[..., topk * MOBA_BLOCK:]
        return (jnp.einsum('bhqnj,bhqnjd->bhqd', p_sel, v_sel)
                + jnp.einsum('bhqj,bhjd->bhqd', p_own, v_own))

    o = lax.map(one_chunk, (q_c, sel_c, jnp.arange(nc)))
    return o.transpose(1, 2, 0, 3, 4).reshape(B, H, s_pad, d)[:, :, :S]

def token_mixer(h, cos_a, sin_a, cos_b, sin_b, w_in,
                mla_q_norm_g, w_uq, mla_kv_norm_g, w_ukv,
                mla_qn_nope_g, mla_qn_rope_g, mla_kn_nope_g, mla_kn_rope_g, w_mla_o,
                moba_qn_g, moba_kn_g, w_moba_o,
                conv_dw_w, conv_dw_b, conv_ln_g, conv_ln_b, w_conv_pw2, b_conv_pw2,
                w_out):
    B, S, _ = h.shape
    z = h @ w_in
    sizes = (MLA_Q_RANK, MLA_KV_RANK, MLA_ROPE_DIM, 3 * MOBA_WIDTH, 2 * CONV_CH, N_BRANCH * D_MODEL)
    q_lat, kv_lat, k_rope, qkv_b, conv_in, gate_logits = jnp.split(
        z, np.cumsum(sizes)[:-1].tolist(), axis=-1)

    q_a = (rms_norm(q_lat, mla_q_norm_g) @ w_uq).reshape(B, S, MLA_HEADS, MLA_QK_DIM).transpose(0, 2, 1, 3)
    q_nope = rms_norm(q_a[..., :MLA_NOPE_DIM], mla_qn_nope_g)
    q_pe = apply_rope(rms_norm(q_a[..., MLA_NOPE_DIM:], mla_qn_rope_g), cos_a, sin_a)
    kv = (rms_norm(kv_lat, mla_kv_norm_g) @ w_ukv).reshape(
        B, S, MLA_HEADS, MLA_NOPE_DIM + MLA_V_DIM).transpose(0, 2, 1, 3)
    k_nope = rms_norm(kv[..., :MLA_NOPE_DIM], mla_kn_nope_g)
    v_a = kv[..., MLA_NOPE_DIM:]
    k_pe = apply_rope(rms_norm(k_rope, mla_kn_rope_g)[:, None], cos_a, sin_a)
    q_full = jnp.concatenate([q_nope, q_pe], axis=-1)
    k_full = jnp.concatenate([k_nope, jnp.broadcast_to(k_pe, (B, MLA_HEADS, S, MLA_ROPE_DIM))], axis=-1)
    o_a = causal_attention(q_full, k_full, v_a)
    o_a = o_a.transpose(0, 2, 1, 3).reshape(B, S, MLA_HEADS * MLA_V_DIM) @ w_mla_o

    qkv = qkv_b.reshape(B, S, 3, MOBA_HEADS, MOBA_HEAD_DIM).transpose(2, 0, 3, 1, 4)
    q_b = apply_rope(rms_norm(qkv[0], moba_qn_g), cos_b, sin_b)
    k_b = apply_rope(rms_norm(qkv[1], moba_kn_g), cos_b, sin_b)
    o_b = moba_attention(q_b, k_b, qkv[2])
    o_b = o_b.transpose(0, 2, 1, 3).reshape(B, S, MOBA_WIDTH) @ w_moba_o

    glu_a, glu_g = jnp.split(conv_in, 2, axis=-1)
    u = glu_a * jax.nn.sigmoid(glu_g)
    u = causal_depthwise_conv(u, conv_dw_w, conv_dw_b)
    u = jax.nn.silu(layer_norm(u, conv_ln_g, conv_ln_b))
    o_c = u @ w_conv_pw2 + b_conv_pw2

    g = jax.nn.sigmoid(gate_logits.reshape(B, S, N_BRANCH, D_MODEL))
    merged = g[:, :, 0] * o_a + g[:, :, 1] * o_b + g[:, :, 2] * o_c
    return merged @ w_out

def channel_mixer(h, w_up, ffn_dw_w, ffn_dw_b, w_down):
    u = causal_depthwise_conv(h @ w_up, ffn_dw_w, ffn_dw_b)
    a, b = jnp.split(u, 2, axis=-1)
    return (jax.nn.silu(a) * b) @ w_down

def first_inputs(seed: int = 0) -> dict:
    key = jax.random.key(seed)
    ks = iter(jax.random.split(key, 48))
    L = DEPTH

    def nrm(shape, fan_in):
        return jax.random.normal(next(ks), shape, jnp.float32) * (fan_in ** -0.5)

    def gain(shape):
        return 1.0 + 0.02 * jax.random.normal(next(ks), shape, jnp.float32)

    def bias(shape):
        return 0.01 * jax.random.normal(next(ks), shape, jnp.float32)

    x = jax.random.normal(next(ks), (BATCH, SEQ, D_MODEL), jnp.float32)
    c = jax.random.normal(next(ks), (BATCH, D_MODEL), jnp.float32)
    offset = jax.random.randint(next(ks), (BATCH, 1), 0, 1024, dtype=jnp.int32)
    positions = (offset + jnp.arange(SEQ, dtype=jnp.int32)[None, :]).astype(jnp.int32)
    return {
        'x': x, 'c': c, 'positions': positions,
        'w_mod': nrm((L, D_MODEL, 6 * D_MODEL), D_MODEL), 'b_mod': bias((L, 6 * D_MODEL)),
        'mix_norm_g': gain((L, D_MODEL)), 'w_in': nrm((L, D_MODEL, D_IN), D_MODEL),
        'mla_q_norm_g': gain((L, MLA_Q_RANK)),
        'w_uq': nrm((L, MLA_Q_RANK, MLA_HEADS * MLA_QK_DIM), MLA_Q_RANK),
        'mla_kv_norm_g': gain((L, MLA_KV_RANK)),
        'w_ukv': nrm((L, MLA_KV_RANK, MLA_HEADS * (MLA_NOPE_DIM + MLA_V_DIM)), MLA_KV_RANK),
        'mla_qn_nope_g': gain((L, MLA_NOPE_DIM)), 'mla_qn_rope_g': gain((L, MLA_ROPE_DIM)),
        'mla_kn_nope_g': gain((L, MLA_NOPE_DIM)), 'mla_kn_rope_g': gain((L, MLA_ROPE_DIM)),
        'w_mla_o': nrm((L, MLA_HEADS * MLA_V_DIM, D_MODEL), MLA_HEADS * MLA_V_DIM),
        'moba_qn_g': gain((L, MOBA_HEAD_DIM)), 'moba_kn_g': gain((L, MOBA_HEAD_DIM)),
        'w_moba_o': nrm((L, MOBA_WIDTH, D_MODEL), MOBA_WIDTH),
        'conv_dw_w': nrm((L, CONV_WIDTH, CONV_CH), CONV_WIDTH), 'conv_dw_b': bias((L, CONV_CH)),
        'conv_ln_g': gain((L, CONV_CH)), 'conv_ln_b': bias((L, CONV_CH)),
        'w_conv_pw2': nrm((L, CONV_CH, D_MODEL), CONV_CH), 'b_conv_pw2': bias((L, D_MODEL)),
        'w_out': nrm((L, D_MODEL, D_MODEL), D_MODEL),
        'ffn_norm_g': gain((L, D_MODEL)), 'w_up': nrm((L, D_MODEL, 2 * D_FF), D_MODEL),
        'ffn_dw_w': nrm((L, FFN_CONV_WIDTH, 2 * D_FF), FFN_CONV_WIDTH), 'ffn_dw_b': bias((L, 2 * D_FF)),
        'w_down': nrm((L, D_FF, D_MODEL), D_FF),
    }

def first_block(x, c, positions, w_mod, b_mod, mix_norm_g, w_in,
              mla_q_norm_g, w_uq, mla_kv_norm_g, w_ukv,
              mla_qn_nope_g, mla_qn_rope_g, mla_kn_nope_g, mla_kn_rope_g, w_mla_o,
              moba_qn_g, moba_kn_g, w_moba_o,
              conv_dw_w, conv_dw_b, conv_ln_g, conv_ln_b, w_conv_pw2, b_conv_pw2,
              w_out, ffn_norm_g, w_up, ffn_dw_w, ffn_dw_b, w_down):
    cos_a, sin_a = rope_tables(positions, MLA_ROPE_DIM)
    cos_b, sin_b = rope_tables(positions, MOBA_HEAD_DIM)
    c_act = jax.nn.silu(c)
    for l in range(DEPTH):
        mod = c_act @ w_mod[l] + b_mod[l]
        sh1, sc1, g1, sh2, sc2, g2 = jnp.split(mod, 6, axis=-1)
        h = modulate(rms_norm(x, mix_norm_g[l]), sh1, sc1)
        y = token_mixer(h, cos_a, sin_a, cos_b, sin_b, w_in[l],
                        mla_q_norm_g[l], w_uq[l], mla_kv_norm_g[l], w_ukv[l],
                        mla_qn_nope_g[l], mla_qn_rope_g[l], mla_kn_nope_g[l], mla_kn_rope_g[l], w_mla_o[l],
                        moba_qn_g[l], moba_kn_g[l], w_moba_o[l],
                        conv_dw_w[l], conv_dw_b[l], conv_ln_g[l], conv_ln_b[l], w_conv_pw2[l], b_conv_pw2[l],
                        w_out[l])
        x = x + g1[:, None, :] * y
        h = modulate(rms_norm(x, ffn_norm_g[l]), sh2, sc2)
        x = x + g2[:, None, :] * channel_mixer(h, w_up[l], ffn_dw_w[l], ffn_dw_b[l], w_down[l])
    return x


GRID_W = 64
CTX_LEN = 256
D_FF_2 = 2752
N_MOD = 9
EPS = 1e-6
D_FOURIER = D_MODEL // 2
FOURIER_CH = 128
FOURIER_GROUPS = D_FOURIER // FOURIER_CH
D_SGU = D_MODEL // 2
SGU_CH = 128
SGU_GROUPS = D_SGU // SGU_CH
CHUNK = 128
HEAD_DIM = 128
N_HEADS = D_MODEL // HEAD_DIM
N_KV_HEADS = 2
GROUP = N_HEADS // N_KV_HEADS
ROPE_AXIS_DIM = HEAD_DIM // 2
Q_BLOCK = 128


def rms_norm_2(x, g):
    xf = x.astype(jnp.float32)
    y = xf * lax.rsqrt(jnp.mean(jnp.square(xf), axis=-1, keepdims=True) + EPS)
    return (y * g.astype(jnp.float32)).astype(x.dtype)

def adaln(cvec, w_mod, b_mod):
    m = jax.nn.silu(cvec) @ w_mod + b_mod
    m = m.reshape(m.shape[0], 1, N_MOD, D_MODEL)
    return [m[:, :, i] for i in range(N_MOD)]

def modulated_norm(x, g, shift, scale):
    return rms_norm_2(x, g) * (1 + scale) + shift

def swiglu(h, w_gu, w_down):
    gate, up = jnp.split(h @ w_gu, 2, axis=-1)
    return (jax.nn.silu(gate) * up) @ w_down

def ffn_half_step(x, mods, g, w_gu, w_down):
    shift, scale, gate = mods
    return x + 0.5 * gate * swiglu(modulated_norm(x, g, shift, scale), w_gu, w_down)

def fourier_mix(a):
    b_, n, _ = a.shape
    a4 = a.reshape(b_, n, FOURIER_GROUPS, FOURIER_CH).astype(jnp.float32)
    f = jnp.fft.fftn(a4, axes=(1, 3), norm="ortho").real
    return f.reshape(b_, n, D_FOURIER).astype(a.dtype)

def chunk_sgu(u, v, g_v, w_s, b_s):
    b_, n, _ = v.shape
    vh = rms_norm_2(v.reshape(b_, n, SGU_GROUPS, SGU_CH), g_v)
    vc = vh.reshape(b_, n // CHUNK, CHUNK, SGU_GROUPS, SGU_CH)
    mixed = jnp.einsum('hpq,bcqhd->bcphd', w_s, vc) + b_s.T[None, None, :, :, None]
    return u * mixed.reshape(b_, n, D_SGU)

def fourier_sgu_mixer(h, w_in, g_v, w_s, b_s, w_out):
    a, uv = jnp.split(h @ w_in, [D_FOURIER], axis=-1)
    u, v = jnp.split(jax.nn.gelu(uv), 2, axis=-1)
    out = jnp.concatenate([fourier_mix(a), chunk_sgu(u, v, g_v, w_s, b_s)], axis=-1)
    return out @ w_out

def axial_angles(rows):
    row = jnp.repeat(jnp.arange(rows, dtype=jnp.float32), GRID_W)
    col = jnp.tile(jnp.arange(GRID_W, dtype=jnp.float32), rows)
    inv_freq = ROPE_THETA ** (-jnp.arange(0, ROPE_AXIS_DIM, 2, dtype=jnp.float32) / ROPE_AXIS_DIM)
    return row[:, None] * inv_freq, col[:, None] * inv_freq

def rotate(x, ang):
    full = jnp.concatenate([ang, ang], axis=-1)[:, None, :]
    cos = jnp.cos(full).astype(x.dtype)
    sin = jnp.sin(full).astype(x.dtype)
    x1, x2 = jnp.split(x, 2, axis=-1)
    return x * cos + jnp.concatenate([-x2, x1], axis=-1) * sin

def axial_rope(x, ang_row, ang_col):
    xr, xc = jnp.split(x, 2, axis=-1)
    return jnp.concatenate([rotate(xr, ang_row), rotate(xc, ang_col)], axis=-1)

def project_kv(kv, g_k):
    b_, n, _ = kv.shape
    k, v = jnp.split(kv, 2, axis=-1)
    k = rms_norm_2(k.reshape(b_, n, N_KV_HEADS, HEAD_DIM), g_k)
    return k, v.reshape(b_, n, N_KV_HEADS, HEAD_DIM)

def project_q(q, g_q):
    b_, n, _ = q.shape
    return rms_norm_2(q.reshape(b_, n, N_HEADS, HEAD_DIM), g_q)

def gqa_attend(q, k, v):
    b_, nq = q.shape[:2]
    qg = q.reshape(b_, nq, N_KV_HEADS, GROUP, HEAD_DIM)
    s = jnp.einsum('bqkgd,bskd->bkgqs', qg, k, preferred_element_type=jnp.float32) * (HEAD_DIM ** -0.5)
    p = jax.nn.softmax(s, axis=-1).astype(v.dtype)
    o = jnp.einsum('bkgqs,bskd->bqkgd', p, v)
    return o.reshape(b_, nq, N_HEADS * HEAD_DIM)

def blocked_attention(q, k_all, v_all):
    b_, n = q.shape[:2]
    n_blk = n // Q_BLOCK
    qb = jnp.moveaxis(q.reshape(b_, n_blk, Q_BLOCK, N_HEADS, HEAD_DIM), 1, 0)
    o = lax.map(lambda qblk: gqa_attend(qblk, k_all, v_all), qb)
    return jnp.moveaxis(o, 0, 1).reshape(b_, n, N_HEADS * HEAD_DIM)

def second_inputs(seed: int = 0) -> dict:
    key = jax.random.key(seed)
    ks = jax.random.split(key, 24)
    n_even = (DEPTH + 1) // 2
    n_odd = DEPTH // 2

    def nrm(k, shape, fan_in, s=1.0):
        return s * jax.random.normal(k, shape, jnp.float32) * (fan_in ** -0.5)

    def gain(k, shape):
        return 1.0 + 0.05 * jax.random.normal(k, shape, jnp.float32)

    return {
        "x": jax.random.normal(ks[0], (BATCH, SEQ, D_MODEL), jnp.float32),
        "c": jax.random.normal(ks[1], (BATCH, D_MODEL), jnp.float32),
        "ctx": jax.random.normal(ks[2], (BATCH, CTX_LEN, D_MODEL), jnp.float32),
        "c_ctx": jax.random.normal(ks[3], (D_MODEL,), jnp.float32),
        "w_mod": nrm(ks[4], (DEPTH, D_MODEL, N_MOD * D_MODEL), D_MODEL, 0.5),
        "b_mod": 0.02 * jax.random.normal(ks[5], (DEPTH, N_MOD * D_MODEL), jnp.float32),
        "g_ffn1": gain(ks[6], (DEPTH, D_MODEL)),
        "w_ffn1_gu": nrm(ks[7], (DEPTH, D_MODEL, 2 * D_FF_2), D_MODEL),
        "w_ffn1_down": nrm(ks[8], (DEPTH, D_FF_2, D_MODEL), D_FF_2),
        "g_mix": gain(ks[9], (DEPTH, D_MODEL)),
        "g_ffn2": gain(ks[10], (DEPTH, D_MODEL)),
        "w_ffn2_gu": nrm(ks[11], (DEPTH, D_MODEL, 2 * D_FF_2), D_MODEL),
        "w_ffn2_down": nrm(ks[12], (DEPTH, D_FF_2, D_MODEL), D_FF_2),
        "g_final": gain(ks[13], (D_MODEL,)),
        "w_in_ab": nrm(ks[14], (n_even, D_MODEL, D_FOURIER + 2 * D_SGU), D_MODEL),
        "g_v": gain(ks[15], (n_even, SGU_GROUPS, SGU_CH)),
        "w_s": nrm(ks[16], (n_even, SGU_GROUPS, CHUNK, CHUNK), CHUNK, 0.5),
        "b_s": 1.0 + 0.02 * jax.random.normal(ks[17], (n_even, SGU_GROUPS, CHUNK), jnp.float32),
        "w_out_ab": nrm(ks[18], (n_even, D_FOURIER + D_SGU, D_MODEL), D_FOURIER + D_SGU),
        "w_qkv": nrm(ks[19], (n_odd, D_MODEL, (N_HEADS + 2 * N_KV_HEADS) * HEAD_DIM), D_MODEL),
        "g_q": gain(ks[20], (n_odd, HEAD_DIM)),
        "g_k": gain(ks[21], (n_odd, HEAD_DIM)),
        "w_o": nrm(ks[22], (n_odd, N_HEADS * HEAD_DIM, D_MODEL), N_HEADS * HEAD_DIM),
    }

def second_block(x, c, ctx, c_ctx, w_mod, b_mod, g_ffn1, w_ffn1_gu, w_ffn1_down, g_mix,
              g_ffn2, w_ffn2_gu, w_ffn2_down, g_final, w_in_ab, g_v, w_s, b_s, w_out_ab,
              w_qkv, g_q, g_k, w_o):
    n_tok = x.shape[1]
    ROWS = n_tok // GRID_W
    ang_row, ang_col = axial_angles(ROWS)
    q_cols = N_HEADS * HEAD_DIM

    for l in range(DEPTH):
        last = l == DEPTH - 1
        even = l % 2 == 0
        j = l // 2
        mx = adaln(c, w_mod[l], b_mod[l])
        mc = adaln(c_ctx[None], w_mod[l], b_mod[l])
        ctx_live = (not last) or (not even)

        x = ffn_half_step(x, mx[0:3], g_ffn1[l], w_ffn1_gu[l], w_ffn1_down[l])
        if ctx_live:
            ctx = ffn_half_step(ctx, mc[0:3], g_ffn1[l], w_ffn1_gu[l], w_ffn1_down[l])

        hx = modulated_norm(x, g_mix[l], mx[3], mx[4])
        if even:
            out_x = fourier_sgu_mixer(hx, w_in_ab[j], g_v[j], w_s[j], b_s[j], w_out_ab[j])
            if not last:
                hc = modulated_norm(ctx, g_mix[l], mc[3], mc[4])
                out_c = fourier_sgu_mixer(hc, w_in_ab[j], g_v[j], w_s[j], b_s[j], w_out_ab[j])
        else:
            hc = modulated_norm(ctx, g_mix[l], mc[3], mc[4])
            qkv_x = hx @ w_qkv[j]
            q_x = axial_rope(project_q(qkv_x[..., :q_cols], g_q[j]), ang_row, ang_col)
            k_x, v_x = project_kv(qkv_x[..., q_cols:], g_k[j])
            k_x = axial_rope(k_x, ang_row, ang_col)
            if last:
                k_c, v_c = project_kv(hc @ w_qkv[j][:, q_cols:], g_k[j])
            else:
                qkv_c = hc @ w_qkv[j]
                k_c, v_c = project_kv(qkv_c[..., q_cols:], g_k[j])
                q_c = project_q(qkv_c[..., :q_cols], g_q[j])
                out_c = gqa_attend(q_c, k_c, v_c) @ w_o[j]
            k_all = jnp.concatenate([k_x, k_c], axis=1)
            v_all = jnp.concatenate([v_x, v_c], axis=1)
            out_x = blocked_attention(q_x, k_all, v_all) @ w_o[j]

        x = x + mx[5] * out_x
        x = ffn_half_step(x, mx[6:9], g_ffn2[l], w_ffn2_gu[l], w_ffn2_down[l])
        if not last:
            ctx = ctx + mc[5] * out_c
            ctx = ffn_half_step(ctx, mc[6:9], g_ffn2[l], w_ffn2_gu[l], w_ffn2_down[l])

    return rms_norm_2(x, g_final)


def setup_inputs(seed=0):
    out = dict(first_inputs(seed))
    for name, value in second_inputs(seed + 1).items():
        if name != "x":
            out[name + "_2"] = value
    return out


def reference(
    x, c, positions, w_mod, b_mod, mix_norm_g, w_in, mla_q_norm_g, w_uq, mla_kv_norm_g, w_ukv,
    mla_qn_nope_g, mla_qn_rope_g, mla_kn_nope_g, mla_kn_rope_g, w_mla_o, moba_qn_g, moba_kn_g,
    w_moba_o, conv_dw_w, conv_dw_b, conv_ln_g, conv_ln_b, w_conv_pw2, b_conv_pw2, w_out,
    ffn_norm_g, w_up, ffn_dw_w, ffn_dw_b, w_down, c_2, ctx_2, c_ctx_2, w_mod_2, b_mod_2,
    g_ffn1_2, w_ffn1_gu_2, w_ffn1_down_2, g_mix_2, g_ffn2_2, w_ffn2_gu_2, w_ffn2_down_2,
    g_final_2, w_in_ab_2, g_v_2, w_s_2, b_s_2, w_out_ab_2, w_qkv_2, g_q_2, g_k_2, w_o_2,
):
    x = first_block(
        x, c, positions, w_mod, b_mod, mix_norm_g, w_in, mla_q_norm_g, w_uq, mla_kv_norm_g,
        w_ukv, mla_qn_nope_g, mla_qn_rope_g, mla_kn_nope_g, mla_kn_rope_g, w_mla_o, moba_qn_g,
        moba_kn_g, w_moba_o, conv_dw_w, conv_dw_b, conv_ln_g, conv_ln_b, w_conv_pw2, b_conv_pw2,
        w_out, ffn_norm_g, w_up, ffn_dw_w, ffn_dw_b, w_down,
    )
    return second_block(
        x, c_2, ctx_2, c_ctx_2, w_mod_2, b_mod_2, g_ffn1_2, w_ffn1_gu_2, w_ffn1_down_2, g_mix_2,
        g_ffn2_2, w_ffn2_gu_2, w_ffn2_down_2, g_final_2, w_in_ab_2, g_v_2, w_s_2, b_s_2,
        w_out_ab_2, w_qkv_2, g_q_2, g_k_2, w_o_2,
    )


_drawn_inputs = setup_inputs


def setup_inputs(seed=0):
    import zlib

    import numpy as np

    out = dict(_drawn_inputs(seed))
    spreads = {}
    factors = {'b_mod': 2.763,
     'mix_norm_g': 6.493,
     'mla_q_norm_g': 8.0,
     'mla_kv_norm_g': 8.0,
     'mla_qn_nope_g': 8.0,
     'mla_qn_rope_g': 8.0,
     'mla_kn_nope_g': 8.0,
     'mla_kn_rope_g': 8.0,
     'moba_qn_g': 8.0,
     'moba_kn_g': 8.0,
     'conv_dw_b': 8.0,
     'conv_ln_g': 8.0,
     'conv_ln_b': 8.0,
     'b_conv_pw2': 8.0,
     'ffn_norm_g': 2.932,
     'ffn_dw_b': 6.698,
     'ctx_2': 5.134,
     'b_mod_2': 3.467,
     'g_ffn1_2': 7.798,
     'g_mix_2': 6.854,
     'g_ffn2_2': 7.69,
     'g_v_2': 8.0,
     'b_s_2': 8.0,
     'g_q_2': 8.0,
     'g_k_2': 8.0}
    for name, (base, spread) in spreads.items():
        noise = np.random.default_rng([zlib.crc32(name.encode()), seed]).standard_normal(out[name].shape)
        drawn = base * np.exp(spread * noise) if base else spread * noise
        out[name] = __import__('jax').numpy.asarray(drawn.astype(out[name].dtype))
    for name, factor in factors.items():
        out[name] = (out[name] * factor).astype(out[name].dtype)
    return out
```

```python
from contextlib import ExitStack, contextmanager

import numpy as np
import concourse.bass as bass
from concourse import mybir

P = 128
D = 1024
KD = D // P
SEQ = 256
TOK = 2 * SEQ
DEPTH = 2
D_FF, D_FF_2 = 2816, 2752
FJ = D_FF // P
Q_RANK, KV_RANK, ROPE_A, NOPE = 384, 256, 32, 64
HEADS = 8
CONV_CH, TAPS, FFN_TAPS = 512, 31, 3
CC = CONV_CH // P
NMOD = (6, 9)
NVEC = (1, 2)
GRID_W = 64
THETA = 10000.0
EPS = 1e-6
UB = 16
RING = 4
CYCLE = UB * RING
BANKS = 8
F32 = mybir.dt.float32
I32 = mybir.dt.int32
ALU = mybir.AluOpType
ACT = mybir.ActivationFunctionType
AX = mybir.AxisListType
TWO_PI = (6.28125, 0.0019350051879882812, 3.019916050561733e-07)
MASKED = -1e30


def weight_blocks():
    s = []

    def align(m):
        while len(s) % m:
            s.append(None)

    def linear(name, nk, ns):
        for n in ns:
            for k in range(nk):
                s.append((name, k, n))

    def wide(name, nk, nn):
        align(4)
        for k in range(nk):
            for n in range(nn):
                s.append((name, k, n))

    def ffn(up, down):
        align(UB)
        for j in range(FJ):
            linear(up, KD, (2 * j, 2 * j + 1))
        linear(down, FJ, range(KD))

    def mods(name, b):
        align(UB)
        linear(name, KD, range(NMOD[b] * KD))

    for l in range(DEPTH):
        mods(f"mod1_{l}", 0)
        linear(f"lat_{l}", KD, range(6))
        linear(f"uq_{l}", Q_RANK // P, range(HEADS))
        linear(f"uk_{l}", KV_RANK // P, range(HEADS))
        wide(f"uv_{l}", KV_RANK // P, 4)
        linear(f"qkb_{l}", KD, range(HEADS))
        wide(f"vb_{l}", KD, 4)
        linear(f"conv_{l}", KD, range(2 * CC))
        for m in range(KD):
            linear(f"gate0_{l}", KD, (m,))
            linear(f"gate1_{l}", KD, (m,))
            linear(f"gate2_{l}", KD, (m,))
            linear(f"pw2_{l}", CC, (m,))
            linear(f"oa_{l}", 4, (m,))
            linear(f"ob_{l}", 4, (m,))
        linear(f"out_{l}", KD, range(KD))
        ffn(f"up_{l}", f"down_{l}")
    for l in range(DEPTH):
        mods(f"mod2_{l}", 1)
        ffn(f"f1up_{l}", f"f1down_{l}")
        if l % 2 == 0:
            linear("ain", KD, range(4))
            linear("uin", KD, range(4))
            wide("vin", KD, 4)
            linear("oab", KD, range(KD))
        else:
            linear("q2", KD, range(8))
            linear("k2", KD, range(2))
            wide("v2", KD, 2)
            linear("o2", KD, range(KD))
        ffn(f"f2up_{l}", f"f2down_{l}")
    align(UB)
    return s


def vector_columns():
    at, n = {}, 0
    sizes = [("inv_freq_a", 1), ("inv_freq_b", 1), ("c", KD * 3), ("eps", 1), ("g_final", KD),
             ("gq2", 1), ("gk2", 1)]
    for l in range(DEPTH):
        sizes += [(f"b_mod1_{l}", NMOD[0] * KD), (f"g_mix1_{l}", KD), (f"g_ffn1_{l}", KD),
                  (f"g_qlat_{l}", 3), (f"g_kvlat_{l}", 2), (f"g_qa_{l}", 1), (f"g_ka_{l}", 1),
                  (f"g_qb_{l}", 1), (f"g_kb_{l}", 1), (f"conv_w_{l}", TAPS * CC), (f"conv_b_{l}", CC),
                  (f"ln_g_{l}", CC), (f"ln_b_{l}", CC), (f"pw2_b_{l}", KD),
                  (f"ffn_w_{l}", FFN_TAPS * 2 * FJ), (f"ffn_b_{l}", 2 * FJ),
                  (f"b_mod2_{l}", NMOD[1] * KD * 2), (f"g2_{l}", 3 * KD)]
    for name, size in sizes:
        at[name] = (n, size)
        n += size
    return at, n


CONST_MATS = ("ones_d", "ones_q", "ones_kv", "ones_c", "head_a", "head_b", "head_c",
              "rot_a", "rot_b", "rot_c", "ident", "ws0", "ws1", "ws2", "ws3")
TABLES = (("dft_c", 256), ("cos_n", 512), ("nsin_n", 512), ("cos_c", 512), ("sin_c", 512),
          ("mask", 512), ("g_v", 512), ("b_s", 512))


def const_columns():
    at, n = {}, 0
    for name in CONST_MATS:
        at[name] = (n, P)
        n += P
    for name, size in TABLES:
        at[name] = (n, size)
        n += size
    return at, n


class Steps:

    def __init__(self, known):
        self.known, self.found, self.n, self.loop = known, {}, 0, None

    def mark(self, name=None):
        self.n += 1
        if name is not None:
            assert name not in self.found, name
            self.found[name] = (self.n, self.loop)
        return 1

    def at(self, name, turn=None):
        n, loop = self.known.get(name, (1, None))
        if loop is None:
            return n
        stride, count = self.known[("loop", loop)]
        return n + (count - 1 if turn is None else turn) * stride

    def has(self, name):
        return name in self.known

    def so_far(self, turn=None):
        if self.loop is None:
            return self.n
        return self.n + turn * self.known.get(("loop", self.loop), (1, 1))[0]

    @contextmanager
    def turns(self, engine, name, count):
        start = self.n
        self.loop = name
        with engine.Fori(0, count) as i:
            yield i
        self.loop = None
        stride = self.n - start
        self.found[("loop", name)] = (stride, count)
        self.n = start + stride * count


GU_TURNS = FJ // RING
GU_REST = FJ - GU_TURNS * RING
MOD_OUTS = CYCLE // KD


def build(nc, stream, cols_d, consts_d, x_d, ctx_d, pos_d, out_d, known, bank_of):
    blocks = weight_blocks()
    vcol, vcols = vector_columns()
    ccol, ccols = const_columns()
    T, A, V = (Steps(known.get(e, {})) for e in "TAV")
    new_banks = {}

    ctx = ExitStack()
    with ctx:
        def sb(name, shape, dt=F32):
            return ctx.enter_context(nc.sbuf_tensor(name, shape, dt))

        def sem(name):
            return ctx.enter_context(nc.semaphore(name))

        ring = sb("ring", [P, RING, UB * P])
        x = sb("x_sb", [P, KD, TOK])
        h = sb("h_sb", [P, KD, TOK])
        hid = sb("hid", [P, FJ, TOK])
        cols = sb("cols", [P, vcols])
        consts = sb("consts", [P, ccols])
        silu_c = sb("silu_c", [P, KD, 3])
        mod = sb("mod", [P, NMOD[1] * KD * 2])
        amod = sb("amod", [P, 3, KD, 2])
        rs = sb("rs", [P, TOK])
        qt = sb("qt", [P, HEADS, SEQ])
        kt = sb("kt", [P, HEADS, SEQ])
        sq = sb("sq", [P, HEADS, SEQ])
        hrs = sb("hrs", [P, 2, TOK])
        rt = sb("rt", [P, 2, TOK])
        lat = sb("lat", [P, 6, SEQ])
        va = sb("va", [P, 2, 512])
        vb = sb("vb", [P, 2, 512])
        z = sb("z", [P, 2, 2, SEQ + FFN_TAPS - 1])
        zc = rt[:, :, :].rearrange("p s (a t) -> p s a t", a=2)
        sg = sb("sg", [P, 2, TOK])
        sg2 = sb("sg2", [P, 2, SEQ])
        probs = sb("probs", [P, 2, 512])
        probs_t = sb("probs_t", [P, 2, 512])
        stat = sb("stat", [P, 2, 8])
        cos_a = sb("cos_a", [P, SEQ])
        sin_a = sb("sin_a", [P, SEQ])
        cos_b = sb("cos_b", [P, SEQ])
        sin_b = sb("sin_b", [P, SEQ])
        pos_i = sg2[:, 0, :].bitcast(I32)

        flat = hid[:, :, :].rearrange("p j t -> p (j t)")

        def part(start, n, **dims):
            names = " ".join(dims)
            return flat[:, start:start + n].rearrange(f"p ({names}) -> p {names}", **dims)

        attn = part(0, 8 * SEQ, c=8, t=SEQ)
        u_pad = part(2048, CC * (SEQ + TAPS - 1), c=CC, t=SEQ + TAPS - 1)
        u_end = 2048 + CC * (SEQ + TAPS - 1)
        dwc = part(u_end, CC * SEQ, c=CC, t=SEQ)
        csq = part(u_end + 1024, CC * SEQ, c=CC, t=SEQ)
        oc = part(u_end + 2048, CC * SEQ, c=CC, t=SEQ)
        merged = part(u_end + 3072, KD * SEQ, c=KD, t=SEQ)
        bt = part(u_end + 5120, HEADS * SEQ, c=HEADS, t=SEQ)
        mixed = part(0, KD * TOK, c=KD, t=TOK)
        spec = part(4096, 4 * 4 * 256, t=4, g=4, f=256)
        a_in = part(8192, 4 * TOK, g=4, t=TOK)

        ps = ctx.enter_context(nc.psum_tensor("ps", [P, BANKS, 512], F32))

        tensor_done = sem("tensor_done")
        scalar_done = sem("scalar_done")
        vector_done = sem("vector_done")
        inputs_landed = sem("inputs_landed")
        weights_landed = [sem(f"weights_landed{s}") for s in range(RING)]
        output_stored = sem("output_stored")
        N_IN = 5 * 16

        def col(name, k=0, n=1):
            return cols[:, vcol[name][0] + k:vcol[name][0] + k + n]

        def mat(name):
            return consts[:, ccol[name][0]:ccol[name][0] + ccol[name][1]]

        def bank(g):
            return ps[:, bank_of.get(g, 0), :]

        block = ctx.enter_context(nc.Block())

        units = len(blocks) // UB
        loops = {}
        for b, name, turns in loop_starts(blocks):
            loops[b // UB] = (name, turns)

        @block.sync
        def _(sp):
            sp.dma_start(cols[:, :], cols_d).then_inc(inputs_landed, 16)
            sp.dma_start(pos_i[:, :], pos_d).then_inc(inputs_landed, 16)

            def load(u, slot):
                sp.dma_start(ring[:, slot, :], stream[u, :, :]).then_inc(weights_landed[slot], 16)

            def slot_read(u):
                if u >= RING:
                    name, turn = unit_step(u - RING)
                    sp.wait_ge(tensor_done, T.at(name, turn))

            def unit_step(u):
                for u0, (name, turns) in loops.items():
                    if u0 <= u < u0 + turns * RING:
                        return ("unit", u0 + (u - u0) % RING), (u - u0) // RING
                return ("unit", u), None

            u = 0
            while u < units:
                if u in loops:
                    name, turns = loops[u]
                    for s in range(RING):
                        slot_read(u + s)
                        load(u + s, (u + s) % RING)
                    if u == 0:
                        sp.dma_start(consts[:, :], consts_d).then_inc(inputs_landed, 16)
                        sp.dma_start(x[:, :, 0:SEQ], x_d).then_inc(inputs_landed, 16)
                        sp.dma_start(x[:, :, SEQ:TOK], ctx_d).then_inc(inputs_landed, 16)
                    with sp.Fori(1, turns) as i:
                        for s in range(RING):
                            sp.wait_ge(tensor_done, T.at(("unit", u + s), i - 1))
                            src = stream[bass.ds(i * RING + (u + s), 1), :, :]
                            sp.dma_start(ring[:, (u + s) % RING, :], src.rearrange("a p n -> (a p) n"))\
                              .then_inc(weights_landed[(u + s) % RING], 16)
                    u += turns * RING
                else:
                    slot_read(u)
                    load(u, u % RING)
                    u += 1
            sp.wait_ge(vector_done, V.at("final"))
            sp.dma_start(out_d, h[:, :, 0:SEQ]).then_inc(output_stored, 16)
            sp.wait_ge(output_stored, 16)

        @block.tensor
        def _(pe):
            cur = [0]
            nbank = [0]
            tenant = {}

            def take_bank(g, i=None):
                b = nbank[0] % BANKS
                nbank[0] += 1
                old = tenant.get(b)
                if i is None and old is not None:
                    wait_read(old)
                new_banks[g] = b
                tenant[b] = g
                return ps[:, b, :]

            def wait_read(g, turn=None):
                if A.has(("read", g)):
                    pe.wait_ge(scalar_done, A.at(("read", g), turn))
                if V.has(("read", g)):
                    pe.wait_ge(vector_done, V.at(("read", g), turn))

            def weights(name, k, n, width=1, i=None):
                while blocks[cur[0]] is None:
                    cur[0] += 1
                b = cur[0]
                assert blocks[b] == (name, k, n), (blocks[b], name, k, n)
                slot, at = (b // UB) % RING, b % UB
                if at == 0:
                    lands = 16 * (b // UB // RING + 1)
                    pe.wait_ge(weights_landed[slot], lands if i is None else lands + 16 * i)
                cur[0] += width
                e = b + width
                last = e % UB == 0 or all(q is None for q in blocks[e:e + UB - e % UB])
                return ring[:, slot, at * P:(at + width) * P], ("unit", b // UB) if last else None

            def product(out, lhsT, rhs, first, last, done=None, unit=None):
                ins = nc.tensor.matmul(out, lhsT, rhs, start=first, stop=last)
                if unit is not None:
                    T.found[unit] = (T.n + 1, T.loop)
                if done is not None or unit is not None:
                    ins.then_inc(tensor_done, T.mark(done))

            def linear(out, name, nk, n, act, done=None, ready=None, i=None):
                for k in range(nk):
                    if ready is not None:
                        ready(k)
                    w, unit = weights(name, k, n, i=i)
                    product(out, w, act(k), k == 0, k == nk - 1, done if k == nk - 1 else None, unit)

            def once(fn):
                seen = set()

                def ready(k):
                    if k not in seen:
                        seen.add(k)
                        fn(k)
                return ready

            def norm(p, T_):
                out = take_bank((p, "ms"))
                for k in range(KD):
                    pe.wait_ge(scalar_done, A.at((p, "sq", k)))
                    product(out[:, 0:T_], mat("ones_d"), h[:, k, 0:T_], k == 0, k == KD - 1,
                            (p, "ms") if k == KD - 1 else None)
                return once(lambda k: pe.wait_ge(scalar_done, A.at((p, "h", k))))

            def mods(l, blk):
                name = f"mod{blk + 1}_{l}"
                p = (name,)
                nv, v0 = NVEC[blk], blk
                turns = NMOD[blk] * KD // MOD_OUTS
                b0 = cur[0]
                while blocks[b0] is None:
                    b0 += 1
                outs = [take_bank((*p, q)) for q in range(2)]
                if blk == 0 and l == 0:
                    pe.wait_ge(scalar_done, A.at("silu c"))
                with T.turns(pe, name, turns) as i:
                    for q in range(2):
                        if V.has(("read", (*p, q))):
                            pe.wait_ge(vector_done, V.at(("read", (*p, q)), i - 1))
                        for m in range(MOD_OUTS // 2):
                            n = q * (MOD_OUTS // 2) + m
                            linear(outs[q][:, m * nv:(m + 1) * nv], name, KD, n,
                                   lambda k: silu_c[:, k, v0:v0 + nv],
                                   (*p, q) if m == MOD_OUTS // 2 - 1 else None, i=i)
                cur[0] = b0 + turns * CYCLE

            def ffn(p, up, down, T_, ready):
                while blocks[cur[0]] is None:
                    cur[0] += 1
                b0 = cur[0]
                two = T_ == SEQ

                def pair(j, out, i=None, fresh=None):
                    if two:
                        linear(out[:, 0:SEQ], up, KD, 2 * j, lambda k: h[:, k, 0:SEQ], None, fresh, i)
                        linear(out[:, SEQ:TOK], up, KD, 2 * j + 1, lambda k: h[:, k, 0:SEQ],
                               (p, "up", j), None, i)
                    else:
                        linear(out[0], up, KD, 2 * j, lambda k: h[:, k, :], (p, "gate", j), fresh, i)
                        linear(out[1], up, KD, 2 * j + 1, lambda k: h[:, k, :], (p, "up", j), None, i)

                def banks(j, i=None):
                    return take_bank((p, "up", j), i) if two else \
                        (take_bank((p, "gate", j), i), take_bank((p, "up", j), i))

                for k in range(KD):
                    ready(k)
                outs = [banks(j) for j in range(RING)]
                with T.turns(pe, (p, "up"), GU_TURNS) as i:
                    for j in range(RING):
                        if not two:
                            wait_read((p, "gate", j), i - 1)
                        wait_read((p, "up", j), i - 1)
                        pair(j, outs[j], i)
                cur[0] = b0 + GU_TURNS * CYCLE
                for j in range(GU_TURNS * RING, FJ):
                    pair(j, banks(j))
                for m in range(KD):
                    out = take_bank((p, "down", m))
                    linear(out[:, 0:T_], down, FJ, m, lambda k: hid[:, k, 0:T_], (p, "down", m),
                           once(lambda k: pe.wait_ge(vector_done, V.at(*hid_step(p, k)))) if m == 0 else None)

            def head_norm(p, pairs, head, rot, tile):
                for c in range(pairs):
                    out = take_bank((p, "hms", c))
                    pe.wait_ge(scalar_done, A.at((p, "hsq", c)))
                    product(out, mat(head), pair_of(sq, c), True, True, (p, "hms", c))
                    if c >= 1:
                        rotate(p, c - 1, rot, tile)
                rotate(p, pairs - 1, rot, tile)

            def rotate(p, c, rot, tile):
                out = take_bank((p, "rot", c))
                pe.wait_ge(vector_done, V.at((p, "hn", c)))
                product(out, mat(rot), pair_of(tile, c), True, True, (p, "rot", c))

            def attention(p, tasks, scores, values, ready):
                ready()
                for t in range(tasks + 3):
                    if t < tasks:
                        out = take_bank((p, "s", t))
                        scores(t, out)
                    if 2 <= t < tasks + 2:
                        s = t - 2
                        out = take_bank((p, "pt", s))
                        pe.wait_ge(vector_done, V.at((p, "p", s)))
                        order = transposed_order(p)
                        for b in range(4):
                            ins = nc.tensor.transpose(out[:, order[b] * P:(order[b] + 1) * P],
                                                      probs[:, s % 2, b * P:(b + 1) * P], mat("ident"))
                        ins.then_inc(tensor_done, T.mark((p, "pt", s)))
                    if t >= 3:
                        s = t - 3
                        pe.wait_ge(scalar_done, A.at((p, "ptc", s)))
                        values(s)

            pe.wait_ge(inputs_landed, N_IN)
            for l in range(DEPTH):
                p = ("b1", l)
                mods(l, 0)
                ready = norm((*p, "mix"), SEQ)
                hx = lambda k: h[:, k, 0:SEQ]
                for c in range(3):
                    out = take_bank((p, "lat", c))
                    linear(out[:, 0:SEQ], f"lat_{l}", KD, 2 * c, hx, None, ready)
                    linear(out[:, SEQ:TOK], f"lat_{l}", KD, 2 * c + 1, hx, (p, "lat", c))
                out = take_bank((p, "latms"))
                for k in range(5):
                    pe.wait_ge(scalar_done, A.at((p, "latsq", k // 2)))
                    q = k < 3
                    product(out[:, 0:SEQ] if q else out[:, SEQ:TOK], mat("ones_q" if q else "ones_kv"),
                            sq[:, k, :], k in (0, 3), k in (2, 4), (p, "latms") if k == 4 else None)
                for c in range(4):
                    out = take_bank((p, "uq", c))
                    for e in range(2):
                        linear(out[:, e * SEQ:(e + 1) * SEQ], f"uq_{l}", 3, 2 * c + e,
                               lambda k: lat[:, k, :], (p, "uq", c) if e else None,
                               (lambda k: pe.wait_ge(vector_done, V.at((p, "latn", k)))) if c == e == 0 else None)
                for c in range(4):
                    out = take_bank((p, "uk", c))
                    for e in range(2):
                        linear(out[:, e * SEQ:(e + 1) * SEQ], f"uk_{l}", 2, 2 * c + e,
                               lambda k: lat[:, 3 + k, :], (p, "uk", c) if e else None,
                               (lambda k: pe.wait_ge(vector_done, V.at((p, "latn", 3 + k)))) if c == e == 0 else None)
                outs = [take_bank((p, "va", b)) for b in range(2)]
                for k in range(2):
                    w, unit = weights(f"uv_{l}", k, 0, 4)
                    for b in range(2):
                        product(outs[b], lat[:, 3 + k, b * P:(b + 1) * P], w, k == 0, k == 1,
                                (p, "va", b) if k == 1 else None, unit if b == 1 else None)
                head_norm((p, "qa"), 4, "head_a", "rot_a", qt)
                for c in range(4):
                    out = take_bank((p, "qkb", c))
                    linear(out[:, 0:SEQ], f"qkb_{l}", KD, 2 * c, hx)
                    linear(out[:, SEQ:TOK], f"qkb_{l}", KD, 2 * c + 1, hx, (p, "qkb", c))
                head_norm((p, "ka"), 4, "head_a", "rot_a", kt)
                outs = [take_bank((p, "vb", b)) for b in range(2)]
                for k in range(KD):
                    w, unit = weights(f"vb_{l}", k, 0, 4)
                    for b in range(2):
                        product(outs[b], h[:, k, b * P:(b + 1) * P], w, k == 0, k == KD - 1,
                                (p, "vb", b) if k == KD - 1 else None, unit if b == 1 else None)
                head_norm((p, "qkb"), 4, "head_b", "rot_b", bt)
                for c in range(CC):
                    out = take_bank((p, "conv", c))
                    linear(out[:, 0:SEQ], f"conv_{l}", KD, 2 * c, hx)
                    linear(out[:, SEQ:TOK], f"conv_{l}", KD, 2 * c + 1, hx, (p, "conv", c))

                def scores(t, out):
                    for b in range(2):
                        if t < HEADS:
                            q, k = qt[:, t, b * P:(b + 1) * P], kt[:, t, :]
                        else:
                            c, r = (t - HEADS) // 2, 64 * (t % 2)
                            q, k = bt[r:r + 64, c, b * P:(b + 1) * P], bt[r:r + 64, 4 + c, :]
                        product(out[:, b * SEQ:(b + 1) * SEQ], q, k, True, True, ((p, "at"), "s", t) if b else None)

                held = [None]

                def values(s):
                    r = 64 * (s % 2)
                    if s % 2 == 0:
                        held[0] = take_bank(((p, "at"), "o", s // 2))
                    v, hh = (va, s) if s < HEADS else (vb, s - HEADS)
                    if s == 0:
                        pe.wait_ge(scalar_done, A.at(("read", (p, "vb", 1))))
                    for b in range(2):
                        product(held[0][r:r + 64, 0:SEQ], v[:, b, hh * 64:(hh + 1) * 64],
                                probs_t[:, s % 2, b * SEQ:(b + 1) * SEQ], b == 0, b == 1,
                                ((p, "at"), "o", s // 2) if b and s % 2 else (((p, "at"), "ov", s) if b else None))

                attention((p, "at"), 16, scores, values,
                          lambda: pe.wait_ge(vector_done, V.at(((p, "qkb"), "roped", 3))))
                out = take_bank((p, "lnm"))
                pe.wait_ge(vector_done, V.at((p, "dwc")))
                for k in range(CC):
                    product(out[:, 0:SEQ], mat("ones_c"), dwc[:, k, :], k == 0, k == CC - 1,
                            (p, "lnm") if k == CC - 1 else None)
                out = take_bank((p, "lnv"))
                pe.wait_ge(scalar_done, A.at((p, "csq")))
                for k in range(CC):
                    product(out[:, 0:SEQ], mat("ones_c"), csq[:, k, :], k == 0, k == CC - 1,
                            (p, "lnv") if k == CC - 1 else None)
                for m in range(KD):
                    out = take_bank((p, "g01", m))
                    linear(out[:, 0:SEQ], f"gate0_{l}", KD, m, hx)
                    linear(out[:, SEQ:TOK], f"gate1_{l}", KD, m, hx, (p, "g01", m))
                    out = take_bank((p, "g2c", m))
                    linear(out[:, 0:SEQ], f"gate2_{l}", KD, m, hx, (p, "g2", m))
                    if m == 0:
                        pe.wait_ge(scalar_done, A.at((p, "oc")))
                    linear(out[:, SEQ:TOK], f"pw2_{l}", CC, m, lambda k: oc[:, k, :], (p, "g2c", m))
                    out = take_bank((p, "oab", m))
                    if m == 0:
                        pe.wait_ge(scalar_done, A.at(("read", ((p, "at"), "o", 7))))
                    linear(out[:, 0:SEQ], f"oa_{l}", 4, m, lambda k: attn[:, k, :])
                    linear(out[:, SEQ:TOK], f"ob_{l}", 4, m, lambda k: attn[:, 4 + k, :], (p, "oab", m))
                for m in range(KD):
                    out = take_bank((p, "out", m))
                    linear(out[:, 0:SEQ], f"out_{l}", KD, m, lambda k: merged[:, k, :], (p, "out", m),
                           (lambda k: pe.wait_ge(vector_done, V.at((p, "merged", k)))) if m == 0 else None)
                ready = norm((*p, "ffn"), SEQ)
                ffn((*p, "ffn"), f"up_{l}", f"down_{l}", SEQ, ready)

            for l in range(DEPTH):
                p = ("b2", l)
                mods(l, 1)
                ready = norm((*p, "f1"), TOK)
                ffn((*p, "f1"), f"f1up_{l}", f"f1down_{l}", TOK, ready)
                ready = norm((*p, "mix"), TOK)
                hx = lambda k: h[:, k, :]
                if l % 2 == 0:
                    for g in range(4):
                        linear(take_bank((p, "a", g)), "ain", KD, g, hx, (p, "a", g), ready)
                    for g in range(4):
                        linear(take_bank((p, "u", g)), "uin", KD, g, hx, (p, "u", g))
                    outs = [take_bank((p, "v", b)) for b in range(4)]
                    for k in range(KD):
                        w, unit = weights("vin", k, 0, 4)
                        for b in range(4):
                            product(outs[b], h[:, k, b * P:(b + 1) * P], w, k == 0, k == KD - 1,
                                    (p, "v", b) if k == KD - 1 else None, unit if b == 3 else None)
                    for b in range(4):
                        for q in range(2):
                            out = take_bank((p, "sp", b, q))
                            for e in range(2):
                                g = 2 * q + e
                                if b == 0:
                                    pe.wait_ge(scalar_done, A.at(("read", (p, "a", g))))
                                product(out[:, e * 256:(e + 1) * 256], a_in[:, g, b * P:(b + 1) * P],
                                        mat("dft_c"), True, True, (p, "sp", b, q) if e else None)
                    for g in range(4):
                        out = take_bank((p, "f", g))
                        for s in range(2):
                            for b in range(2):
                                t = 2 * s + b
                                if g == 0:
                                    pe.wait_ge(scalar_done, A.at(("read", (p, "sp", t, 1))))
                                o = out[:, s * SEQ:(s + 1) * SEQ]
                                product(o, spec[:, t, g, 0:128], mat("cos_n")[:, b * 256:(b + 1) * 256],
                                        b == 0, False)
                                product(o, spec[:, t, g, 128:256], mat("nsin_n")[:, b * 256:(b + 1) * 256],
                                        False, b == 1, (p, "f", g) if s and b else None)
                    for g in range(4):
                        out = take_bank((p, "mx", g))
                        if g == 0:
                            pe.wait_ge(vector_done, V.at((p, "vn")))
                        for t in range(4):
                            product(out[:, t * P:(t + 1) * P], vt_of(kt)[:, t, g * P:(g + 1) * P], mat(f"ws{g}"),
                                    True, True, (p, "mx", g) if t == 3 else None)
                    for m in range(KD):
                        linear(take_bank((p, "out", m)), "oab", KD, m, lambda k: mixed[:, k, :], (p, "out", m),
                               (lambda k: pe.wait_ge(scalar_done, A.at(("read", (p, "f", k)))) if k < 4 else
                                pe.wait_ge(vector_done, V.at((p, "sgu", k - 4)))) if m == 0 else None)
                else:
                    for c in range(4):
                        out = take_bank((p, "q", c))
                        linear(out[:, 0:SEQ], "q2", KD, 2 * c, lambda k: h[:, k, 0:SEQ], None, ready)
                        linear(out[:, SEQ:TOK], "q2", KD, 2 * c + 1, lambda k: h[:, k, 0:SEQ], (p, "q", c))
                    for c in range(2):
                        linear(take_bank((p, "k", c)), "k2", KD, c, hx, (p, "k", c))
                    outs = [take_bank((p, "v", b)) for b in range(4)]
                    for k in range(KD):
                        w, unit = weights("v2", k, 0, 2)
                        for b in range(4):
                            product(outs[b][:, 0:256], h[:, k, b * P:(b + 1) * P], w, k == 0, k == KD - 1,
                                    (p, "v", b) if k == KD - 1 else None, unit if b == 3 else None)
                    head_norm((p, "q"), 4, "head_c", "rot_c", qt)
                    head_norm((p, "k"), 2, "head_c", "rot_c", kt)
                    held = [None]

                    def scores(t, out):
                        hh, b = divmod(t, 2)
                        product(out, qt[:, hh, b * P:(b + 1) * P], pair_of(kt, hh // 4), True, True,
                                ((p, "at"), "s", t))

                    def values(s):
                        hh, b = divmod(s, 2)
                        if b == 0:
                            held[0] = take_bank(((p, "at"), "o", hh))
                        for c in range(4):
                            product(held[0][:, b * P:(b + 1) * P], v2_of(va)[:, c, (hh // 4) * P:(hh // 4 + 1) * P],
                                    probs_t[:, s % 2, c * P:(c + 1) * P], c == 0, c == 3,
                                    (((p, "at"), "o", hh) if b else ((p, "at"), "ov", s)) if c == 3 else None)

                    def both():
                        pe.wait_ge(vector_done, V.at(((p, "k"), "roped", 1)))
                        pe.wait_ge(scalar_done, A.at(("read", (p, "v", 3))))

                    attention((p, "at"), 16, scores, values, both)
                    for m in range(KD):
                        out = take_bank((p, "out", m))
                        linear(out[:, 0:SEQ], "o2", KD, m, lambda k: attn[:, k, :], (p, "out", m),
                               (lambda k: pe.wait_ge(scalar_done, A.at(("read", ((p, "at"), "o", k))))) if m == 0 else None)
                T_ = TOK if l == 0 else SEQ
                ready = norm((*p, "f2"), T_)
                ffn2(p, l, T_, ready, ffn)
            norm("fin", SEQ)

        @block.scalar
        def _(act):
            def own(i=None):
                if A.n:
                    act.wait_ge(scalar_done, A.so_far(i))

            def norm(p, T_, halves, after, shift):
                for k in range(KD):
                    if after is not None:
                        act.wait_ge(vector_done, V.at(after(k)))
                    nc.scalar.activation(h[:, k, 0:T_], x[:, k, 0:T_], ACT.Square)\
                      .then_inc(scalar_done, A.mark((p, "sq", k)))
                act.wait_ge(tensor_done, T.at((p, "ms")))
                nc.scalar.activation(rs[:, 0:T_], bank((p, "ms"))[:, 0:T_], ACT.Sqrt, bias=col("eps"))\
                  .then_inc(scalar_done, A.mark(("read", (p, "ms"))))
                if shift is None:
                    return
                for k in range(KD):
                    act.wait_ge(vector_done, V.at((p, "hn", k)))
                    for v in range(halves):
                        t = slice(v * SEQ, (v + 1) * SEQ)
                        nc.scalar.activation(h[:, k, t], h[:, k, t], ACT.Identity, bias=shift(k, v))\
                          .then_inc(scalar_done, A.mark((p, "h", k) if v == halves - 1 else None))

            def copy_pair(dst, g, read=True):
                act.wait_ge(tensor_done, T.at(g))
                nc.scalar.activation(dst, bank(g), ACT.Copy)\
                  .then_inc(scalar_done, A.mark(("read", g) if read else None))

            def squares(p, pairs, tile, from_bank=None):
                for c in range(pairs):
                    if from_bank is not None:
                        copy_pair(pair_of(tile, c), from_bank(c))
                    own()
                    nc.scalar.activation(pair_of(sq, c), pair_of(tile, c), ACT.Square)\
                      .then_inc(scalar_done, A.mark((p, "hsq", c)))

            def roots(p, pairs):
                for c in range(pairs):
                    act.wait_ge(tensor_done, T.at((p, "hms", c)))
                    if c >= 2:
                        act.wait_ge(vector_done, V.at((p, "hn", c - 2)))
                    nc.scalar.activation(hrs[:, c % 2, :], bank((p, "hms", c)), ACT.Sqrt, bias=col("eps"))\
                      .then_inc(scalar_done, A.mark(("read", (p, "hms", c))))

            def softmax(p, t, J, scale):
                act.wait_ge(vector_done, V.at((p, "nm", t)))
                W = 512 // J
                for b in range(J):
                    nc.scalar.activation(probs[:, t % 2, b * W:(b + 1) * W], probs[:, t % 2, b * W:(b + 1) * W],
                                         ACT.Exp, bias=stat[:, t % 2, b:b + 1], scale=scale,
                                         accum_out=stat[:, t % 2, 2 + b:3 + b])\
                      .then_inc(scalar_done, A.mark((p, "e", t) if b == J - 1 else None))

            def attention(p, tasks, J, scale, out_of):
                for t in range(tasks + 2):
                    if t < tasks:
                        softmax(p, t, J, scale(t))
                    if t >= 1 and t - 1 < tasks:
                        s = t - 1
                        act.wait_ge(tensor_done, T.at((p, "pt", s)))
                        if s >= 2:
                            act.wait_ge(tensor_done, T.at(out_step(p, s - 2)))
                        nc.scalar.activation(probs_t[:, s % 2, :], bank((p, "pt", s)), ACT.Copy)\
                          .then_inc(scalar_done, A.mark((p, "ptc", s)))
                        A.found[("read", (p, "pt", s))] = A.found[(p, "ptc", s)]
                    if t >= 2 and (t - 2) % 2 == 1:
                        c = (t - 2) // 2
                        act.wait_ge(tensor_done, T.at((p, "o", c)))
                        nc.scalar.activation(out_of(c), bank((p, "o", c))[:, 0:SEQ], ACT.Copy)\
                          .then_inc(scalar_done, A.mark(("read", (p, "o", c))))

            def ffn1(p):
                def pair(j, i=None, turn=None, first=False):
                    act.wait_ge(tensor_done, T.at((p, "up", j), i))
                    if not first:
                        act.wait_ge(vector_done, conv_before(V, p, j, i))
                    nc.scalar.activation(z[:, j % 2, :, FFN_TAPS - 1:], two(bank((p, "up", j))), ACT.Copy)\
                      .then_inc(scalar_done, A.mark((p, "z", j)))
                    A.found[("read", (p, "up", j))] = A.found[(p, "z", j)]

                def silu(j, i=None):
                    act.wait_ge(vector_done, V.at((p, "cv", j), i))
                    nc.scalar.activation(zc[:, j % 2, 0, :], zc[:, j % 2, 0, :], ACT.Silu)\
                      .then_inc(scalar_done, A.mark((p, "si", j)))

                with A.turns(act, (p, "up"), GU_TURNS) as i:
                    for j in range(RING):
                        pair(j, i)
                        silu(j, i)
                for j in range(GU_TURNS * RING, FJ):
                    pair(j)
                    silu(j)

            def ffn2_(p, T_):
                def gate(j, i=None):
                    g = (p, "up", j) if T_ == SEQ else (p, "gate", j)
                    act.wait_ge(tensor_done, T.at(g, i))
                    act.wait_ge(vector_done, conv_before(V, p, j, i))
                    ins = nc.scalar.activation(sg[:, j % 2, 0:T_], bank(g)[:, 0:T_], ACT.Silu)
                    ins.then_inc(scalar_done, A.mark((p, "si", j)))
                    A.found[("read", g)] = A.found[(p, "si", j)]

                with A.turns(act, (p, "up"), GU_TURNS) as i:
                    for j in range(RING):
                        gate(j, i)
                for j in range(GU_TURNS * RING, FJ):
                    gate(j)

            act.wait_ge(inputs_landed, N_IN)
            nc.scalar.activation(silu_c[:, :, :], col("c", 0, KD * 3).rearrange("p (k v) -> p k v", v=3), ACT.Silu)\
              .then_inc(scalar_done, A.mark("silu c"))
            for n, t in enumerate((cos_a, sin_a, cos_b, sin_b)):
                act.wait_ge(vector_done, V.at(("angle", n)))
                nc.scalar.activation(t[:, :], t[:, :], ACT.Sin).then_inc(scalar_done, A.mark(("table", n)))
            for l in range(DEPTH):
                p = ("b1", l)
                norm((*p, "mix"), SEQ, 1, None if l == 0 else lambda k: x_step(("b1", l - 1, "ffn"), "down", k),
                     lambda k, v: mod[:, k:k + 1])
                for c in range(3):
                    copy_pair(lat[:, 2 * c:2 * c + 2, :].rearrange("p a t -> p (a t)"), (p, "lat", c))
                    own()
                    nc.scalar.activation(sq[:, 2 * c:2 * c + 2, :], lat[:, 2 * c:2 * c + 2, :], ACT.Square)\
                      .then_inc(scalar_done, A.mark((p, "latsq", c)))
                act.wait_ge(tensor_done, T.at((p, "latms")))
                nc.scalar.activation(rs[:, :], bank((p, "latms")), ACT.Sqrt, bias=col("eps"))\
                  .then_inc(scalar_done, A.mark(("read", (p, "latms"))))
                squares((p, "qa"), 4, qt, lambda c: (p, "uq", c))
                for c in range(4):
                    act.wait_ge(tensor_done, T.at((p, "uk", c)))
                    nc.scalar.activation(kt[0:64, 2 * c:2 * c + 2, :], two(bank((p, "uk", c)))[0:64], ACT.Copy)\
                      .then_inc(scalar_done, A.mark(("read", (p, "uk", c))))
                for b in range(2):
                    copy_pair(va[:, b, :], (p, "va", b))
                shared = lat[64:96, 5:6, :].to_broadcast([32, HEADS, SEQ])
                nc.scalar.activation(kt[64:96, :, :], shared, ACT.Copy).then_inc(scalar_done, A.mark())
                roots((p, "qa"), 4)
                squares((p, "ka"), 4, kt)
                for c in range(4):
                    copy_pair(pair_of(bt, c), (p, "qkb", c))
                roots((p, "ka"), 4)
                squares((p, "qkb"), 4, bt)
                for b in range(2):
                    copy_pair(vb[:, b, :], (p, "vb", b))
                roots((p, "qkb"), 4)
                for c in range(CC):
                    act.wait_ge(tensor_done, T.at((p, "conv", c)))
                    if c >= 2:
                        act.wait_ge(vector_done, V.at(("read", (p, "conv", c - 2))))
                    nc.scalar.activation(sg2[:, c % 2, :], bank((p, "conv", c))[:, SEQ:TOK], ACT.Sigmoid)\
                      .then_inc(scalar_done, A.mark((p, "glu", c)))
                attention((p, "at"), 16, 2, lambda t: (NOPE + ROPE_A) ** -0.5 if t < HEADS else 64 ** -0.5,
                          lambda c: attn[:, c, :])
                act.wait_ge(vector_done, V.at((p, "cen")))
                nc.scalar.activation(csq[:, :, :], dwc[:, :, :], ACT.Square).then_inc(scalar_done, A.mark((p, "csq")))
                act.wait_ge(tensor_done, T.at((p, "lnv")))
                nc.scalar.activation(rs[:, 0:SEQ], bank((p, "lnv"))[:, 0:SEQ], ACT.Sqrt, bias=col("eps"))\
                  .then_inc(scalar_done, A.mark(("read", (p, "lnv"))))
                act.wait_ge(vector_done, V.at((p, "lnn")))
                for c in range(CC):
                    nc.scalar.activation(oc[:, c, :], dwc[:, c, :], ACT.Silu, bias=col(f"ln_b_{l}", c),
                                         scale=col(f"ln_g_{l}", c))\
                      .then_inc(scalar_done, A.mark((p, "oc") if c == CC - 1 else None))
                for m in range(KD):
                    if m >= 2:
                        act.wait_ge(vector_done, V.at((p, "merged", m - 2)))
                    act.wait_ge(tensor_done, T.at((p, "g01", m)))
                    nc.scalar.activation(sg[:, m % 2, :], bank((p, "g01", m)), ACT.Sigmoid)\
                      .then_inc(scalar_done, A.mark(("read", (p, "g01", m))))
                    act.wait_ge(tensor_done, T.at((p, "g2c", m)))
                    nc.scalar.activation(sg2[:, m % 2, :], bank((p, "g2c", m))[:, 0:SEQ], ACT.Sigmoid)\
                      .then_inc(scalar_done, A.mark((p, "sg2", m)))
                norm((*p, "ffn"), SEQ, 1, lambda k: x_step(p, "out", k), lambda k, v: mod[:, 3 * KD + k:3 * KD + k + 1])
                ffn1((*p, "ffn"))
            for l in range(DEPTH):
                p = ("b2", l)

                def shift(n):
                    return lambda k, v: mod[:, (n * KD + k) * 2 + v:(n * KD + k) * 2 + v + 1]

                before = ("b1", 1, "ffn") if l == 0 else ("b2", 0, "f2")
                norm((*p, "f1"), TOK, 2, lambda k: x_step(before, "down", k), shift(0))
                ffn2_((*p, "f1"), TOK)
                norm((*p, "mix"), TOK, 2, lambda k: x_step((*p, "f1"), "down", k), shift(3))
                if l % 2 == 0:
                    for g in range(4):
                        copy_pair(a_in[:, g, :], (p, "a", g))
                    for g in range(4):
                        act.wait_ge(tensor_done, T.at((p, "u", g)))
                        nc.scalar.activation(pair_of(qt, g), bank((p, "u", g)), ACT.Gelu_apprx_tanh)\
                          .then_inc(scalar_done, A.mark(("read", (p, "u", g))))
                    for b in range(4):
                        act.wait_ge(tensor_done, T.at((p, "v", b)))
                        nc.scalar.activation(vt_of(kt)[:, b, :], bank((p, "v", b)), ACT.Gelu_apprx_tanh)\
                          .then_inc(scalar_done, A.mark(("read", (p, "v", b))))
                    for b in range(4):
                        for q in range(2):
                            copy_pair(spec[:, b, 2 * q:2 * q + 2, :].rearrange("p a f -> p (a f)"), (p, "sp", b, q))
                    act.wait_ge(vector_done, V.at((p, "vss")))
                    nc.scalar.activation(rs[:, 0:16], rs[:, 0:16], ACT.Sqrt, bias=col("eps"), scale=1.0 / P)\
                      .then_inc(scalar_done, A.mark((p, "vrt")))
                    for g in range(4):
                        copy_pair(mixed[:, g, :], (p, "f", g))
                else:
                    squares((p, "q"), 4, qt, lambda c: (p, "q", c))
                    for c in range(2):
                        copy_pair(pair_of(kt, c), (p, "k", c))
                    for b in range(4):
                        act.wait_ge(tensor_done, T.at((p, "v", b)))
                        nc.scalar.activation(v2_of(va)[:, b, :], bank((p, "v", b))[:, 0:256], ACT.Copy)\
                          .then_inc(scalar_done, A.mark(("read", (p, "v", b))))
                    roots((p, "q"), 4)
                    squares((p, "k"), 2, kt)
                    roots((p, "k"), 2)
                    attention((p, "at"), 16, 1, lambda t: 128 ** -0.5, lambda c: attn[:, c, :])
                T_ = TOK if l == 0 else SEQ
                norm((*p, "f2"), T_, T_ // SEQ, lambda k: x_step(p, "out", k), shift(6))
                ffn2_((*p, "f2"), T_)
            norm("fin", SEQ, 1, lambda k: x_step(("b2", 1, "f2"), "down", k), None)

        @block.vector
        def _(dve):
            def own(i=None):
                if V.n:
                    dve.wait_ge(vector_done, V.so_far(i))

            def step(ins, name=None, i=None):
                ins.then_inc(vector_done, V.mark(name))
                own(i)

            def mods(l, blk):
                name = f"mod{blk + 1}_{l}"
                nv = NVEC[blk]
                half = MOD_OUTS // 2 * nv
                b0 = vcol[f"b_{name.split('_')[0]}_{l}"][0]
                with V.turns(dve, name, NMOD[blk] * KD // MOD_OUTS) as i:
                    for q in range(2):
                        dve.wait_ge(tensor_done, T.at((name, q), i))
                        at = i * (2 * half) + q * half
                        step(nc.vector.tensor_tensor(mod[:, bass.ds(at, half)], bank((name, q))[:, 0:half],
                                                     cols[:, bass.ds(at + b0, half)], ALU.add),
                             ("read", (name, q)), i)

            def adapt(slot, scale_at, gains, v, nv):
                sc = mod[:, scale_at * KD * nv + v:(scale_at + 1) * KD * nv:nv] if nv > 1 else \
                    mod[:, scale_at * KD:(scale_at + 1) * KD]
                step(nc.vector.scalar_tensor_tensor(out=amod[:, slot, :, v], in0=sc, scalar=1.0, in1=gains,
                                                    op0=ALU.add, op1=ALU.mult))

            def norm(p, T_, slot, gain=None):
                dve.wait_ge(scalar_done, A.at(("read", (p, "ms"))))
                step(nc.vector.reciprocal(rs[:, 0:T_], rs[:, 0:T_]))
                for k in range(KD):
                    for v in range(T_ // SEQ):
                        t = slice(v * SEQ, (v + 1) * SEQ)
                        g = gain(k) if gain else amod[:, slot, k, v:v + 1]
                        last = v == T_ // SEQ - 1
                        name = ("final" if k == KD - 1 else None) if gain else ((p, "hn", k) if last else None)
                        nc.vector.scalar_tensor_tensor(out=h[:, k, t], in0=x[:, k, t], scalar=g, in1=rs[:, t],
                                                       op0=ALU.mult, op1=ALU.mult)\
                          .then_inc(vector_done, V.mark(name))

            def update(p, what, T_, gate):
                for m in range(KD):
                    dve.wait_ge(tensor_done, T.at((p, what, m)))
                    for v in range(T_ // SEQ):
                        t = slice(v * SEQ, (v + 1) * SEQ)
                        last = v == T_ // SEQ - 1
                        nc.vector.scalar_tensor_tensor(out=x[:, m, t], in0=bank((p, what, m))[:, t],
                                                       scalar=gate(m, v), in1=x[:, m, t],
                                                       op0=ALU.mult, op1=ALU.add)\
                          .then_inc(vector_done, V.mark(("read", (p, what, m)) if last else None))

            def head_norm(p, pairs, tile, gain, cos, sin):
                for c in range(pairs + 1):
                    if c < pairs:
                        b = hrs[:, c % 2, :]
                        dve.wait_ge(scalar_done, A.at(("read", (p, "hms", c))))
                        step(nc.vector.reciprocal(b, b))
                        step(nc.vector.scalar_tensor_tensor(out=pair_of(tile, c), in0=pair_of(tile, c),
                                                            scalar=gain(c), in1=b, op0=ALU.mult, op1=ALU.mult),
                             (p, "hn", c))
                    if c >= 1:
                        e = c - 1
                        dve.wait_ge(tensor_done, T.at((p, "rot", e)))
                        a, b2 = rt[:, 0, :], rt[:, 1, :]
                        tp = pair_of(tile, e)
                        shaped = two if cos(e).shape[1] == SEQ else (lambda q: q)
                        wide = (lambda q: q.rearrange("p (a t) -> p a t", a=1).to_broadcast([P, 2, SEQ])) \
                            if cos(e).shape[1] == SEQ else (lambda q: q)
                        step(nc.vector.tensor_tensor(shaped(b2), shaped(bank((p, "rot", e))), wide(sin(e)), ALU.mult),
                             ("read", (p, "rot", e)))
                        step(nc.vector.tensor_tensor(shaped(a), shaped(tp), wide(cos(e)), ALU.mult))
                        step(nc.vector.tensor_tensor(tp, a, b2, ALU.add), (p, "roped", e))

            def attention(p, tasks, J, scale, masked, between=None):
                W = 512 // J

                def first(t):
                    dve.wait_ge(tensor_done, T.at((p, "s", t)))
                    if t >= 2:
                        dve.wait_ge(tensor_done, T.at((p, "pt", t - 2)))
                    pr = probs[:, t % 2, :]
                    if masked:
                        step(nc.vector.tensor_tensor(pr, bank((p, "s", t)), mat("mask"), ALU.add), ("read", (p, "s", t)))
                    else:
                        step(nc.vector.tensor_copy(pr, bank((p, "s", t))), ("read", (p, "s", t)))
                    st = stat[:, t % 2, :]
                    step(nc.vector.tensor_reduce(st[:, 4:4 + J], pr.rearrange("p (j w) -> p j w", w=W), AX.X, ALU.max))
                    step(nc.vector.tensor_scalar(st[:, 0:J], st[:, 4:4 + J], -scale(t), None, ALU.mult), (p, "nm", t))

                def second(t):
                    dve.wait_ge(scalar_done, A.at((p, "e", t)))
                    st = stat[:, t % 2, :]
                    step(nc.vector.reciprocal(st[:, 6:6 + J], st[:, 2:2 + J]))
                    for b in range(J):
                        o = probs[:, t % 2, b * W:(b + 1) * W]
                        step(nc.vector.tensor_scalar(o, o, st[:, 6 + b:7 + b], None, ALU.mult),
                             (p, "p", t) if b == J - 1 else None)

                for t in range(tasks + 1):
                    if t < tasks:
                        first(t)
                        if between is not None:
                            between(t)
                    if t >= 1:
                        second(t - 1)

            def ffn1(p, l):
                w0, b0 = vcol[f"ffn_w_{l}"][0], vcol[f"ffn_b_{l}"][0]

                def c(at, j, i):
                    if i is None:
                        return cols[:, at + j:at + j + 1]
                    return cols[:, bass.ds(i * RING + (at + j), 1)]

                def pair(j, i=None):
                    s = j % 2
                    dve.wait_ge(scalar_done, A.at((p, "z", j), i))
                    for ab in range(2):
                        def w(tap):
                            return c(w0 + (tap * 2 + ab) * FJ, j, i)
                        nc.vector.tensor_scalar(zc[:, s, ab, :], z[:, s, ab, 2:2 + SEQ], w(2), c(b0 + ab * FJ, j, i),
                                                ALU.mult, ALU.add).then_inc(vector_done, V.mark())
                    own(i)
                    for tap in (1, 0):
                        for ab in range(2):
                            nc.vector.scalar_tensor_tensor(out=zc[:, s, ab, :], in0=z[:, s, ab, tap:tap + SEQ],
                                                           scalar=c(w0 + (tap * 2 + ab) * FJ, j, i),
                                                           in1=zc[:, s, ab, :], op0=ALU.mult, op1=ALU.add)\
                              .then_inc(vector_done, V.mark((p, "cv", j) if (tap, ab) == (0, 1) else None))
                        own(i)

                def join(j, i=None):
                    out = hid[:, j, 0:SEQ] if i is None else \
                        hid[:, bass.ds(i * RING + j, 1), 0:SEQ].rearrange("p a t -> p (a t)")
                    dve.wait_ge(scalar_done, A.at((p, "si", j), i))
                    step(nc.vector.tensor_tensor(out, zc[:, j % 2, 0, :], zc[:, j % 2, 1, :], ALU.mult),
                         (p, "hid", j), i)

                with V.turns(dve, (p, "up"), GU_TURNS) as i:
                    for j in range(RING):
                        pair(j, i)
                        join(j, i)
                for j in range(GU_TURNS * RING, FJ):
                    pair(j)
                    join(j)

            def ffn2_(p, T_):
                def join(j, i=None):
                    out = hid[:, j, 0:T_] if i is None else \
                        hid[:, bass.ds(i * RING + j, 1), 0:T_].rearrange("p a t -> p (a t)")
                    g = (p, "up", j)
                    dve.wait_ge(tensor_done, T.at(g, i))
                    dve.wait_ge(scalar_done, A.at((p, "si", j), i))
                    up = bank(g)[:, SEQ:TOK] if T_ == SEQ else bank(g)
                    step(nc.vector.tensor_tensor(out, sg[:, j % 2, 0:T_], up, ALU.mult), (p, "hid", j), i)
                    V.found[("read", g)] = V.found[(p, "hid", j)]

                with V.turns(dve, (p, "up"), GU_TURNS) as i:
                    for j in range(RING):
                        join(j, i)
                for j in range(GU_TURNS * RING, FJ):
                    join(j)

            dve.wait_ge(inputs_landed, N_IN)
            step(nc.vector.tensor_copy(rs[:, 0:SEQ], pos_i[:, :]))
            for n, (t, f, quarter) in enumerate(((cos_a, "inv_freq_a", 1), (sin_a, "inv_freq_a", 0),
                                                 (cos_b, "inv_freq_b", 1), (sin_b, "inv_freq_b", 0))):
                ang, k = rt[:, 0, 0:SEQ], rt[:, 1, 0:SEQ]
                step(nc.vector.tensor_scalar(ang, rs[:, 0:SEQ], col(f), None, ALU.mult))
                step(nc.vector.tensor_scalar(k, ang, 1.0 / (2.0 * np.pi), 0.25 * quarter, ALU.mult, ALU.add))
                step(nc.vector.tensor_scalar(k, k, 12582912.0, None, ALU.add))
                step(nc.vector.tensor_scalar(k, k, 12582912.0, None, ALU.subtract))
                for part_ in TWO_PI:
                    step(nc.vector.scalar_tensor_tensor(out=ang, in0=k, scalar=-part_, in1=ang,
                                                        op0=ALU.mult, op1=ALU.add))
                if quarter:
                    step(nc.vector.tensor_scalar(ang, ang, np.pi / 2, None, ALU.add))
                step(nc.vector.tensor_scalar(t[:, :], ang, 3.1415925, -3.1415925, ALU.min, ALU.max), ("angle", n))
            step(nc.vector.memset(z[:, :, :, :], 0.0))
            step(nc.vector.memset(kt[96:128, :, :], 0.0), "kt zero")
            for l in range(DEPTH):
                p = ("b1", l)
                mods(l, 0)
                adapt(0, 1, col(f"g_mix1_{l}", 0, KD), 0, 1)
                adapt(1, 4, col(f"g_ffn1_{l}", 0, KD), 0, 1)
                norm((*p, "mix"), SEQ, 0)
                dve.wait_ge(scalar_done, A.at(("read", (p, "latms"))))
                step(nc.vector.reciprocal(rs[:, :], rs[:, :]))
                for k in range(5):
                    g = col(f"g_qlat_{l}", k) if k < 3 else col(f"g_kvlat_{l}", k - 3)
                    r = rs[:, 0:SEQ] if k < 3 else rs[:, SEQ:TOK]
                    step(nc.vector.scalar_tensor_tensor(out=lat[:, k, :], in0=lat[:, k, :], scalar=g, in1=r,
                                                        op0=ALU.mult, op1=ALU.mult), (p, "latn", k))
                if l == 0:
                    dve.wait_ge(scalar_done, A.at(("table", 3)))
                head_norm((p, "qa"), 4, qt, lambda c: col(f"g_qa_{l}"), lambda e: cos_a[:, :], lambda e: sin_a[:, :])
                head_norm((p, "ka"), 4, kt, lambda c: col(f"g_ka_{l}"), lambda e: cos_a[:, :], lambda e: sin_a[:, :])
                head_norm((p, "qkb"), 4, bt, lambda c: col(f"g_qb_{l}" if c < 2 else f"g_kb_{l}"),
                          lambda e: cos_b[:, :], lambda e: sin_b[:, :])
                step(nc.vector.memset(u_pad[:, :, 0:TAPS - 1], 0.0))
                for c in range(CC):
                    dve.wait_ge(scalar_done, A.at((p, "glu", c)))
                    step(nc.vector.tensor_tensor(u_pad[:, c, TAPS - 1:], bank((p, "conv", c))[:, 0:SEQ],
                                                 sg2[:, c % 2, :], ALU.mult), ("read", (p, "conv", c)))

                def taps(t):
                    for tap in range(2 * t, min(2 * t + 2, TAPS)):
                        for c in range(CC):
                            w = col(f"conv_w_{l}", tap * CC + c)
                            name = (p, "dwc") if tap == TAPS - 1 and c == CC - 1 else None
                            if tap == 0:
                                nc.vector.tensor_scalar(dwc[:, c, :], u_pad[:, c, 0:SEQ], w, col(f"conv_b_{l}", c),
                                                        ALU.mult, ALU.add).then_inc(vector_done, V.mark(name))
                            else:
                                nc.vector.scalar_tensor_tensor(out=dwc[:, c, :], in0=u_pad[:, c, tap:tap + SEQ],
                                                               scalar=w, in1=dwc[:, c, :], op0=ALU.mult, op1=ALU.add)\
                                  .then_inc(vector_done, V.mark(name))
                        own()

                attention((p, "at"), 16, 2, lambda t: (NOPE + ROPE_A) ** -0.5 if t < HEADS else 64 ** -0.5, True, taps)
                dve.wait_ge(tensor_done, T.at((p, "lnm")))

                def spread(a):
                    return a.rearrange("p (a t) -> p a t", a=1).to_broadcast([P, CC, SEQ])

                step(nc.vector.tensor_tensor(dwc[:, :, :], dwc[:, :, :], spread(bank((p, "lnm"))[:, 0:SEQ]),
                                             ALU.subtract), (p, "cen"))
                V.found[("read", (p, "lnm"))] = V.found[(p, "cen")]
                dve.wait_ge(scalar_done, A.at(("read", (p, "lnv"))))
                step(nc.vector.reciprocal(rs[:, 0:SEQ], rs[:, 0:SEQ]))
                step(nc.vector.tensor_tensor(dwc[:, :, :], dwc[:, :, :], spread(rs[:, 0:SEQ]), ALU.mult), (p, "lnn"))
                for m in range(KD):
                    a, b = rt[:, 0, :], rt[:, 1, 0:SEQ]
                    dve.wait_ge(tensor_done, T.at((p, "g2c", m)))
                    dve.wait_ge(scalar_done, A.at((p, "sg2", m)))
                    step(nc.vector.scalar_tensor_tensor(out=b, in0=bank((p, "g2c", m))[:, SEQ:TOK],
                                                        scalar=col(f"pw2_b_{l}", m), in1=sg2[:, m % 2, :],
                                                        op0=ALU.add, op1=ALU.mult), ("read", (p, "g2c", m)))
                    dve.wait_ge(tensor_done, T.at((p, "oab", m)))
                    step(nc.vector.tensor_tensor(a, bank((p, "oab", m)), sg[:, m % 2, :], ALU.mult),
                         ("read", (p, "oab", m)))
                    step(nc.vector.tensor_tensor(b, b, a[:, 0:SEQ], ALU.add))
                    step(nc.vector.tensor_tensor(merged[:, m, :], b, a[:, SEQ:TOK], ALU.add), (p, "merged", m))
                update(p, "out", SEQ, lambda m, v: mod[:, 2 * KD + m:2 * KD + m + 1])
                norm((*p, "ffn"), SEQ, 1)
                ffn1((*p, "ffn"), l)
                update((*p, "ffn"), "down", SEQ, lambda m, v: mod[:, 5 * KD + m:5 * KD + m + 1])
                own()
            for l in range(DEPTH):
                p = ("b2", l)
                mods(l, 1)
                for n in range(3):
                    for v in range(2):
                        adapt(n, 3 * n + 1, col(f"g2_{l}", n * KD, KD), v, 2)
                for n in (2, 8):
                    g = mod[:, n * KD * 2:(n + 1) * KD * 2]
                    step(nc.vector.tensor_scalar(g, g, 0.5, None, ALU.mult))

                def gate(n):
                    return lambda m, v: mod[:, (n * KD + m) * 2 + v:(n * KD + m) * 2 + v + 1]

                norm((*p, "f1"), TOK, 0)
                ffn2_((*p, "f1"), TOK)
                update((*p, "f1"), "down", TOK, gate(2))
                norm((*p, "mix"), TOK, 1)
                if l % 2 == 0:
                    vt = vt_of(kt)
                    for b in range(4):
                        dve.wait_ge(scalar_done, A.at(("read", (p, "v", b))))
                        step(nc.vector.tensor_tensor(vt_of(sq)[:, b, :], vt[:, b, :], vt[:, b, :], ALU.mult))
                        step(nc.vector.tensor_reduce(rs[:, 4 * b:4 * b + 4],
                                                     vt_of(sq)[:, b, :].rearrange("p (g d) -> p g d", g=4),
                                                     AX.X, ALU.add), (p, "vss") if b == 3 else None)
                    dve.wait_ge(scalar_done, A.at((p, "vrt")))
                    step(nc.vector.reciprocal(rs[:, 0:16], rs[:, 0:16]))
                    for b in range(4):
                        for g in range(4):
                            o = vt[:, b, g * P:(g + 1) * P]
                            step(nc.vector.scalar_tensor_tensor(out=o, in0=o, scalar=rs[:, 4 * b + g:4 * b + g + 1],
                                                                in1=mat("g_v")[:, g * P:(g + 1) * P],
                                                                op0=ALU.mult, op1=ALU.mult),
                                 (p, "vn") if b == g == 3 else None)
                    for g in range(4):
                        dve.wait_ge(tensor_done, T.at((p, "mx", g)))
                        bs = mat("b_s")[:, g * P:(g + 1) * P].rearrange("p (a t) -> p a t", a=1)\
                            .to_broadcast([P, 4, P])
                        o = rt[:, 0, :]
                        step(nc.vector.tensor_tensor(o.rearrange("p (a t) -> p a t", a=4),
                                                     bank((p, "mx", g)).rearrange("p (a t) -> p a t", a=4),
                                                     bs, ALU.add), ("read", (p, "mx", g)))
                        step(nc.vector.tensor_tensor(mixed[:, 4 + g, :], o, pair_of(qt, g), ALU.mult), (p, "sgu", g))
                else:
                    head_norm((p, "q"), 4, qt, lambda c: col("gq2"), lambda e: mat("cos_c")[:, 0:SEQ],
                              lambda e: mat("sin_c")[:, 0:SEQ])
                    head_norm((p, "k"), 2, kt, lambda c: col("gk2"), lambda e: mat("cos_c"), lambda e: mat("sin_c"))
                    attention((p, "at"), 16, 1, lambda t: 128 ** -0.5, False)
                update(p, "out", TOK if l == 0 else SEQ, gate(5))
                T_ = TOK if l == 0 else SEQ
                norm((*p, "f2"), T_, 2)
                ffn2_((*p, "f2"), T_)
                update((*p, "f2"), "down", T_, gate(8))
                own()
            norm("fin", SEQ, None, lambda k: col("g_final", k))

    return {"T": T.found, "A": A.found, "V": V.found}, new_banks


def two(a):
    return a.rearrange("p (a t) -> p a t", a=2)


def pair_of(tile, c):
    return tile[:, 2 * c:2 * c + 2, :].rearrange("p a t -> p (a t)")


def vt_of(tile):
    return tile[:, :, :].rearrange("p (b e) t -> p b (e t)", b=4)


def v2_of(tile):
    return tile[:, :, :].rearrange("p e (b t) -> p (e b) t", b=2)


def transposed_order(p):
    return (0, 2, 1, 3) if p[0][0] == "b1" else (0, 1, 2, 3)


def out_step(p, s):
    return (p, "o", s // 2) if s % 2 else (p, "ov", s)


def x_step(p, what, k):
    return ("read", (p, what, k))


def hid_step(p, k):
    if k < GU_TURNS * RING:
        return (p, "hid", k % RING), k // RING
    return (p, "hid", k), None


def conv_before(V, p, j, i):
    if i is None:
        return V.at(*hid_step(p, j - 2))
    if j >= 2:
        return V.at((p, "hid", j - 2), i)
    return V.at((p, "hid", j + RING - 2), i - 1)


def ffn2(p, l, T_, ready, ffn):
    ffn((*p, "f2"), f"f2up_{l}", f"f2down_{l}", T_, ready)


def loop_starts(blocks):
    out, seen = [], set()
    for b, q in enumerate(blocks):
        if q is None or q[0] in seen:
            continue
        seen.add(q[0])
        name = q[0]
        if name.startswith("mod"):
            blk = int(name[3]) - 1
            out.append((b, name, NMOD[blk] * KD * KD // CYCLE))
        elif name.startswith(("up_", "f1up_", "f2up_")):
            out.append((b, name, GU_TURNS))
    return out


def _columns(a):
    return np.asarray(a).reshape(-1, P).T


def _constants():
    m = {}
    m["ones_d"] = np.full((P, P), 1.0 / D)
    m["ones_q"] = np.full((P, P), 1.0 / Q_RANK)
    m["ones_kv"] = np.full((P, P), 1.0 / KV_RANK)
    m["ones_c"] = np.full((P, P), 1.0 / CONV_CH)
    m["head_c"] = np.full((P, P), 1.0 / P)
    a = np.zeros((P, P))
    a[0:64, 0:64] = 1.0 / 64
    a[64:96, 64:96] = 1.0 / 32
    m["head_a"] = a
    b = np.zeros((P, P))
    b[0:64, 0:64] = b[64:128, 64:128] = 1.0 / 64
    m["head_b"] = b

    def rot(starts, half):
        r = np.zeros((P, P))
        for s in starts:
            for i in range(half):
                r[s + half + i, s + i] = -1.0
                r[s + i, s + half + i] = 1.0
        return r

    m["rot_a"] = rot((64,), 16)
    m["rot_b"] = rot((0, 64), 32)
    m["rot_c"] = rot((0, 64), 32)
    m["ident"] = np.eye(P)

    def dft(n):
        a = 2 * np.pi * (np.outer(np.arange(n), np.arange(n)) % n) / n
        return np.cos(a) / np.sqrt(n), np.sin(a) / np.sqrt(n)

    c, s = dft(P)
    m["dft_c"] = np.concatenate([c, s], 1)
    c, s = dft(SEQ)
    m["cos_n"] = np.concatenate([c[0:P], c[P:]], 1)
    m["nsin_n"] = -np.concatenate([s[0:P], s[P:]], 1)
    inv = THETA ** (-np.arange(0, 64, 2, dtype=np.float32) / np.float32(64))
    row = np.repeat(np.arange(SEQ // GRID_W), GRID_W).astype(np.float32)
    colm = np.tile(np.arange(GRID_W), SEQ // GRID_W).astype(np.float32)
    ang = np.concatenate([np.tile((row[:, None] * inv).T, (2, 1)), np.tile((colm[:, None] * inv).T, (2, 1))], 0)
    m["cos_c"] = np.concatenate([np.cos(ang), np.ones((P, SEQ))], 1)
    m["sin_c"] = np.concatenate([np.sin(ang), np.zeros((P, SEQ))], 1)
    mask = np.zeros((P, 2, SEQ))
    for q in range(2):
        mask[:, q, :] = np.where(np.arange(SEQ)[None] <= (q * P + np.arange(P))[:, None], 0.0, MASKED)
    m["mask"] = mask.reshape(P, 2 * SEQ)
    return {k: v.astype(np.float32) for k, v in m.items()}


def _pack(w):
    f = np.float32
    mats = {}
    o = np.cumsum([0, Q_RANK, KV_RANK, ROPE_A, 512, 512, 512, 512, 512, D, D, D])
    for l in range(DEPTH):
        mats[f"mod1_{l}"] = w["w_mod"][l]
        mats[f"mod2_{l}"] = w["w_mod_2"][l]
        wi = w["w_in"][l]
        rope = np.zeros((D, P), f)
        rope[:, 64:96] = wi[:, o[2]:o[3]]
        mats[f"lat_{l}"] = np.concatenate([wi[:, o[0]:o[2]], rope], 1)
        uq = np.zeros((Q_RANK, HEADS, P), f)
        uq[:, :, 0:96] = w["w_uq"][l].reshape(Q_RANK, HEADS, 96)
        mats[f"uq_{l}"] = uq.reshape(Q_RANK, HEADS * P)
        kv = w["w_ukv"][l].reshape(KV_RANK, HEADS, P)
        uk = np.zeros((KV_RANK, HEADS, P), f)
        uk[:, :, 0:64] = kv[:, :, 0:64]
        mats[f"uk_{l}"] = uk.reshape(KV_RANK, HEADS * P)
        mats[f"uv_{l}"] = kv[:, :, 64:128].reshape(KV_RANK, 512)
        mats[f"qkb_{l}"] = wi[:, o[3]:o[5]]
        mats[f"vb_{l}"] = wi[:, o[5]:o[6]]
        mats[f"conv_{l}"] = wi[:, o[6]:o[8]].reshape(D, 2, CC, P).transpose(0, 2, 1, 3).reshape(D, D)
        for n in range(3):
            mats[f"gate{n}_{l}"] = wi[:, o[8 + n]:o[9 + n]]
        mats[f"pw2_{l}"] = w["w_conv_pw2"][l]
        mats[f"oa_{l}"] = w["w_mla_o"][l]
        mats[f"ob_{l}"] = w["w_moba_o"][l]
        mats[f"out_{l}"] = w["w_out"][l]
        mats[f"up_{l}"] = w["w_up"][l].reshape(D, 2, FJ, P).transpose(0, 2, 1, 3).reshape(D, 2 * D_FF)
        mats[f"down_{l}"] = w["w_down"][l]
        for n in (1, 2):
            gu = np.zeros((D, 2, D_FF), f)
            gu[:, :, 0:D_FF_2] = w[f"w_ffn{n}_gu_2"][l].reshape(D, 2, D_FF_2)
            mats[f"f{n}up_{l}"] = gu.reshape(D, 2, FJ, P).transpose(0, 2, 1, 3).reshape(D, 2 * D_FF)
            dn = np.zeros((D_FF, D), f)
            dn[0:D_FF_2] = w[f"w_ffn{n}_down_2"][l]
            mats[f"f{n}down_{l}"] = dn
    wab = w["w_in_ab_2"][0]
    mats["ain"], mats["uin"], mats["vin"] = wab[:, 0:512], wab[:, 512:1024], wab[:, 1024:1536]
    mats["oab"] = w["w_out_ab_2"][0]
    qkv = w["w_qkv_2"][0]
    mats["q2"], mats["k2"], mats["v2"] = qkv[:, 0:1024], qkv[:, 1024:1280], qkv[:, 1280:1536]
    mats["o2"] = w["w_o_2"][0]

    blocks = weight_blocks()
    stream = np.zeros((len(blocks) // UB, P, UB, P), f)
    for b, q in enumerate(blocks):
        if q is not None:
            name, k, n = q
            stream[b // UB, :, b % UB, :] = mats[name][k * P:(k + 1) * P, n * P:(n + 1) * P]

    vcol, vcols = vector_columns()
    cols = np.zeros((P, vcols), f)

    def put(name, a):
        s, n = vcol[name]
        cols[:, s:s + n] = a

    inv_a = (1.0 / (THETA ** (np.arange(0, 32, 2, dtype=f) / f(32)))).astype(f)
    inv_b = (1.0 / (THETA ** (np.arange(0, 64, 2, dtype=f) / f(64)))).astype(f)
    a = np.zeros((P, 1), f)
    a[64:96, 0] = np.tile(inv_a, 2)
    put("inv_freq_a", a)
    put("inv_freq_b", np.tile(inv_b, 4)[:, None])
    put("c", np.stack([_columns(w["c"][0]), _columns(w["c_2"][0]), _columns(w["c_ctx_2"])], 2).reshape(P, KD * 3))
    put("eps", f(EPS))
    put("g_final", _columns(w["g_final_2"]))
    put("gq2", w["g_q_2"][0][:, None])
    put("gk2", w["g_k_2"][0][:, None])
    for l in range(DEPTH):
        put(f"b_mod1_{l}", _columns(w["b_mod"][l]))
        put(f"b_mod2_{l}", np.repeat(_columns(w["b_mod_2"][l]), 2, axis=1))
        put(f"g_mix1_{l}", _columns(w["mix_norm_g"][l]))
        put(f"g_ffn1_{l}", _columns(w["ffn_norm_g"][l]))
        put(f"g_qlat_{l}", _columns(w["mla_q_norm_g"][l]))
        put(f"g_kvlat_{l}", _columns(w["mla_kv_norm_g"][l]))
        for n, (a, b) in (("qa", ("mla_qn_nope_g", "mla_qn_rope_g")), ("ka", ("mla_kn_nope_g", "mla_kn_rope_g"))):
            g = np.zeros((P, 1), f)
            g[0:64, 0], g[64:96, 0] = w[a][l], w[b][l]
            put(f"g_{n}_{l}", g)
        put(f"g_qb_{l}", np.tile(w["moba_qn_g"][l], 2)[:, None])
        put(f"g_kb_{l}", np.tile(w["moba_kn_g"][l], 2)[:, None])
        put(f"conv_w_{l}", _columns(w["conv_dw_w"][l].reshape(-1)))
        put(f"conv_b_{l}", _columns(w["conv_dw_b"][l]))
        put(f"ln_g_{l}", _columns(w["conv_ln_g"][l]))
        put(f"ln_b_{l}", _columns(w["conv_ln_b"][l]))
        put(f"pw2_b_{l}", _columns(w["b_conv_pw2"][l]))
        put(f"ffn_w_{l}", _columns(w["ffn_dw_w"][l].reshape(-1)))
        put(f"ffn_b_{l}", _columns(w["ffn_dw_b"][l]))
        put(f"g2_{l}", np.concatenate([_columns(w[n][l]) for n in ("g_ffn1_2", "g_mix_2", "g_ffn2_2")], 1))

    ccol, ccols = const_columns()
    consts = np.zeros((P, ccols), f)
    made = _constants()
    for g in range(4):
        made[f"ws{g}"] = w["w_s_2"][0, g].T
    made["g_v"] = np.broadcast_to(w["g_v_2"][0].reshape(1, 512), (P, 512))
    made["b_s"] = np.broadcast_to(w["b_s_2"][0].reshape(1, 512), (P, 512))
    for name, (s, n) in ccol.items():
        consts[:, s:s + n] = made[name]
    return stream.reshape(-1, P, UB * P), cols, consts


def kernel(**inputs):
    import concourse.bacc as bacc
    from concourse.bass_utils import run_bass_kernel_spmd

    w = {k: np.asarray(v) for k, v in inputs.items()}
    stream, cols, consts = _pack(w)
    arrays = {
        "stream": stream, "columns": cols, "constants": consts,
        "x_in": np.ascontiguousarray(w["x"][0].T.reshape(KD, P, SEQ).transpose(1, 0, 2)),
        "ctx_in": np.ascontiguousarray(w["ctx_2"][0].T.reshape(KD, P, SEQ).transpose(1, 0, 2)),
        "positions_in": np.ascontiguousarray(np.broadcast_to(w["positions"].astype(np.int32), (P, SEQ))),
    }

    def program(known, banks):
        nc = bacc.Bacc("TRN2", target_bir_lowering=False, num_devices=1)
        args = [nc.dram_tensor(k, a.shape, mybir.dt.from_np(a.dtype), kind="ExternalInput").ap()
                for k, a in arrays.items()]
        out = nc.dram_tensor("out", (P, KD, SEQ), F32, kind="ExternalOutput").ap()
        return nc, build(nc, *args, out, known, banks)

    _, (known, banks) = program({}, {})
    nc, _ = program(known, banks)
    r = run_bass_kernel_spmd(nc, [arrays], core_ids=[0])
    y = r.results[0]["out"]
    return y.transpose(2, 1, 0).reshape(1, SEQ, D)
```

```python
from contextlib import ExitStack, contextmanager

import numpy as np
import concourse.bass as bass
from concourse import mybir

P = 128
D = 1024
KD = D // P
SEQ = 256
TOK = 2 * SEQ
DEPTH = 2
D_FF, D_FF_2 = 2816, 2752
FJ = D_FF // P
Q_RANK, KV_RANK, ROPE_A, NOPE = 384, 256, 32, 64
HEADS = 8
CONV_CH, TAPS, FFN_TAPS = 512, 31, 3
CC = CONV_CH // P
NMOD = (6, 9)
NVEC = (1, 2)
GRID_W = 64
THETA = 10000.0
EPS = 1e-6
UB = 16
RING = 4
CYCLE = UB * RING
BANKS = 6
ROWS_BANK, COLS_BANK = 6, 7
F32 = mybir.dt.float32
I32 = mybir.dt.int32
ALU = mybir.AluOpType
ACT = mybir.ActivationFunctionType
AX = mybir.AxisListType
TWO_PI = (6.28125, 0.0019350051879882812, 3.019916050561733e-07)
MASKED = -1e30


FFN_MODS = ("mod1_1", "mod2_0", "mod2_1")
MIXER_MODS = ([("mod1_0", g) for g in (2, 3, 4, 5)],
              [("mod1_1", 5)] + [("mod2_0", g) for g in (5, 6, 7, 8)],
              [("mod2_1", g) for g in (5, 6, 7, 8)])
def weight_blocks():
    s = []

    def align(m):
        while len(s) % m:
            s.append(None)

    def linear(name, nk, ns):
        for n in ns:
            for k in range(nk):
                s.append((name, k, n))

    def wide(name, nk, nn):
        align(4)
        for k in range(nk):
            for n in range(nn):
                s.append((name, k, n))

    def mods(*groups):
        align(UB)
        for name, g in groups:
            for k in range(KD):
                for n in range(KD):
                    s.append((name, k, g * KD + n))

    def ffn(up, down, guest=None):
        align(UB)
        for j in range(FJ):
            linear(up, KD, (2 * j, 2 * j + 1))
            if guest is not None and j < GU_TURNS * RING and j % RING < 2:
                for k in range(KD // 2):
                    for n in range(KD):
                        s.append((guest, j % RING * (KD // 2) + k, j // RING * KD + n))
        linear(down, FJ, range(KD))

    mods(("mod1_0", 0), ("mod1_0", 1))
    for l in range(DEPTH):
        linear(f"lat_{l}", KD, range(6))
        mods(MIXER_MODS[l][0])
        linear(f"uq_{l}", Q_RANK // P, range(HEADS))
        linear(f"uk_{l}", KV_RANK // P, range(HEADS))
        wide(f"uv_{l}", KV_RANK // P, 4)
        mods(MIXER_MODS[l][1])
        linear(f"qkb_{l}", KD, range(HEADS))
        wide(f"vb_{l}", KD, 4)
        mods(MIXER_MODS[l][2])
        linear(f"conv_{l}", KD, range(2 * CC))
        mods(*MIXER_MODS[l][3:])
        for m in range(KD):
            linear(f"gate0_{l}", KD, (m,))
            linear(f"gate1_{l}", KD, (m,))
            linear(f"gate2_{l}", KD, (m,))
            linear(f"pw2_{l}", CC, (m,))
            linear(f"oa_{l}", 4, (m,))
            linear(f"ob_{l}", 4, (m,))
        linear(f"out_{l}", KD, range(KD))
        ffn(f"up_{l}", f"down_{l}", FFN_MODS[l])
    for l in range(DEPTH):
        ffn(f"f1up_{l}", f"f1down_{l}", FFN_MODS[2] if l == 0 else None)
        if l % 2 == 0:
            linear("ain", KD, range(4))
            linear("uin", KD, range(4))
            mods(MIXER_MODS[2][0])
            wide("vin", KD, 4)
            mods(*MIXER_MODS[2][1:])
            linear("oab", KD, range(KD))
        else:
            linear("q2", KD, range(8))
            linear("k2", KD, range(2))
            wide("v2", KD, 2)
            linear("o2", KD, range(KD))
        ffn(f"f2up_{l}", f"f2down_{l}")
    align(UB)
    return s


def vector_columns():
    at, n = {}, 0
    sizes = [("inv_freq_a", 1), ("inv_freq_b", 1), ("c", KD * 32), ("eps", 1), ("g_final", KD),
             ("gq2", 1), ("gk2", 1)]
    for l in range(DEPTH):
        sizes += [(f"b_mod1_{l}", NMOD[0] * KD), (f"g_mix1_{l}", KD), (f"g_ffn1_{l}", KD),
                  (f"g_qlat_{l}", 3), (f"g_kvlat_{l}", 2), (f"g_qa_{l}", 1), (f"g_ka_{l}", 1),
                  (f"g_qb_{l}", 1), (f"g_kb_{l}", 1), (f"conv_w_{l}", TAPS * CC), (f"conv_b_{l}", CC),
                  (f"ln_g_{l}", CC), (f"ln_b_{l}", CC), (f"pw2_b_{l}", KD),
                  (f"ffn_w_{l}", FFN_TAPS * 2 * FJ), (f"ffn_b_{l}", 2 * FJ),
                  (f"b_mod2_{l}", NMOD[1] * KD * 2), (f"g2_{l}", 3 * KD)]
    for name, size in sizes:
        at[name] = (n, size)
        n += size
    return at, n


CONST_MATS = ("ones_d", "ones_q", "ones_kv", "ones_c", "head_a", "head_b", "head_c",
              "rot_a", "rot_b", "rot_c", "ident", "ws0", "ws1", "ws2", "ws3")
TABLES = (("dft_c", 256), ("cos_n", 512), ("nsin_n", 512), ("cos_c", 512), ("sin_c", 512),
          ("mask", 512), ("g_v", 512), ("b_s", 512),
          ("pick1", 2), ("pick2", 4))


def const_columns():
    at, n = {}, 0
    for name in CONST_MATS:
        at[name] = (n, P)
        n += P
    for name, size in TABLES:
        at[name] = (n, size)
        n += size
    return at, n


class Steps:

    def __init__(self, known):
        self.known, self.found, self.n, self.loop = known, {}, 0, None

    def mark(self, name=None):
        self.n += 1
        if name is not None:
            assert name not in self.found, name
            self.found[name] = (self.n, self.loop)
        return 1

    def at(self, name, turn=None):
        n, loop = self.known.get(name, (1, None))
        if loop is None:
            return n
        stride, count = self.known[("loop", loop)]
        return n + (count - 1 if turn is None else turn) * stride

    def has(self, name):
        return name in self.known

    def so_far(self, turn=None):
        if self.loop is None:
            return self.n
        return self.n + turn * self.known.get(("loop", self.loop), (1, 1))[0]

    @contextmanager
    def turns(self, engine, name, count):
        start = self.n
        self.loop = name
        with engine.Fori(0, count) as i:
            yield i
        self.loop = None
        stride = self.n - start
        self.found[("loop", name)] = (stride, count)
        self.n = start + stride * count


GU_TURNS = FJ // RING
GU_REST = FJ - GU_TURNS * RING


def build(nc, stream, cols_d, consts_d, x_d, ctx_d, pos_d, out_d, known, bank_of):
    blocks = weight_blocks()
    vcol, vcols = vector_columns()
    ccol, ccols = const_columns()
    T, A, V = (Steps(known.get(e, {})) for e in "TAV")
    new_banks = {}

    ctx = ExitStack()
    with ctx:
        def sb(name, shape, dt=F32):
            return ctx.enter_context(nc.sbuf_tensor(name, shape, dt))

        def sem(name):
            return ctx.enter_context(nc.semaphore(name))

        ring = sb("ring", [P, RING, UB * P])
        x = sb("x_sb", [P, KD, TOK])
        h = sb("h_sb", [P, KD, TOK])
        hid = sb("hid", [P, FJ, TOK])
        cols = sb("cols", [P, vcols])
        consts = sb("consts", [P, ccols])
        silu_c = sb("silu_c", [P, KD, 32])
        mods_sb = sb("mods_sb", [P, 2, NMOD[1] * KD * 2])
        rows = sb("rows", [P, 512])
        amod = sb("amod", [P, 3, KD, 2])
        rs = sb("rs", [P, TOK])
        qt = sb("qt", [P, HEADS, SEQ])
        kt = sb("kt", [P, HEADS, SEQ])
        sq = sb("sq", [P, HEADS, SEQ])
        hrs = sb("hrs", [P, 2, TOK])
        rt = sb("rt", [P, 2, TOK])
        va = sb("va", [P, 2, 512])
        vb = sb("vb", [P, 2, 512])
        z = sb("z", [P, 2, 2, SEQ + FFN_TAPS - 1])
        zc = rt[:, :, :].rearrange("p s (a t) -> p s a t", a=2)
        sg = sb("sg", [P, 2, TOK])
        sg2 = sb("sg2", [P, 2, SEQ])
        probs = sb("probs", [P, 2, 512])
        probs_t = sb("probs_t", [P, 2, 512])
        stat = sb("stat", [P, 2, 8])
        cos_a = sb("cos_a", [P, SEQ])
        sin_a = sb("sin_a", [P, SEQ])
        cos_b = sb("cos_b", [P, SEQ])
        sin_b = sb("sin_b", [P, SEQ])
        pos_i = sg2[:, 0, :].bitcast(I32)

        flat = hid[:, :, :].rearrange("p j t -> p (j t)")

        def part(start, n, **dims):
            names = " ".join(dims)
            return flat[:, start:start + n].rearrange(f"p ({names}) -> p {names}", **dims)

        attn = part(0, 8 * SEQ, c=8, t=SEQ)
        u_pad = part(2048, CC * (SEQ + TAPS - 1), c=CC, t=SEQ + TAPS - 1)
        u_end = 2048 + CC * (SEQ + TAPS - 1)
        dwc = part(u_end, CC * SEQ, c=CC, t=SEQ)
        csq = part(u_end + 1024, CC * SEQ, c=CC, t=SEQ)
        oc = part(u_end + 2048, CC * SEQ, c=CC, t=SEQ)
        lat = part(u_end + 3072, 6 * SEQ, c=6, t=SEQ)
        merged = qt
        bt = part(u_end + 5120, HEADS * SEQ, c=HEADS, t=SEQ)
        mixed = part(0, KD * TOK, c=KD, t=TOK)
        spec = part(4096, 4 * 4 * 256, t=4, g=4, f=256)
        a_in = part(8192, 4 * TOK, g=4, t=TOK)

        ps = ctx.enter_context(nc.psum_tensor("ps", [P, 8, 512], F32))

        tensor_done = sem("tensor_done")
        scalar_done = sem("scalar_done")
        vector_done = sem("vector_done")
        inputs_landed = sem("inputs_landed")
        weights_landed = [sem(f"weights_landed{s}") for s in range(RING)]
        output_stored = sem("output_stored")
        N_IN = 5 * 16

        def col(name, k=0, n=1):
            return cols[:, vcol[name][0] + k:vcol[name][0] + k + n]

        def mat(name):
            return consts[:, ccol[name][0]:ccol[name][0] + ccol[name][1]]

        def bank(g):
            return ps[:, bank_of.get(g, 0), :]

        block = ctx.enter_context(nc.Block())

        units = len(blocks) // UB
        loops = {}
        for b, name, turns, width in loop_starts(blocks):
            loops[b // UB] = (name, turns, width)

        @block.sync
        def _(sp):
            sp.dma_start(cols[:, :], cols_d).then_inc(inputs_landed, 16)
            sp.dma_start(pos_i[:, :], pos_d).then_inc(inputs_landed, 16)

            def load(u, slot):
                sp.dma_start(ring[:, slot, :], stream[u, :, :]).then_inc(weights_landed[slot], 16)

            def slot_read(u):
                if u >= RING:
                    name, turn = unit_step(u - RING)
                    sp.wait_ge(tensor_done, T.at(name, turn))

            def unit_step(u):
                for u0, (name, turns, width) in loops.items():
                    if u0 <= u < u0 + turns * width:
                        return ("unit", u0 + (u - u0) % width), (u - u0) // width
                return ("unit", u), None

            u = 0
            while u < units:
                if u in loops:
                    name, turns, width = loops[u]
                    for s in range(width):
                        slot_read(u + s)
                        load(u + s, (u + s) % RING)
                    with sp.Fori(1, turns) as i:
                        for s in range(width):
                            sp.wait_ge(tensor_done, T.at(("unit", u + s - RING), i) if s >= RING else
                                       T.at(("unit", u + s - RING + width), i - 1))
                            src = stream[bass.ds(i * width + (u + s), 1), :, :]
                            sp.dma_start(ring[:, (u + s) % RING, :], src.rearrange("a p n -> (a p) n"))\
                              .then_inc(weights_landed[(u + s) % RING], 16)
                    u += turns * width
                else:
                    slot_read(u)
                    load(u, u % RING)
                    if u == 1:
                        sp.dma_start(consts[:, :], consts_d).then_inc(inputs_landed, 16)
                        sp.dma_start(x[:, :, 0:SEQ], x_d).then_inc(inputs_landed, 16)
                        sp.dma_start(x[:, :, SEQ:TOK], ctx_d).then_inc(inputs_landed, 16)
                    u += 1
            sp.wait_ge(vector_done, V.at("final"))
            sp.dma_start(out_d, h[:, :, 0:SEQ]).then_inc(output_stored, 16)
            sp.wait_ge(output_stored, 16)

        @block.tensor
        def _(pe):
            cur = [0]
            nbank = [0]
            tenant = {}
            turn_units = [RING]

            def take_bank(g, i=None):
                b = nbank[0] % BANKS
                nbank[0] += 1
                old = tenant.get(b)
                if i is None and old is not None:
                    wait_read(old)
                new_banks[g] = b
                tenant[b] = g
                return ps[:, b, :]

            def wait_read(g, turn=None):
                if A.has(("read", g)):
                    pe.wait_ge(scalar_done, A.at(("read", g), turn))
                if V.has(("read", g)):
                    pe.wait_ge(vector_done, V.at(("read", g), turn))

            def weights(name, k, n, width=1, i=None):
                while blocks[cur[0]] is None:
                    cur[0] += 1
                b = cur[0]
                assert blocks[b] == (name, k, n), (blocks[b], name, k, n)
                slot, at = (b // UB) % RING, b % UB
                if at == 0:
                    lands = 16 * (b // UB // RING + 1)
                    pe.wait_ge(weights_landed[slot], lands if i is None else lands + 16 * (turn_units[0] // RING) * i)
                cur[0] += width
                e = b + width
                last = e % UB == 0 or all(q is None for q in blocks[e:e + UB - e % UB])
                return ring[:, slot, at * P:(at + width) * P], ("unit", b // UB) if last else None

            def product(out, lhsT, rhs, first, last, done=None, unit=None):
                ins = nc.tensor.matmul(out, lhsT, rhs, start=first, stop=last)
                if unit is not None:
                    T.found[unit] = (T.n + 1, T.loop)
                if done is not None or unit is not None:
                    ins.then_inc(tensor_done, T.mark(done))

            def linear(out, name, nk, n, act, done=None, ready=None, i=None):
                for k in range(nk):
                    if ready is not None:
                        ready(k)
                    w, unit = weights(name, k, n, i=i)
                    product(out, w, act(k), k == 0, k == nk - 1, done if k == nk - 1 else None, unit)

            def once(fn):
                seen = set()

                def ready(k):
                    if k not in seen:
                        seen.add(k)
                        fn(k)
                return ready

            def norm(p, T_):
                out = take_bank((p, "ms"))
                for k in range(KD):
                    pe.wait_ge(scalar_done, A.at((p, "sq", k)))
                    product(out[:, 0:T_], mat("ones_d"), h[:, k, 0:T_], k == 0, k == KD - 1,
                            (p, "ms") if k == KD - 1 else None)
                return once(lambda k: pe.wait_ge(scalar_done, A.at((p, "h", k))))

            def mod_rows(name, g, half=None, i=None, before=None):
                if half != 1:
                    for q in before or last_mod:
                        pe.wait_ge(scalar_done, A.at(("read", (q, "rows")), None if before is None else i - 1))
                for k in range(KD) if half is None else range(half * KD // 2, (half + 1) * KD // 2):
                    for r in range(2):
                        w, unit = weights(name, k, g * KD + 4 * r, 4, i)
                        t = 32 * (2 * (k % 2) + r)
                        done = ((name, g), "rows") if k == KD - 1 and r == 1 else None
                        product(ps[t:t + 32, ROWS_BANK, :], silu_c[:, k, :], w, k < 2, k >= KD - 2, done, unit)

            def mod_cols(name, g, i=None, before=None):
                n = 2 * NVEC[int(name[3]) - 1]
                for q in before or last_mod:
                    pe.wait_ge(vector_done, V.at(("read", (q, "cols")), None if before is None else i - 1))
                pe.wait_ge(scalar_done, A.at(("read", ((name, g), "rows")), i))
                for q in range(4):
                    product(ps[:, COLS_BANK, q * n:(q + 1) * n], rows[:, q * P:(q + 1) * P], mat(f"pick{name[3]}"),
                            True, True, ((name, g), "cols") if q == 3 else None)
                last_mod[:] = [(name, g)]

            last_mod, pending = [], []

            def hook(*group):
                if pending:
                    mod_cols(*pending.pop())
                if group:
                    mod_rows(*group)
                    pending.append(group)

            def ffn(p, up, down, T_, ready, guest=None):
                while blocks[cur[0]] is None:
                    cur[0] += 1
                b0 = cur[0]
                shared = T_ == SEQ
                kinds = ("up",) if shared else ("gate", "up")

                def pair(j, outs, i=None):
                    if shared:
                        linear(outs[0][:, 0:SEQ], up, KD, 2 * j, lambda k: h[:, k, 0:SEQ], i=i)
                        linear(outs[0][:, SEQ:TOK], up, KD, 2 * j + 1, lambda k: h[:, k, 0:SEQ], (p, "up", j), i=i)
                    else:
                        linear(outs[0], up, KD, 2 * j, lambda k: h[:, k, :], (p, "gate", j), i=i)
                        linear(outs[1], up, KD, 2 * j + 1, lambda k: h[:, k, :], (p, "up", j), i=i)

                for k in range(KD):
                    ready(k)
                names = [(p, kind, j) for j in range(RING) for kind in kinds]
                free = [take_bank(names[n] if n < len(names) else (p, "spare", n), None) for n in range(BANKS)]
                for n, g in enumerate(names):
                    b = (nbank[0] + n) % BANKS
                    new_banks[g] = b
                    tenant[b] = g
                turn_units[0] = 2 * RING if guest else RING
                if guest:
                    hook()
                with T.turns(pe, (p, "up"), GU_TURNS) as i:
                    for n, g in enumerate(names):
                        same = n - BANKS
                        if same >= 0:
                            wait_read(names[same], i)
                        else:
                            held = [m for m in range(len(names)) if m % BANKS == n % BANKS][-1]
                            wait_read(names[held], i - 1)
                        if g[1] == "up":
                            j = g[2]
                            outs = [ps[:, new_banks[(p, kind, j)], :] for kind in kinds]
                            pair(j, outs, i)
                            if guest and j < 2:
                                mod_rows(guest, 0, j, i, [(guest, 0)])
                            if guest and j == 2:
                                mod_cols(guest, 0, i, [(guest, 0)])
                cur[0] = b0 + GU_TURNS * turn_units[0] * UB
                for j in range(GU_TURNS * RING, FJ):
                    pair(j, [take_bank((p, kind, j)) for kind in kinds])
                for m in range(KD):
                    out = take_bank((p, "down", m))
                    linear(out[:, 0:T_], down, FJ, m, lambda k: hid[:, k, 0:T_], (p, "down", m),
                           once(lambda k: pe.wait_ge(vector_done, V.at(*hid_step(p, k)))) if m == 0 else None)

            def head_norm(p, pairs, head, rot, tile):
                for c in range(pairs):
                    out = take_bank((p, "hms", c))
                    pe.wait_ge(scalar_done, A.at((p, "hsq", c)))
                    product(out, mat(head), pair_of(sq, c), True, True, (p, "hms", c))
                    if c >= 1:
                        rotate(p, c - 1, rot, tile)
                rotate(p, pairs - 1, rot, tile)

            def rotate(p, c, rot, tile):
                out = take_bank((p, "rot", c))
                pe.wait_ge(vector_done, V.at((p, "hn", c)))
                product(out, mat(rot), pair_of(tile, c), True, True, (p, "rot", c))

            def attention(p, tasks, scores, values, ready):
                ready()
                for t in range(tasks + 3):
                    if t < tasks:
                        out = take_bank((p, "s", t))
                        scores(t, out)
                    if 2 <= t < tasks + 2:
                        s = t - 2
                        out = take_bank((p, "pt", s))
                        pe.wait_ge(vector_done, V.at((p, "p", s)))
                        order = transposed_order(p)
                        for b in range(4):
                            ins = nc.tensor.transpose(out[:, order[b] * P:(order[b] + 1) * P],
                                                      probs[:, s % 2, b * P:(b + 1) * P], mat("ident"))
                        ins.then_inc(tensor_done, T.mark((p, "pt", s)))
                    if t >= 3:
                        s = t - 3
                        pe.wait_ge(scalar_done, A.at((p, "ptc", s)))
                        values(s)

            pe.wait_ge(inputs_landed, N_IN)
            pe.wait_ge(scalar_done, A.at("silu c"))
            hook("mod1_0", 0)
            hook("mod1_0", 1)
            hook()
            for l in range(DEPTH):
                p = ("b1", l)
                guests = MIXER_MODS[l]
                ready = norm((*p, "mix"), SEQ)
                hx = lambda k: h[:, k, 0:SEQ]
                for c in range(3):
                    out = take_bank((p, "lat", c))
                    linear(out[:, 0:SEQ], f"lat_{l}", KD, 2 * c, hx, None, ready)
                    linear(out[:, SEQ:TOK], f"lat_{l}", KD, 2 * c + 1, hx, (p, "lat", c))
                hook(*guests[0])
                out = take_bank((p, "latms"))
                for k in range(5):
                    pe.wait_ge(scalar_done, A.at((p, "latsq", k // 2)))
                    q = k < 3
                    product(out[:, 0:SEQ] if q else out[:, SEQ:TOK], mat("ones_q" if q else "ones_kv"),
                            sq[:, k, :], k in (0, 3), k in (2, 4), (p, "latms") if k == 4 else None)
                for c in range(4):
                    out = take_bank((p, "uq", c))
                    for e in range(2):
                        linear(out[:, e * SEQ:(e + 1) * SEQ], f"uq_{l}", 3, 2 * c + e,
                               lambda k: lat[:, k, :], (p, "uq", c) if e else None,
                               (lambda k: pe.wait_ge(vector_done, V.at((p, "latn", k)))) if c == e == 0 else None)
                for c in range(4):
                    out = take_bank((p, "uk", c))
                    for e in range(2):
                        linear(out[:, e * SEQ:(e + 1) * SEQ], f"uk_{l}", 2, 2 * c + e,
                               lambda k: lat[:, 3 + k, :], (p, "uk", c) if e else None,
                               (lambda k: pe.wait_ge(vector_done, V.at((p, "latn", 3 + k)))) if c == e == 0 else None)
                outs = [take_bank((p, "va", b)) for b in range(2)]
                for k in range(2):
                    w, unit = weights(f"uv_{l}", k, 0, 4)
                    for b in range(2):
                        product(outs[b], lat[:, 3 + k, b * P:(b + 1) * P], w, k == 0, k == 1,
                                (p, "va", b) if k == 1 else None, unit if b == 1 else None)
                hook(*guests[1])
                head_norm((p, "qa"), 4, "head_a", "rot_a", qt)
                for c in range(4):
                    out = take_bank((p, "qkb", c))
                    linear(out[:, 0:SEQ], f"qkb_{l}", KD, 2 * c, hx)
                    linear(out[:, SEQ:TOK], f"qkb_{l}", KD, 2 * c + 1, hx, (p, "qkb", c))
                head_norm((p, "ka"), 4, "head_a", "rot_a", kt)
                outs = [take_bank((p, "vb", b)) for b in range(2)]
                for k in range(KD):
                    w, unit = weights(f"vb_{l}", k, 0, 4)
                    for b in range(2):
                        product(outs[b], h[:, k, b * P:(b + 1) * P], w, k == 0, k == KD - 1,
                                (p, "vb", b) if k == KD - 1 else None, unit if b == 1 else None)
                hook(*guests[2])
                head_norm((p, "qkb"), 4, "head_b", "rot_b", bt)
                for c in range(CC):
                    out = take_bank((p, "conv", c))
                    linear(out[:, 0:SEQ], f"conv_{l}", KD, 2 * c, hx)
                    linear(out[:, SEQ:TOK], f"conv_{l}", KD, 2 * c + 1, hx, (p, "conv", c))

                for guest in guests[3:]:
                    hook(*guest)

                def scores(t, out):
                    for b in range(2):
                        if t < HEADS:
                            q, k = qt[:, t, b * P:(b + 1) * P], kt[:, t, :]
                        else:
                            c, r = (t - HEADS) // 2, 64 * (t % 2)
                            q, k = bt[r:r + 64, c, b * P:(b + 1) * P], bt[r:r + 64, 4 + c, :]
                        product(out[:, b * SEQ:(b + 1) * SEQ], q, k, True, True, ((p, "at"), "s", t) if b else None)

                held = [None]

                def values(s):
                    r = 64 * (s % 2)
                    if s % 2 == 0:
                        held[0] = take_bank(((p, "at"), "o", s // 2))
                    v, hh = (va, s) if s < HEADS else (vb, s - HEADS)
                    if s == 0:
                        pe.wait_ge(scalar_done, A.at(("read", (p, "vb", 1))))
                    for b in range(2):
                        product(held[0][r:r + 64, 0:SEQ], v[:, b, hh * 64:(hh + 1) * 64],
                                probs_t[:, s % 2, b * SEQ:(b + 1) * SEQ], b == 0, b == 1,
                                ((p, "at"), "o", s // 2) if b and s % 2 else (((p, "at"), "ov", s) if b else None))

                attention((p, "at"), 16, scores, values,
                          lambda: pe.wait_ge(vector_done, V.at(((p, "qkb"), "roped", 3))))
                out = take_bank((p, "lnm"))
                pe.wait_ge(vector_done, V.at((p, "dwc")))
                for k in range(CC):
                    product(out[:, 0:SEQ], mat("ones_c"), dwc[:, k, :], k == 0, k == CC - 1,
                            (p, "lnm") if k == CC - 1 else None)
                out = take_bank((p, "lnv"))
                pe.wait_ge(scalar_done, A.at((p, "csq")))
                for k in range(CC):
                    product(out[:, 0:SEQ], mat("ones_c"), csq[:, k, :], k == 0, k == CC - 1,
                            (p, "lnv") if k == CC - 1 else None)
                hook()
                for m in range(KD):
                    out = take_bank((p, "g01", m))
                    linear(out[:, 0:SEQ], f"gate0_{l}", KD, m, hx)
                    linear(out[:, SEQ:TOK], f"gate1_{l}", KD, m, hx, (p, "g01", m))
                    out = take_bank((p, "g2c", m))
                    linear(out[:, 0:SEQ], f"gate2_{l}", KD, m, hx, (p, "g2", m))
                    if m == 0:
                        pe.wait_ge(scalar_done, A.at((p, "oc")))
                    linear(out[:, SEQ:TOK], f"pw2_{l}", CC, m, lambda k: oc[:, k, :], (p, "g2c", m))
                    out = take_bank((p, "oab", m))
                    if m == 0:
                        pe.wait_ge(scalar_done, A.at(("read", ((p, "at"), "o", 7))))
                    linear(out[:, 0:SEQ], f"oa_{l}", 4, m, lambda k: attn[:, k, :])
                    linear(out[:, SEQ:TOK], f"ob_{l}", 4, m, lambda k: attn[:, 4 + k, :], (p, "oab", m))
                for m in range(KD):
                    out = take_bank((p, "out", m))
                    linear(out[:, 0:SEQ], f"out_{l}", KD, m, lambda k: merged[:, k, :], (p, "out", m),
                           (lambda k: pe.wait_ge(vector_done, V.at((p, "merged", k)))) if m == 0 else None)
                ready = norm((*p, "ffn"), SEQ)
                ffn((*p, "ffn"), f"up_{l}", f"down_{l}", SEQ, ready, FFN_MODS[l])

            for l in range(DEPTH):
                p = ("b2", l)
                ready = norm((*p, "f1"), TOK)
                ffn((*p, "f1"), f"f1up_{l}", f"f1down_{l}", TOK, ready, FFN_MODS[2] if l == 0 else None)
                ready = norm((*p, "mix"), TOK)
                hx = lambda k: h[:, k, :]
                if l % 2 == 0:
                    for g in range(4):
                        linear(take_bank((p, "a", g)), "ain", KD, g, hx, (p, "a", g), ready)
                    for g in range(4):
                        linear(take_bank((p, "u", g)), "uin", KD, g, hx, (p, "u", g))
                    hook(*MIXER_MODS[2][0])
                    outs = [take_bank((p, "v", b)) for b in range(4)]
                    for k in range(KD):
                        w, unit = weights("vin", k, 0, 4)
                        for b in range(4):
                            product(outs[b], h[:, k, b * P:(b + 1) * P], w, k == 0, k == KD - 1,
                                    (p, "v", b) if k == KD - 1 else None, unit if b == 3 else None)
                    for guest in MIXER_MODS[2][1:]:
                        hook(*guest)
                    hook()
                    for b in range(4):
                        for q in range(2):
                            out = take_bank((p, "sp", b, q))
                            for e in range(2):
                                g = 2 * q + e
                                if b == 0:
                                    pe.wait_ge(scalar_done, A.at(("read", (p, "a", g))))
                                product(out[:, e * 256:(e + 1) * 256], a_in[:, g, b * P:(b + 1) * P],
                                        mat("dft_c"), True, True, (p, "sp", b, q) if e else None)
                    for g in range(4):
                        out = take_bank((p, "f", g))
                        for s in range(2):
                            for b in range(2):
                                t = 2 * s + b
                                if g == 0:
                                    pe.wait_ge(scalar_done, A.at(("read", (p, "sp", t, 1))))
                                o = out[:, s * SEQ:(s + 1) * SEQ]
                                product(o, spec[:, t, g, 0:128], mat("cos_n")[:, b * 256:(b + 1) * 256],
                                        b == 0, False)
                                product(o, spec[:, t, g, 128:256], mat("nsin_n")[:, b * 256:(b + 1) * 256],
                                        False, b == 1, (p, "f", g) if s and b else None)
                    for g in range(4):
                        out = take_bank((p, "mx", g))
                        if g == 0:
                            pe.wait_ge(vector_done, V.at((p, "vn")))
                        for t in range(4):
                            product(out[:, t * P:(t + 1) * P], vt_of(kt)[:, t, g * P:(g + 1) * P], mat(f"ws{g}"),
                                    True, True, (p, "mx", g) if t == 3 else None)
                    for m in range(KD):
                        linear(take_bank((p, "out", m)), "oab", KD, m, lambda k: mixed[:, k, :], (p, "out", m),
                               (lambda k: pe.wait_ge(scalar_done, A.at(("read", (p, "f", k)))) if k < 4 else
                                pe.wait_ge(vector_done, V.at((p, "sgu", k - 4)))) if m == 0 else None)
                else:
                    for c in range(4):
                        out = take_bank((p, "q", c))
                        linear(out[:, 0:SEQ], "q2", KD, 2 * c, lambda k: h[:, k, 0:SEQ], None, ready)
                        linear(out[:, SEQ:TOK], "q2", KD, 2 * c + 1, lambda k: h[:, k, 0:SEQ], (p, "q", c))
                    for c in range(2):
                        linear(take_bank((p, "k", c)), "k2", KD, c, hx, (p, "k", c))
                    outs = [take_bank((p, "v", b)) for b in range(4)]
                    for k in range(KD):
                        w, unit = weights("v2", k, 0, 2)
                        for b in range(4):
                            product(outs[b][:, 0:256], h[:, k, b * P:(b + 1) * P], w, k == 0, k == KD - 1,
                                    (p, "v", b) if k == KD - 1 else None, unit if b == 3 else None)
                    head_norm((p, "q"), 4, "head_c", "rot_c", qt)
                    head_norm((p, "k"), 2, "head_c", "rot_c", kt)
                    held = [None]

                    def scores(t, out):
                        hh, b = divmod(t, 2)
                        product(out, qt[:, hh, b * P:(b + 1) * P], pair_of(kt, hh // 4), True, True,
                                ((p, "at"), "s", t))

                    def values(s):
                        hh, b = divmod(s, 2)
                        if b == 0:
                            held[0] = take_bank(((p, "at"), "o", hh))
                        for c in range(4):
                            product(held[0][:, b * P:(b + 1) * P], v2_of(va)[:, c, (hh // 4) * P:(hh // 4 + 1) * P],
                                    probs_t[:, s % 2, c * P:(c + 1) * P], c == 0, c == 3,
                                    (((p, "at"), "o", hh) if b else ((p, "at"), "ov", s)) if c == 3 else None)

                    def both():
                        pe.wait_ge(vector_done, V.at(((p, "k"), "roped", 1)))
                        pe.wait_ge(scalar_done, A.at(("read", (p, "v", 3))))

                    attention((p, "at"), 16, scores, values, both)
                    for m in range(KD):
                        out = take_bank((p, "out", m))
                        linear(out[:, 0:SEQ], "o2", KD, m, lambda k: attn[:, k, :], (p, "out", m),
                               (lambda k: pe.wait_ge(scalar_done, A.at(("read", ((p, "at"), "o", k))))) if m == 0 else None)
                T_ = TOK if l == 0 else SEQ
                ready = norm((*p, "f2"), T_)
                ffn2(p, l, T_, ready, ffn)
            norm("fin", SEQ)

        @block.scalar
        def _(act):
            def own(i=None):
                if A.n:
                    act.wait_ge(scalar_done, A.so_far(i))

            def norm(p, T_, halves, after, shift):
                for k in range(KD):
                    if after is not None:
                        act.wait_ge(vector_done, V.at(after(k)))
                    nc.scalar.activation(h[:, k, 0:T_], x[:, k, 0:T_], ACT.Square)\
                      .then_inc(scalar_done, A.mark((p, "sq", k)))
                act.wait_ge(tensor_done, T.at((p, "ms")))
                nc.scalar.activation(rs[:, 0:T_], bank((p, "ms"))[:, 0:T_], ACT.Sqrt, bias=col("eps"))\
                  .then_inc(scalar_done, A.mark(("read", (p, "ms"))))
                if shift is None:
                    return
                for k in range(KD):
                    act.wait_ge(vector_done, V.at((p, "hn", k)))
                    for v in range(halves):
                        t = slice(v * SEQ, (v + 1) * SEQ)
                        nc.scalar.activation(h[:, k, t], h[:, k, t], ACT.Identity, bias=shift(k, v))\
                          .then_inc(scalar_done, A.mark((p, "h", k) if v == halves - 1 else None))

            def copy_pair(dst, g, read=True):
                act.wait_ge(tensor_done, T.at(g))
                nc.scalar.activation(dst, bank(g), ACT.Copy)\
                  .then_inc(scalar_done, A.mark(("read", g) if read else None))

            def squares(p, pairs, tile, from_bank=None):
                for c in range(pairs):
                    if from_bank is not None:
                        copy_pair(pair_of(tile, c), from_bank(c))
                    own()
                    nc.scalar.activation(pair_of(sq, c), pair_of(tile, c), ACT.Square)\
                      .then_inc(scalar_done, A.mark((p, "hsq", c)))

            def roots(p, pairs):
                for c in range(pairs):
                    act.wait_ge(tensor_done, T.at((p, "hms", c)))
                    if c >= 2:
                        act.wait_ge(vector_done, V.at((p, "hn", c - 2)))
                    nc.scalar.activation(hrs[:, c % 2, :], bank((p, "hms", c)), ACT.Sqrt, bias=col("eps"))\
                      .then_inc(scalar_done, A.mark(("read", (p, "hms", c))))

            def softmax(p, t, J, scale):
                act.wait_ge(vector_done, V.at((p, "nm", t)))
                W = 512 // J
                for b in range(J):
                    nc.scalar.activation(probs[:, t % 2, b * W:(b + 1) * W], probs[:, t % 2, b * W:(b + 1) * W],
                                         ACT.Exp, bias=stat[:, t % 2, b:b + 1], scale=scale,
                                         accum_out=stat[:, t % 2, 2 + b:3 + b])\
                      .then_inc(scalar_done, A.mark((p, "e", t) if b == J - 1 else None))

            def attention(p, tasks, J, scale, out_of):
                for t in range(tasks + 2):
                    if t < tasks:
                        softmax(p, t, J, scale(t))
                    if t >= 1 and t - 1 < tasks:
                        s = t - 1
                        act.wait_ge(tensor_done, T.at((p, "pt", s)))
                        if s >= 2:
                            act.wait_ge(tensor_done, T.at(out_step(p, s - 2)))
                        nc.scalar.activation(probs_t[:, s % 2, :], bank((p, "pt", s)), ACT.Copy)\
                          .then_inc(scalar_done, A.mark((p, "ptc", s)))
                        A.found[("read", (p, "pt", s))] = A.found[(p, "ptc", s)]
                    if t >= 2 and (t - 2) % 2 == 1:
                        c = (t - 2) // 2
                        act.wait_ge(tensor_done, T.at((p, "o", c)))
                        nc.scalar.activation(out_of(c), bank((p, "o", c))[:, 0:SEQ], ACT.Copy)\
                          .then_inc(scalar_done, A.mark(("read", (p, "o", c))))

            def ffn1(p, guest):
                def pair(j, i=None, turn=None, first=False):
                    act.wait_ge(tensor_done, T.at((p, "up", j), i))
                    if not first:
                        act.wait_ge(vector_done, conv_before(V, p, j, i))
                    nc.scalar.activation(z[:, j % 2, :, FFN_TAPS - 1:], two(bank((p, "up", j))), ACT.Copy)\
                      .then_inc(scalar_done, A.mark((p, "z", j)))
                    A.found[("read", (p, "up", j))] = A.found[(p, "z", j)]

                def silu(j, i=None):
                    act.wait_ge(vector_done, V.at((p, "cv", j), i))
                    nc.scalar.activation(zc[:, j % 2, 0, :], zc[:, j % 2, 0, :], ACT.Silu)\
                      .then_inc(scalar_done, A.mark((p, "si", j)))

                cols_before[:] = [(guest, 0)]
                with A.turns(act, (p, "up"), GU_TURNS) as i:
                    for j in range(RING):
                        pair(j, i)
                        if j == 1:
                            mod_rows(guest, 0, i)
                        silu(j, i)
                for j in range(GU_TURNS * RING, FJ):
                    pair(j)
                    silu(j)

            def ffn2_(p, T_, guest=None):
                def gate(j, i=None):
                    g = (p, "up", j) if T_ == SEQ else (p, "gate", j)
                    act.wait_ge(tensor_done, T.at(g, i))
                    act.wait_ge(vector_done, conv_before(V, p, j, i))
                    ins = nc.scalar.activation(sg[:, j % 2, 0:T_], bank(g)[:, 0:T_], ACT.Silu)
                    ins.then_inc(scalar_done, A.mark((p, "si", j)))
                    A.found[("read", g)] = A.found[(p, "si", j)]

                if guest:
                    cols_before[:] = [(guest, 0)]
                with A.turns(act, (p, "up"), GU_TURNS) as i:
                    for j in range(RING):
                        gate(j, i)
                        if guest and j == 1:
                            mod_rows(guest, 0, i)
                for j in range(GU_TURNS * RING, FJ):
                    gate(j)

            def mod_rows(name, g, i=None):
                act.wait_ge(tensor_done, T.at(((name, g), "rows"), i))
                if cols_before:
                    act.wait_ge(tensor_done, T.at((cols_before[0], "cols"), None if i is None else i - 1))
                nc.scalar.activation(rows[:, :], ps[:, ROWS_BANK, :], ACT.Copy)\
                  .then_inc(scalar_done, A.mark(("read", ((name, g), "rows"))))
                cols_before[:] = [(name, g)]

            cols_before = []

            act.wait_ge(inputs_landed, N_IN)
            nc.scalar.activation(silu_c[:, :, :], col("c", 0, KD * 32).rearrange("p (k v) -> p k v", v=32), ACT.Silu)\
              .then_inc(scalar_done, A.mark("silu c"))
            mod_rows("mod1_0", 0)
            mod_rows("mod1_0", 1)
            for n, t in enumerate((cos_a, sin_a, cos_b, sin_b)):
                act.wait_ge(vector_done, V.at(("angle", n)))
                nc.scalar.activation(t[:, :], t[:, :], ACT.Sin).then_inc(scalar_done, A.mark(("table", n)))
            for l in range(DEPTH):
                p = ("b1", l)
                norm((*p, "mix"), SEQ, 1, None if l == 0 else lambda k: x_step(("b1", l - 1, "ffn"), "down", k),
                     lambda k, v: mods_sb[:, l, k:k + 1])
                for c in range(3):
                    copy_pair(lat[:, 2 * c:2 * c + 2, :].rearrange("p a t -> p (a t)"), (p, "lat", c))
                    own()
                    nc.scalar.activation(sq[:, 2 * c:2 * c + 2, :], lat[:, 2 * c:2 * c + 2, :], ACT.Square)\
                      .then_inc(scalar_done, A.mark((p, "latsq", c)))
                guests = MIXER_MODS[l]
                act.wait_ge(tensor_done, T.at((p, "latms")))
                nc.scalar.activation(rs[:, :], bank((p, "latms")), ACT.Sqrt, bias=col("eps"))\
                  .then_inc(scalar_done, A.mark(("read", (p, "latms"))))
                mod_rows(*guests[0])
                squares((p, "qa"), 4, qt, lambda c: (p, "uq", c))
                for c in range(4):
                    act.wait_ge(tensor_done, T.at((p, "uk", c)))
                    nc.scalar.activation(kt[0:64, 2 * c:2 * c + 2, :], two(bank((p, "uk", c)))[0:64], ACT.Copy)\
                      .then_inc(scalar_done, A.mark(("read", (p, "uk", c))))
                for b in range(2):
                    copy_pair(va[:, b, :], (p, "va", b))
                shared = lat[64:96, 5:6, :].to_broadcast([32, HEADS, SEQ])
                nc.scalar.activation(kt[64:96, :, :], shared, ACT.Copy).then_inc(scalar_done, A.mark())
                mod_rows(*guests[1])
                roots((p, "qa"), 4)
                squares((p, "ka"), 4, kt)
                for c in range(4):
                    copy_pair(pair_of(bt, c), (p, "qkb", c))
                roots((p, "ka"), 4)
                squares((p, "qkb"), 4, bt)
                for b in range(2):
                    copy_pair(vb[:, b, :], (p, "vb", b))
                mod_rows(*guests[2])
                roots((p, "qkb"), 4)
                for c in range(CC):
                    act.wait_ge(tensor_done, T.at((p, "conv", c)))
                    if c >= 2:
                        act.wait_ge(vector_done, V.at(("read", (p, "conv", c - 2))))
                    nc.scalar.activation(sg2[:, c % 2, :], bank((p, "conv", c))[:, SEQ:TOK], ACT.Sigmoid)\
                      .then_inc(scalar_done, A.mark((p, "glu", c)))
                for guest in guests[3:]:
                    mod_rows(*guest)
                attention((p, "at"), 16, 2, lambda t: (NOPE + ROPE_A) ** -0.5 if t < HEADS else 64 ** -0.5,
                          lambda c: attn[:, c, :])
                act.wait_ge(vector_done, V.at((p, "cen")))
                nc.scalar.activation(csq[:, :, :], dwc[:, :, :], ACT.Square).then_inc(scalar_done, A.mark((p, "csq")))
                act.wait_ge(tensor_done, T.at((p, "lnv")))
                nc.scalar.activation(rs[:, 0:SEQ], bank((p, "lnv"))[:, 0:SEQ], ACT.Sqrt, bias=col("eps"))\
                  .then_inc(scalar_done, A.mark(("read", (p, "lnv"))))
                act.wait_ge(vector_done, V.at((p, "lnn")))
                for c in range(CC):
                    nc.scalar.activation(oc[:, c, :], dwc[:, c, :], ACT.Silu, bias=col(f"ln_b_{l}", c),
                                         scale=col(f"ln_g_{l}", c))\
                      .then_inc(scalar_done, A.mark((p, "oc") if c == CC - 1 else None))
                for m in range(KD):
                    if m >= 2:
                        act.wait_ge(vector_done, V.at((p, "merged", m - 2)))
                    act.wait_ge(tensor_done, T.at((p, "g01", m)))
                    nc.scalar.activation(sg[:, m % 2, :], bank((p, "g01", m)), ACT.Sigmoid)\
                      .then_inc(scalar_done, A.mark(("read", (p, "g01", m))))
                    act.wait_ge(tensor_done, T.at((p, "g2c", m)))
                    nc.scalar.activation(sg2[:, m % 2, :], bank((p, "g2c", m))[:, 0:SEQ], ACT.Sigmoid)\
                      .then_inc(scalar_done, A.mark((p, "sg2", m)))
                norm((*p, "ffn"), SEQ, 1, lambda k: x_step(p, "out", k), lambda k, v: mods_sb[:, l, 3 * KD + k:3 * KD + k + 1])
                ffn1((*p, "ffn"), FFN_MODS[l])
            for l in range(DEPTH):
                p = ("b2", l)

                def shift(n):
                    return lambda k, v: mods_sb[:, l, (n * KD + k) * 2 + v:(n * KD + k) * 2 + v + 1]

                before = ("b1", 1, "ffn") if l == 0 else ("b2", 0, "f2")
                norm((*p, "f1"), TOK, 2, lambda k: x_step(before, "down", k), shift(0))
                ffn2_((*p, "f1"), TOK, FFN_MODS[2] if l == 0 else None)
                norm((*p, "mix"), TOK, 2, lambda k: x_step((*p, "f1"), "down", k), shift(3))
                if l % 2 == 0:
                    for g in range(4):
                        copy_pair(a_in[:, g, :], (p, "a", g))
                    for g in range(4):
                        act.wait_ge(tensor_done, T.at((p, "u", g)))
                        nc.scalar.activation(pair_of(qt, g), bank((p, "u", g)), ACT.Gelu_apprx_tanh)\
                          .then_inc(scalar_done, A.mark(("read", (p, "u", g))))
                    mod_rows(*MIXER_MODS[2][0])
                    for b in range(4):
                        act.wait_ge(tensor_done, T.at((p, "v", b)))
                        nc.scalar.activation(vt_of(kt)[:, b, :], bank((p, "v", b)), ACT.Gelu_apprx_tanh)\
                          .then_inc(scalar_done, A.mark(("read", (p, "v", b))))
                    for guest in MIXER_MODS[2][1:]:
                        mod_rows(*guest)
                    for b in range(4):
                        for q in range(2):
                            copy_pair(spec[:, b, 2 * q:2 * q + 2, :].rearrange("p a f -> p (a f)"), (p, "sp", b, q))
                    act.wait_ge(vector_done, V.at((p, "vss")))
                    nc.scalar.activation(rs[:, 0:16], rs[:, 0:16], ACT.Sqrt, bias=col("eps"), scale=1.0 / P)\
                      .then_inc(scalar_done, A.mark((p, "vrt")))
                    for g in range(4):
                        copy_pair(mixed[:, g, :], (p, "f", g))
                else:
                    squares((p, "q"), 4, qt, lambda c: (p, "q", c))
                    for c in range(2):
                        copy_pair(pair_of(kt, c), (p, "k", c))
                    for b in range(4):
                        act.wait_ge(tensor_done, T.at((p, "v", b)))
                        nc.scalar.activation(v2_of(va)[:, b, :], bank((p, "v", b))[:, 0:256], ACT.Copy)\
                          .then_inc(scalar_done, A.mark(("read", (p, "v", b))))
                    roots((p, "q"), 4)
                    squares((p, "k"), 2, kt)
                    roots((p, "k"), 2)
                    attention((p, "at"), 16, 1, lambda t: 128 ** -0.5, lambda c: attn[:, c, :])
                T_ = TOK if l == 0 else SEQ
                norm((*p, "f2"), T_, T_ // SEQ, lambda k: x_step(p, "out", k), shift(6))
                ffn2_((*p, "f2"), T_)
            norm("fin", SEQ, 1, lambda k: x_step(("b2", 1, "f2"), "down", k), None)

        @block.vector
        def _(dve):
            def own(i=None):
                if V.n:
                    dve.wait_ge(vector_done, V.so_far(i))

            def step(ins, name=None, i=None):
                ins.then_inc(vector_done, V.mark(name))
                own(i)

            def mod_cols(name, g, i=None):
                nv = NVEC[int(name[3]) - 1]
                l = int(name[5])
                b0 = vcol[f"b_{name}"][0]
                dve.wait_ge(tensor_done, T.at(((name, g), "cols"), i))
                if i is None:
                    at = g * KD * nv
                    out, bias = mods_sb[:, l, at:at + KD * nv], cols[:, b0 + at:b0 + at + KD * nv]
                else:
                    at = i * (KD * nv)
                    out, bias = mods_sb[:, l, bass.ds(at, KD * nv)], cols[:, bass.ds(at + b0, KD * nv)]
                src = ps[:, COLS_BANK, 0:KD * nv].rearrange("p (q r v) -> p r q v", q=4, r=2)
                step(nc.vector.tensor_tensor(out.rearrange("p (r q v) -> p r q v", q=4, r=2), src,
                                             bias.rearrange("p (r q v) -> p r q v", q=4, r=2), ALU.add),
                     ("read", ((name, g), "cols")), i)

            pending = []

            def hook(*group):
                if pending:
                    mod_cols(*pending.pop())
                if group:
                    pending.append(group)

            def adapt(l, slot, scale_at, gains, v, nv):
                sc = mods_sb[:, l, scale_at * KD * nv:(scale_at + 1) * KD * nv].rearrange("p (k v) -> p k v", v=nv)
                step(nc.vector.scalar_tensor_tensor(out=amod[:, slot, :, v], in0=sc[:, :, v], scalar=1.0, in1=gains,
                                                    op0=ALU.add, op1=ALU.mult))

            def norm(p, T_, slot, gain=None):
                dve.wait_ge(scalar_done, A.at(("read", (p, "ms"))))
                step(nc.vector.reciprocal(rs[:, 0:T_], rs[:, 0:T_]))
                for k in range(KD):
                    for v in range(T_ // SEQ):
                        t = slice(v * SEQ, (v + 1) * SEQ)
                        g = gain(k) if gain else amod[:, slot, k, v:v + 1]
                        last = v == T_ // SEQ - 1
                        name = ("final" if k == KD - 1 else None) if gain else ((p, "hn", k) if last else None)
                        nc.vector.scalar_tensor_tensor(out=h[:, k, t], in0=x[:, k, t], scalar=g, in1=rs[:, t],
                                                       op0=ALU.mult, op1=ALU.mult)\
                          .then_inc(vector_done, V.mark(name))

            def update(p, what, T_, gate):
                for m in range(KD):
                    dve.wait_ge(tensor_done, T.at((p, what, m)))
                    for v in range(T_ // SEQ):
                        t = slice(v * SEQ, (v + 1) * SEQ)
                        last = v == T_ // SEQ - 1
                        nc.vector.scalar_tensor_tensor(out=x[:, m, t], in0=bank((p, what, m))[:, t],
                                                       scalar=gate(m, v), in1=x[:, m, t],
                                                       op0=ALU.mult, op1=ALU.add)\
                          .then_inc(vector_done, V.mark(("read", (p, what, m)) if last else None))

            def head_norm(p, pairs, tile, gain, cos, sin):
                for c in range(pairs + 1):
                    if c < pairs:
                        b = hrs[:, c % 2, :]
                        dve.wait_ge(scalar_done, A.at(("read", (p, "hms", c))))
                        step(nc.vector.reciprocal(b, b))
                        step(nc.vector.scalar_tensor_tensor(out=pair_of(tile, c), in0=pair_of(tile, c),
                                                            scalar=gain(c), in1=b, op0=ALU.mult, op1=ALU.mult),
                             (p, "hn", c))
                    if c >= 1:
                        e = c - 1
                        dve.wait_ge(tensor_done, T.at((p, "rot", e)))
                        a, b2 = rt[:, 0, :], rt[:, 1, :]
                        tp = pair_of(tile, e)
                        shaped = two if cos(e).shape[1] == SEQ else (lambda q: q)
                        wide = (lambda q: q.rearrange("p (a t) -> p a t", a=1).to_broadcast([P, 2, SEQ])) \
                            if cos(e).shape[1] == SEQ else (lambda q: q)
                        step(nc.vector.tensor_tensor(shaped(b2), shaped(bank((p, "rot", e))), wide(sin(e)), ALU.mult),
                             ("read", (p, "rot", e)))
                        step(nc.vector.tensor_tensor(shaped(a), shaped(tp), wide(cos(e)), ALU.mult))
                        step(nc.vector.tensor_tensor(tp, a, b2, ALU.add), (p, "roped", e))

            def attention(p, tasks, J, scale, masked, between=None):
                W = 512 // J

                def first(t):
                    dve.wait_ge(tensor_done, T.at((p, "s", t)))
                    if t >= 2:
                        dve.wait_ge(tensor_done, T.at((p, "pt", t - 2)))
                    pr = probs[:, t % 2, :]
                    if masked:
                        step(nc.vector.tensor_tensor(pr, bank((p, "s", t)), mat("mask"), ALU.add), ("read", (p, "s", t)))
                    else:
                        step(nc.vector.tensor_copy(pr, bank((p, "s", t))), ("read", (p, "s", t)))
                    st = stat[:, t % 2, :]
                    step(nc.vector.tensor_reduce(st[:, 4:4 + J], pr.rearrange("p (j w) -> p j w", w=W), AX.X, ALU.max))
                    step(nc.vector.tensor_scalar(st[:, 0:J], st[:, 4:4 + J], -scale(t), None, ALU.mult), (p, "nm", t))

                def second(t):
                    dve.wait_ge(scalar_done, A.at((p, "e", t)))
                    st = stat[:, t % 2, :]
                    step(nc.vector.reciprocal(st[:, 6:6 + J], st[:, 2:2 + J]))
                    for b in range(J):
                        o = probs[:, t % 2, b * W:(b + 1) * W]
                        step(nc.vector.tensor_scalar(o, o, st[:, 6 + b:7 + b], None, ALU.mult),
                             (p, "p", t) if b == J - 1 else None)

                for t in range(tasks + 1):
                    if t < tasks:
                        first(t)
                        if between is not None:
                            between(t)
                    if t >= 1:
                        second(t - 1)

            def ffn1(p, l, guest):
                w0, b0 = vcol[f"ffn_w_{l}"][0], vcol[f"ffn_b_{l}"][0]

                def c(at, j, i):
                    if i is None:
                        return cols[:, at + j:at + j + 1]
                    return cols[:, bass.ds(i * RING + (at + j), 1)]

                def pair(j, i=None):
                    s = j % 2
                    dve.wait_ge(scalar_done, A.at((p, "z", j), i))
                    for ab in range(2):
                        def w(tap):
                            return c(w0 + (tap * 2 + ab) * FJ, j, i)
                        nc.vector.tensor_scalar(zc[:, s, ab, :], z[:, s, ab, 2:2 + SEQ], w(2), c(b0 + ab * FJ, j, i),
                                                ALU.mult, ALU.add).then_inc(vector_done, V.mark())
                    own(i)
                    for tap in (1, 0):
                        for ab in range(2):
                            nc.vector.scalar_tensor_tensor(out=zc[:, s, ab, :], in0=z[:, s, ab, tap:tap + SEQ],
                                                           scalar=c(w0 + (tap * 2 + ab) * FJ, j, i),
                                                           in1=zc[:, s, ab, :], op0=ALU.mult, op1=ALU.add)\
                              .then_inc(vector_done, V.mark((p, "cv", j) if (tap, ab) == (0, 1) else None))
                        own(i)

                def join(j, i=None):
                    out = hid[:, j, 0:SEQ] if i is None else \
                        hid[:, bass.ds(i * RING + j, 1), 0:SEQ].rearrange("p a t -> p (a t)")
                    dve.wait_ge(scalar_done, A.at((p, "si", j), i))
                    step(nc.vector.tensor_tensor(out, zc[:, j % 2, 0, :], zc[:, j % 2, 1, :], ALU.mult),
                         (p, "hid", j), i)

                with V.turns(dve, (p, "up"), GU_TURNS) as i:
                    for j in range(RING):
                        pair(j, i)
                        join(j, i)
                        if j == 2:
                            mod_cols(guest, 0, i)
                for j in range(GU_TURNS * RING, FJ):
                    pair(j)
                    join(j)

            def ffn2_(p, T_, guest=None):
                def join(j, i=None):
                    out = hid[:, j, 0:T_] if i is None else \
                        hid[:, bass.ds(i * RING + j, 1), 0:T_].rearrange("p a t -> p (a t)")
                    g = (p, "up", j)
                    dve.wait_ge(tensor_done, T.at(g, i))
                    dve.wait_ge(scalar_done, A.at((p, "si", j), i))
                    up = bank(g)[:, SEQ:TOK] if T_ == SEQ else bank(g)
                    step(nc.vector.tensor_tensor(out, sg[:, j % 2, 0:T_], up, ALU.mult), (p, "hid", j), i)
                    V.found[("read", g)] = V.found[(p, "hid", j)]

                with V.turns(dve, (p, "up"), GU_TURNS) as i:
                    for j in range(RING):
                        join(j, i)
                        if guest and j == 2:
                            mod_cols(guest, 0, i)
                for j in range(GU_TURNS * RING, FJ):
                    join(j)

            dve.wait_ge(inputs_landed, N_IN)
            step(nc.vector.tensor_copy(rs[:, 0:SEQ], pos_i[:, :]))
            for n, (t, f, quarter) in enumerate(((cos_a, "inv_freq_a", 1), (sin_a, "inv_freq_a", 0),
                                                 (cos_b, "inv_freq_b", 1), (sin_b, "inv_freq_b", 0))):
                ang, k = rt[:, 0, 0:SEQ], rt[:, 1, 0:SEQ]
                step(nc.vector.tensor_scalar(ang, rs[:, 0:SEQ], col(f), None, ALU.mult))
                step(nc.vector.tensor_scalar(k, ang, 1.0 / (2.0 * np.pi), 0.25 * quarter, ALU.mult, ALU.add))
                step(nc.vector.tensor_scalar(k, k, 12582912.0, None, ALU.add))
                step(nc.vector.tensor_scalar(k, k, 12582912.0, None, ALU.subtract))
                for part_ in TWO_PI:
                    step(nc.vector.scalar_tensor_tensor(out=ang, in0=k, scalar=-part_, in1=ang,
                                                        op0=ALU.mult, op1=ALU.add))
                if quarter:
                    step(nc.vector.tensor_scalar(ang, ang, np.pi / 2, None, ALU.add))
                step(nc.vector.tensor_scalar(t[:, :], ang, 3.1415925, -3.1415925, ALU.min, ALU.max), ("angle", n))
            step(nc.vector.memset(z[:, :, :, :], 0.0))
            step(nc.vector.memset(kt[96:128, :, :], 0.0), "kt zero")
            hook("mod1_0", 0)
            hook("mod1_0", 1)
            hook()
            for l in range(DEPTH):
                p = ("b1", l)
                guests = MIXER_MODS[l]
                adapt(l, 0, 1, col(f"g_mix1_{l}", 0, KD), 0, 1)
                norm((*p, "mix"), SEQ, 0)
                dve.wait_ge(scalar_done, A.at(("read", (p, "latms"))))
                step(nc.vector.reciprocal(rs[:, :], rs[:, :]))
                for k in range(5):
                    g = col(f"g_qlat_{l}", k) if k < 3 else col(f"g_kvlat_{l}", k - 3)
                    r = rs[:, 0:SEQ] if k < 3 else rs[:, SEQ:TOK]
                    step(nc.vector.scalar_tensor_tensor(out=lat[:, k, :], in0=lat[:, k, :], scalar=g, in1=r,
                                                        op0=ALU.mult, op1=ALU.mult), (p, "latn", k))
                hook(*guests[0])
                if l == 0:
                    dve.wait_ge(scalar_done, A.at(("table", 3)))
                hook(*guests[1])
                head_norm((p, "qa"), 4, qt, lambda c: col(f"g_qa_{l}"), lambda e: cos_a[:, :], lambda e: sin_a[:, :])
                head_norm((p, "ka"), 4, kt, lambda c: col(f"g_ka_{l}"), lambda e: cos_a[:, :], lambda e: sin_a[:, :])
                hook(*guests[2])
                head_norm((p, "qkb"), 4, bt, lambda c: col(f"g_qb_{l}" if c < 2 else f"g_kb_{l}"),
                          lambda e: cos_b[:, :], lambda e: sin_b[:, :])
                step(nc.vector.memset(u_pad[:, :, 0:TAPS - 1], 0.0))
                for c in range(CC):
                    dve.wait_ge(scalar_done, A.at((p, "glu", c)))
                    step(nc.vector.tensor_tensor(u_pad[:, c, TAPS - 1:], bank((p, "conv", c))[:, 0:SEQ],
                                                 sg2[:, c % 2, :], ALU.mult), ("read", (p, "conv", c)))

                def taps(t):
                    for tap in range(2 * t, min(2 * t + 2, TAPS)):
                        for c in range(CC):
                            w = col(f"conv_w_{l}", tap * CC + c)
                            name = (p, "dwc") if tap == TAPS - 1 and c == CC - 1 else None
                            if tap == 0:
                                nc.vector.tensor_scalar(dwc[:, c, :], u_pad[:, c, 0:SEQ], w, col(f"conv_b_{l}", c),
                                                        ALU.mult, ALU.add).then_inc(vector_done, V.mark(name))
                            else:
                                nc.vector.scalar_tensor_tensor(out=dwc[:, c, :], in0=u_pad[:, c, tap:tap + SEQ],
                                                               scalar=w, in1=dwc[:, c, :], op0=ALU.mult, op1=ALU.add)\
                                  .then_inc(vector_done, V.mark(name))
                        own()

                for guest in guests[3:]:
                    hook(*guest)
                attention((p, "at"), 16, 2, lambda t: (NOPE + ROPE_A) ** -0.5 if t < HEADS else 64 ** -0.5, True, taps)
                dve.wait_ge(tensor_done, T.at((p, "lnm")))

                def spread(a):
                    return a.rearrange("p (a t) -> p a t", a=1).to_broadcast([P, CC, SEQ])

                step(nc.vector.tensor_tensor(dwc[:, :, :], dwc[:, :, :], spread(bank((p, "lnm"))[:, 0:SEQ]),
                                             ALU.subtract), (p, "cen"))
                V.found[("read", (p, "lnm"))] = V.found[(p, "cen")]
                dve.wait_ge(scalar_done, A.at(("read", (p, "lnv"))))
                step(nc.vector.reciprocal(rs[:, 0:SEQ], rs[:, 0:SEQ]))
                step(nc.vector.tensor_tensor(dwc[:, :, :], dwc[:, :, :], spread(rs[:, 0:SEQ]), ALU.mult), (p, "lnn"))
                hook()
                for m in range(KD):
                    a, b = rt[:, 0, :], rt[:, 1, 0:SEQ]
                    dve.wait_ge(tensor_done, T.at((p, "g2c", m)))
                    dve.wait_ge(scalar_done, A.at((p, "sg2", m)))
                    step(nc.vector.scalar_tensor_tensor(out=b, in0=bank((p, "g2c", m))[:, SEQ:TOK],
                                                        scalar=col(f"pw2_b_{l}", m), in1=sg2[:, m % 2, :],
                                                        op0=ALU.add, op1=ALU.mult), ("read", (p, "g2c", m)))
                    dve.wait_ge(tensor_done, T.at((p, "oab", m)))
                    step(nc.vector.tensor_tensor(a, bank((p, "oab", m)), sg[:, m % 2, :], ALU.mult),
                         ("read", (p, "oab", m)))
                    step(nc.vector.tensor_tensor(b, b, a[:, 0:SEQ], ALU.add))
                    step(nc.vector.tensor_tensor(merged[:, m, :], b, a[:, SEQ:TOK], ALU.add), (p, "merged", m))
                update(p, "out", SEQ, lambda m, v: mods_sb[:, l, 2 * KD + m:2 * KD + m + 1])
                adapt(l, 1, 4, col(f"g_ffn1_{l}", 0, KD), 0, 1)
                norm((*p, "ffn"), SEQ, 1)
                ffn1((*p, "ffn"), l, FFN_MODS[l])
                update((*p, "ffn"), "down", SEQ, lambda m, v: mods_sb[:, l, 5 * KD + m:5 * KD + m + 1])
                own()
            for l in range(DEPTH):
                p = ("b2", l)
                for n in range(3):
                    for v in range(2):
                        adapt(l, n, 3 * n + 1, col(f"g2_{l}", n * KD, KD), v, 2)
                for n in (2, 8):
                    g = mods_sb[:, l, n * KD * 2:(n + 1) * KD * 2]
                    step(nc.vector.tensor_scalar(g, g, 0.5, None, ALU.mult))

                def gate(n):
                    return lambda m, v: mods_sb[:, l, (n * KD + m) * 2 + v:(n * KD + m) * 2 + v + 1]

                norm((*p, "f1"), TOK, 0)
                ffn2_((*p, "f1"), TOK, FFN_MODS[2] if l == 0 else None)
                update((*p, "f1"), "down", TOK, gate(2))
                norm((*p, "mix"), TOK, 1)
                if l % 2 == 0:
                    vt = vt_of(kt)
                    hook(*MIXER_MODS[2][0])
                    for guest in MIXER_MODS[2][1:]:
                        hook(*guest)
                    hook()
                    for b in range(4):
                        dve.wait_ge(scalar_done, A.at(("read", (p, "v", b))))
                        step(nc.vector.tensor_tensor(vt_of(sq)[:, b, :], vt[:, b, :], vt[:, b, :], ALU.mult))
                        step(nc.vector.tensor_reduce(rs[:, 4 * b:4 * b + 4],
                                                     vt_of(sq)[:, b, :].rearrange("p (g d) -> p g d", g=4),
                                                     AX.X, ALU.add), (p, "vss") if b == 3 else None)
                    dve.wait_ge(scalar_done, A.at((p, "vrt")))
                    step(nc.vector.reciprocal(rs[:, 0:16], rs[:, 0:16]))
                    for b in range(4):
                        for g in range(4):
                            o = vt[:, b, g * P:(g + 1) * P]
                            step(nc.vector.scalar_tensor_tensor(out=o, in0=o, scalar=rs[:, 4 * b + g:4 * b + g + 1],
                                                                in1=mat("g_v")[:, g * P:(g + 1) * P],
                                                                op0=ALU.mult, op1=ALU.mult),
                                 (p, "vn") if b == g == 3 else None)
                    for g in range(4):
                        dve.wait_ge(tensor_done, T.at((p, "mx", g)))
                        bs = mat("b_s")[:, g * P:(g + 1) * P].rearrange("p (a t) -> p a t", a=1)\
                            .to_broadcast([P, 4, P])
                        o = rt[:, 0, :]
                        step(nc.vector.tensor_tensor(o.rearrange("p (a t) -> p a t", a=4),
                                                     bank((p, "mx", g)).rearrange("p (a t) -> p a t", a=4),
                                                     bs, ALU.add), ("read", (p, "mx", g)))
                        step(nc.vector.tensor_tensor(mixed[:, 4 + g, :], o, pair_of(qt, g), ALU.mult), (p, "sgu", g))
                else:
                    head_norm((p, "q"), 4, qt, lambda c: col("gq2"), lambda e: mat("cos_c")[:, 0:SEQ],
                              lambda e: mat("sin_c")[:, 0:SEQ])
                    head_norm((p, "k"), 2, kt, lambda c: col("gk2"), lambda e: mat("cos_c"), lambda e: mat("sin_c"))
                    attention((p, "at"), 16, 1, lambda t: 128 ** -0.5, False)
                update(p, "out", TOK if l == 0 else SEQ, gate(5))
                T_ = TOK if l == 0 else SEQ
                norm((*p, "f2"), T_, 2)
                ffn2_((*p, "f2"), T_)
                update((*p, "f2"), "down", T_, gate(8))
                own()
            norm("fin", SEQ, None, lambda k: col("g_final", k))

    return {"T": T.found, "A": A.found, "V": V.found}, new_banks


def two(a):
    return a.rearrange("p (a t) -> p a t", a=2)


def pair_of(tile, c):
    return tile[:, 2 * c:2 * c + 2, :].rearrange("p a t -> p (a t)")


def vt_of(tile):
    return tile[:, :, :].rearrange("p (b e) t -> p b (e t)", b=4)


def v2_of(tile):
    return tile[:, :, :].rearrange("p e (b t) -> p (e b) t", b=2)


def transposed_order(p):
    return (0, 2, 1, 3) if p[0][0] == "b1" else (0, 1, 2, 3)


def out_step(p, s):
    return (p, "o", s // 2) if s % 2 else (p, "ov", s)


def x_step(p, what, k):
    return ("read", (p, what, k))


def hid_step(p, k):
    if k < GU_TURNS * RING:
        return (p, "hid", k % RING), k // RING
    return (p, "hid", k), None


def conv_before(V, p, j, i):
    if i is None:
        return V.at(*hid_step(p, j - 2))
    if j >= 2:
        return V.at((p, "hid", j - 2), i)
    return V.at((p, "hid", j + RING - 2), i - 1)


def ffn2(p, l, T_, ready, ffn):
    ffn((*p, "f2"), f"f2up_{l}", f"f2down_{l}", T_, ready)


def loop_starts(blocks):
    out, seen = [], set()
    guests = {"up_0", "up_1", "f1up_0"}
    for b, q in enumerate(blocks):
        if q is None or q[0] in seen:
            continue
        seen.add(q[0])
        if q[0].startswith(("up_", "f1up_", "f2up_")):
            out.append((b, q[0], GU_TURNS, 2 * RING if q[0] in guests else RING))
    return out


def _columns(a):
    return np.asarray(a).reshape(-1, P).T


def _constants():
    m = {}
    m["ones_d"] = np.full((P, P), 1.0 / D)
    m["ones_q"] = np.full((P, P), 1.0 / Q_RANK)
    m["ones_kv"] = np.full((P, P), 1.0 / KV_RANK)
    m["ones_c"] = np.full((P, P), 1.0 / CONV_CH)
    m["head_c"] = np.full((P, P), 1.0 / P)
    a = np.zeros((P, P))
    a[0:64, 0:64] = 1.0 / 64
    a[64:96, 64:96] = 1.0 / 32
    m["head_a"] = a
    b = np.zeros((P, P))
    b[0:64, 0:64] = b[64:128, 64:128] = 1.0 / 64
    m["head_b"] = b

    def rot(starts, half):
        r = np.zeros((P, P))
        for s in starts:
            for i in range(half):
                r[s + half + i, s + i] = -1.0
                r[s + i, s + half + i] = 1.0
        return r

    m["rot_a"] = rot((64,), 16)
    m["rot_b"] = rot((0, 64), 32)
    m["rot_c"] = rot((0, 64), 32)
    m["ident"] = np.eye(P)

    def dft(n):
        a = 2 * np.pi * (np.outer(np.arange(n), np.arange(n)) % n) / n
        return np.cos(a) / np.sqrt(n), np.sin(a) / np.sqrt(n)

    c, s = dft(P)
    m["dft_c"] = np.concatenate([c, s], 1)
    c, s = dft(SEQ)
    m["cos_n"] = np.concatenate([c[0:P], c[P:]], 1)
    m["nsin_n"] = -np.concatenate([s[0:P], s[P:]], 1)
    inv = THETA ** (-np.arange(0, 64, 2, dtype=np.float32) / np.float32(64))
    row = np.repeat(np.arange(SEQ // GRID_W), GRID_W).astype(np.float32)
    colm = np.tile(np.arange(GRID_W), SEQ // GRID_W).astype(np.float32)
    ang = np.concatenate([np.tile((row[:, None] * inv).T, (2, 1)), np.tile((colm[:, None] * inv).T, (2, 1))], 0)
    m["cos_c"] = np.concatenate([np.cos(ang), np.ones((P, SEQ))], 1)
    m["sin_c"] = np.concatenate([np.sin(ang), np.zeros((P, SEQ))], 1)
    mask = np.zeros((P, 2, SEQ))
    for q in range(2):
        mask[:, q, :] = np.where(np.arange(SEQ)[None] <= (q * P + np.arange(P))[:, None], 0.0, MASKED)
    m["mask"] = mask.reshape(P, 2 * SEQ)
    pick1, pick2 = np.zeros((P, 2)), np.zeros((P, 4))
    for k in range(2):
        for r in range(2):
            t = 32 * (2 * k + r)
            pick1[t, r] = 1.0
            pick2[t + 1, 2 * r] = pick2[t + 2, 2 * r + 1] = 1.0
    m["pick1"], m["pick2"] = pick1, pick2
    return {k: v.astype(np.float32) for k, v in m.items()}


def _pack(w):
    f = np.float32
    mats = {}
    o = np.cumsum([0, Q_RANK, KV_RANK, ROPE_A, 512, 512, 512, 512, 512, D, D, D])
    for l in range(DEPTH):
        mats[f"mod1_{l}"] = w["w_mod"][l]
        mats[f"mod2_{l}"] = w["w_mod_2"][l]
        wi = w["w_in"][l]
        rope = np.zeros((D, P), f)
        rope[:, 64:96] = wi[:, o[2]:o[3]]
        mats[f"lat_{l}"] = np.concatenate([wi[:, o[0]:o[2]], rope], 1)
        uq = np.zeros((Q_RANK, HEADS, P), f)
        uq[:, :, 0:96] = w["w_uq"][l].reshape(Q_RANK, HEADS, 96)
        mats[f"uq_{l}"] = uq.reshape(Q_RANK, HEADS * P)
        kv = w["w_ukv"][l].reshape(KV_RANK, HEADS, P)
        uk = np.zeros((KV_RANK, HEADS, P), f)
        uk[:, :, 0:64] = kv[:, :, 0:64]
        mats[f"uk_{l}"] = uk.reshape(KV_RANK, HEADS * P)
        mats[f"uv_{l}"] = kv[:, :, 64:128].reshape(KV_RANK, 512)
        mats[f"qkb_{l}"] = wi[:, o[3]:o[5]]
        mats[f"vb_{l}"] = wi[:, o[5]:o[6]]
        mats[f"conv_{l}"] = wi[:, o[6]:o[8]].reshape(D, 2, CC, P).transpose(0, 2, 1, 3).reshape(D, D)
        for n in range(3):
            mats[f"gate{n}_{l}"] = wi[:, o[8 + n]:o[9 + n]]
        mats[f"pw2_{l}"] = w["w_conv_pw2"][l]
        mats[f"oa_{l}"] = w["w_mla_o"][l]
        mats[f"ob_{l}"] = w["w_moba_o"][l]
        mats[f"out_{l}"] = w["w_out"][l]
        mats[f"up_{l}"] = w["w_up"][l].reshape(D, 2, FJ, P).transpose(0, 2, 1, 3).reshape(D, 2 * D_FF)
        mats[f"down_{l}"] = w["w_down"][l]
        for n in (1, 2):
            gu = np.zeros((D, 2, D_FF), f)
            gu[:, :, 0:D_FF_2] = w[f"w_ffn{n}_gu_2"][l].reshape(D, 2, D_FF_2)
            mats[f"f{n}up_{l}"] = gu.reshape(D, 2, FJ, P).transpose(0, 2, 1, 3).reshape(D, 2 * D_FF)
            dn = np.zeros((D_FF, D), f)
            dn[0:D_FF_2] = w[f"w_ffn{n}_down_2"][l]
            mats[f"f{n}down_{l}"] = dn
    wab = w["w_in_ab_2"][0]
    mats["ain"], mats["uin"], mats["vin"] = wab[:, 0:512], wab[:, 512:1024], wab[:, 1024:1536]
    mats["oab"] = w["w_out_ab_2"][0]
    qkv = w["w_qkv_2"][0]
    mats["q2"], mats["k2"], mats["v2"] = qkv[:, 0:1024], qkv[:, 1024:1280], qkv[:, 1280:1536]
    mats["o2"] = w["w_o_2"][0]

    blocks = weight_blocks()
    stream = np.zeros((len(blocks) // UB, P, UB, P), f)
    for b, q in enumerate(blocks):
        if q is not None:
            name, k, n = q
            stream[b // UB, :, b % UB, :] = mats[name][k * P:(k + 1) * P, n * P:(n + 1) * P]

    vcol, vcols = vector_columns()
    cols = np.zeros((P, vcols), f)

    def put(name, a):
        s, n = vcol[name]
        cols[:, s:s + n] = a

    inv_a = (1.0 / (THETA ** (np.arange(0, 32, 2, dtype=f) / f(32)))).astype(f)
    inv_b = (1.0 / (THETA ** (np.arange(0, 64, 2, dtype=f) / f(64)))).astype(f)
    a = np.zeros((P, 1), f)
    a[64:96, 0] = np.tile(inv_a, 2)
    put("inv_freq_a", a)
    put("inv_freq_b", np.tile(inv_b, 4)[:, None])
    c = np.zeros((P, KD, 32), f)
    for n, a in enumerate((w["c"][0], w["c_2"][0], w["c_ctx_2"])):
        c[:, :, n] = _columns(a)
    put("c", c.reshape(P, KD * 32))
    put("eps", f(EPS))
    put("g_final", _columns(w["g_final_2"]))
    put("gq2", w["g_q_2"][0][:, None])
    put("gk2", w["g_k_2"][0][:, None])
    for l in range(DEPTH):
        put(f"b_mod1_{l}", _columns(w["b_mod"][l]))
        put(f"b_mod2_{l}", np.repeat(_columns(w["b_mod_2"][l]), 2, axis=1))
        put(f"g_mix1_{l}", _columns(w["mix_norm_g"][l]))
        put(f"g_ffn1_{l}", _columns(w["ffn_norm_g"][l]))
        put(f"g_qlat_{l}", _columns(w["mla_q_norm_g"][l]))
        put(f"g_kvlat_{l}", _columns(w["mla_kv_norm_g"][l]))
        for n, (a, b) in (("qa", ("mla_qn_nope_g", "mla_qn_rope_g")), ("ka", ("mla_kn_nope_g", "mla_kn_rope_g"))):
            g = np.zeros((P, 1), f)
            g[0:64, 0], g[64:96, 0] = w[a][l], w[b][l]
            put(f"g_{n}_{l}", g)
        put(f"g_qb_{l}", np.tile(w["moba_qn_g"][l], 2)[:, None])
        put(f"g_kb_{l}", np.tile(w["moba_kn_g"][l], 2)[:, None])
        put(f"conv_w_{l}", _columns(w["conv_dw_w"][l].reshape(-1)))
        put(f"conv_b_{l}", _columns(w["conv_dw_b"][l]))
        put(f"ln_g_{l}", _columns(w["conv_ln_g"][l]))
        put(f"ln_b_{l}", _columns(w["conv_ln_b"][l]))
        put(f"pw2_b_{l}", _columns(w["b_conv_pw2"][l]))
        put(f"ffn_w_{l}", _columns(w["ffn_dw_w"][l].reshape(-1)))
        put(f"ffn_b_{l}", _columns(w["ffn_dw_b"][l]))
        put(f"g2_{l}", np.concatenate([_columns(w[n][l]) for n in ("g_ffn1_2", "g_mix_2", "g_ffn2_2")], 1))

    ccol, ccols = const_columns()
    consts = np.zeros((P, ccols), f)
    made = _constants()
    for g in range(4):
        made[f"ws{g}"] = w["w_s_2"][0, g].T
    made["g_v"] = np.broadcast_to(w["g_v_2"][0].reshape(1, 512), (P, 512))
    made["b_s"] = np.broadcast_to(w["b_s_2"][0].reshape(1, 512), (P, 512))
    for name, (s, n) in ccol.items():
        consts[:, s:s + n] = made[name]
    return stream.reshape(-1, P, UB * P), cols, consts


def kernel(**inputs):
    import concourse.bacc as bacc
    from concourse.bass_utils import run_bass_kernel_spmd

    w = {k: np.asarray(v) for k, v in inputs.items()}
    stream, cols, consts = _pack(w)
    arrays = {
        "stream": stream, "columns": cols, "constants": consts,
        "x_in": np.ascontiguousarray(w["x"][0].T.reshape(KD, P, SEQ).transpose(1, 0, 2)),
        "ctx_in": np.ascontiguousarray(w["ctx_2"][0].T.reshape(KD, P, SEQ).transpose(1, 0, 2)),
        "positions_in": np.ascontiguousarray(np.broadcast_to(w["positions"].astype(np.int32), (P, SEQ))),
    }

    def program(known, banks):
        nc = bacc.Bacc("TRN2", target_bir_lowering=False, num_devices=1)
        args = [nc.dram_tensor(k, a.shape, mybir.dt.from_np(a.dtype), kind="ExternalInput").ap()
                for k, a in arrays.items()]
        out = nc.dram_tensor("out", (P, KD, SEQ), F32, kind="ExternalOutput").ap()
        return nc, build(nc, *args, out, known, banks)

    _, (known, banks) = program({}, {})
    nc, _ = program(known, banks)
    r = run_bass_kernel_spmd(nc, [arrays], core_ids=[0])
    y = r.results[0]["out"]
    return y.transpose(2, 1, 0).reshape(1, SEQ, D)
```

```python
from contextlib import ExitStack, contextmanager

import numpy as np
import concourse.bass as bass
from concourse import mybir

P = 128
D = 1024
KD = D // P
SEQ = 256
TOK = 2 * SEQ
DEPTH = 2
D_FF, D_FF_2 = 2816, 2752
FJ = D_FF // P
Q_RANK, KV_RANK, ROPE_A, NOPE = 384, 256, 32, 64
HEADS = 8
CONV_CH, TAPS, FFN_TAPS = 512, 31, 3
CC = CONV_CH // P
NMOD = (6, 9)
NVEC = (1, 2)
GRID_W = 64
THETA = 10000.0
EPS = 1e-6
UB = 8
RING = 8
HEADS_RING = 4
PAIRS = 4
PAIR_UNITS = 2 * KD // UB
TURN_SPLITS = PAIRS * PAIR_UNITS
BANKS = 6
ROWS_BANK, COLS_BANK = 6, 7
F32 = mybir.dt.float32
F32R = mybir.dt.float32r
I32 = mybir.dt.int32
ALU = mybir.AluOpType
ACT = mybir.ActivationFunctionType
AX = mybir.AxisListType
TWO_PI = (6.28125, 0.0019350051879882812, 3.019916050561733e-07)
MASKED = -1e30


FFN_MODS = ("mod1_1", "mod2_0", "mod2_1")
MIXER_MODS = ([("mod1_0", g) for g in (2, 3, 4, 5)],
              [("mod1_1", 5)] + [("mod2_0", g) for g in (5, 6, 7, 8)],
              [("mod2_1", g) for g in (4, 5, 6, 7, 8)])
def is_split(name):
    return name is not None and not name.startswith(("mod", "uq", "uk", "uv", "pw2", "oa", "ob", "out", "o2"))


def hidden_ranges(width):
    return ((0, FJ),) if width == SEQ else ((0, FJ // 2), (FJ // 2, FJ))


def together(ks):
    return [(e, k) for k in ks for e in (0, 1)]


def late(ks, n=2):
    ks = list(ks)
    return [(e, k) for part_ in (ks[:-n], ks[-n:]) for e in (0, 1) for k in part_]


def up_order(width):
    return together(range(KD)) if width == TOK else late(range(KD), KD)


def weight_blocks():
    s, loops = [], []

    def align(m):
        while len(s) % m:
            s.append(None)

    def put(name, k, n):
        if s and s[-1] is not None and is_split(s[-1][0]) != is_split(name):
            align(UB)
        s.append((name, k, n))

    def linear(name, ks, ns):
        for n in ns:
            for k in range(ks) if isinstance(ks, int) else ks:
                put(name, k, n)

    def pair(name, order, n):
        for e, k in order:
            put(name, k, n + e)

    def wide(name, nk, nn):
        align(UB)
        for k in range(nk):
            for n in range(nn):
                put(name, k, n)

    def mods(*groups):
        align(UB)
        for name, g in groups:
            for k in range(KD):
                for n in range(KD):
                    put(name, k, g * KD + n)

    def ffn(up, down, width, guest=None):
        align(UB)
        for lo, hi in hidden_ranges(width):
            turns = (hi - lo) // PAIRS
            loops.append((len(s) // UB, up, turns, TURN_SPLITS + (KD if guest else 0)))
            for j in range(lo, hi):
                t, q = divmod(j - lo, PAIRS)
                pair(up, up_order(width), 2 * j)
                if guest is not None and t < turns and q in (1, 2):
                    for k in range(KD // 2):
                        for n in range(KD):
                            put(guest, (q - 1) * (KD // 2) + k, (guest_groups(lo) + t) * KD + n)
            pair(down, late(range(lo, hi)), 0)
            linear(down, range(lo, hi), range(2, KD))
            align(UB)

    mods(("mod1_0", 0), ("mod1_0", 1))
    for l in range(DEPTH):
        linear(f"lat_{l}", KD, range(6))
        mods(MIXER_MODS[l][0])
        linear(f"uq_{l}", Q_RANK // P, range(HEADS))
        linear(f"uk_{l}", KV_RANK // P, range(HEADS))
        wide(f"uv_{l}", KV_RANK // P, 4)
        mods(MIXER_MODS[l][1])
        linear(f"qkb_{l}", KD, range(HEADS))
        linear(f"conv_{l}", KD, range(2 * CC))
        wide(f"vb_{l}", KD, 4)
        mods(*MIXER_MODS[l][2:])
        for m in range(KD):
            linear(f"gate0_{l}", KD, (m,))
            linear(f"gate1_{l}", KD, (m,))
        for m in range(KD):
            linear(f"gate2_{l}", KD, (m,))
            linear(f"pw2_{l}", CC, (m,))
            linear(f"oa_{l}", 4, (m,))
            linear(f"ob_{l}", 4, (m,))
        pair(f"out_{l}", late(range(KD)), 0)
        linear(f"out_{l}", KD, range(2, KD))
        ffn(f"up_{l}", f"down_{l}", SEQ, FFN_MODS[l])
    for l in range(DEPTH):
        ffn(f"f1up_{l}", f"f1down_{l}", TOK, FFN_MODS[2] if l == 0 else None)
        if l % 2 == 0:
            pair("ain", together(range(KD)), 0)
            linear("ain", KD, range(2, 4))
            linear("uin", KD, range(4))
            mods(MIXER_MODS[2][0])
            wide("vin", KD, 4)
            mods(*MIXER_MODS[2][1:])
            pair("oab", late(range(KD)), 0)
            linear("oab", KD, range(2, KD))
        else:
            linear("q2", KD, range(8))
            linear("k2", KD, range(2))
            wide("v2", KD, 2)
            pair("o2", late(range(KD)), 0)
            linear("o2", KD, range(2, KD))
        ffn(f"f2up_{l}", f"f2down_{l}", TOK if l == 0 else SEQ)
    align(UB)
    return s, loops


def guest_groups(lo):
    return 0 if lo == 0 else lo // PAIRS


def vector_columns():
    at, n = {}, 0
    sizes = [("inv_freq_a", 1), ("inv_freq_b", 1), ("c", KD * 32), ("eps", 1), ("g_final", KD),
             ("gq2", 1), ("gk2", 1)]
    for l in range(DEPTH):
        sizes += [(f"b_mod1_{l}", NMOD[0] * KD), (f"g_mix1_{l}", KD), (f"g_ffn1_{l}", KD),
                  (f"g_qlat_{l}", 3), (f"g_kvlat_{l}", 2), (f"g_qa_{l}", 1), (f"g_ka_{l}", 1),
                  (f"g_qb_{l}", 1), (f"g_kb_{l}", 1), (f"conv_w_{l}", TAPS * CC), (f"conv_b_{l}", CC),
                  (f"ln_g_{l}", CC), (f"ln_b_{l}", CC), (f"pw2_b_{l}", KD),
                  (f"ffn_w_{l}", FFN_TAPS * 2 * FJ), (f"ffn_b_{l}", 2 * FJ),
                  (f"b_mod2_{l}", NMOD[1] * KD * 2), (f"g2_{l}", 3 * KD)]
    for name, size in sizes:
        at[name] = (n, size)
        n += size
    return at, n


CONST_MATS = ("ones", "head_a", "head_b", "rot_a", "rot_b", "ident", "ws0", "ws1", "ws2", "ws3")
TABLES = (("dft_c", 256), ("cos_n", 512), ("nsin_n", 512), ("cos_c", 512), ("sin_c", 512),
          ("mask", 512), ("g_v", 512), ("b_s", 512),
          ("pick1", 2), ("pick2", 4))


def const_columns():
    at, n = {}, 0
    for name in CONST_MATS:
        at[name] = (n, P)
        n += P
    for name, size in TABLES:
        at[name] = (n, size)
        n += size
    return at, n


class Steps:

    def __init__(self, known):
        self.known, self.found, self.n, self.loop = known, {}, 0, None
        self.guessed = []
        self.unit = 0

    def mark(self, name=None):
        self.n += 1
        if name is not None:
            assert name not in self.found, name
            self.found[name] = (self.n, self.loop, self.unit)
        return 1

    def unit_of(self, name):
        return self.known.get(name, (0, None, 0))[2]

    def at(self, name, turn=None):
        if name not in self.known:
            self.guessed.append(name)
        n, loop, _ = self.known.get(name, (1, None, 0))
        if loop is None:
            return n
        stride, count = self.known[("loop", loop)]
        return n + (count - 1 if turn is None else turn) * stride

    def has(self, name):
        return name in self.known

    def so_far(self, turn=None):
        if self.loop is None:
            return self.n
        return self.n + turn * self.known.get(("loop", self.loop), (1, 1))[0]

    @contextmanager
    def turns(self, engine, name, count):
        start = self.n
        self.loop = name
        with engine.Fori(0, count) as i:
            yield i
        self.loop = None
        stride = self.n - start
        self.found[("loop", name)] = (stride, count)
        self.n = start + stride * count


def build(nc, stream, cols_d, consts_d, x_d, ctx_d, pos_d, out_d, known, bank_of):
    blocks, loop_list = weight_blocks()
    vcol, vcols = vector_columns()
    ccol, ccols = const_columns()
    T, A, V = (Steps(known.get(e, {})) for e in "TAV")
    new_banks = {}

    ctx = ExitStack()
    with ctx:
        def sb(name, shape, dt=F32):
            return ctx.enter_context(nc.sbuf_tensor(name, shape, dt))

        def sem(name):
            return ctx.enter_context(nc.semaphore(name))

        def alias(name, shape, dt, of):
            return nc.alloc_sbuf_tensor_at(name, shape, dt, offset=places[of])

        places = {}

        def placed(name, shape, dt=F32):
            places[name] = -(-nc.sbuf_base // 32) * 32
            return sb(name, shape, dt)

        ring = placed("ring", [P, RING, UB * P])
        rests = alias("rests", [P, RING, UB * P], F32R, "ring")
        heads = sb("heads", [P, HEADS_RING, UB * P], F32R)
        x = sb("x_sb", [P, 2, KD, SEQ])
        hr = sb("h_split", [P, 2, KD, TOK], F32R)
        area = placed("area", [P, FJ * TOK])
        hidr = alias("hid_split", [P, FJ * TOK], F32R, "area")
        cols = sb("cols", [P, vcols])
        consts = sb("consts", [P, ccols])
        mods_sb = sb("mods_sb", [P, 2, NMOD[1] * KD * 2])
        rows = sb("rows", [P, 512])
        amod = sb("amod", [P, 3, KD, 2])
        rs = sb("rs", [P, TOK])
        qt = sb("qt", [P, HEADS, SEQ])
        kt = sb("kt", [P, HEADS, SEQ])
        sq = sb("sq", [P, HEADS, SEQ])
        rt = sb("rt", [P, 2, TOK])
        zc = rt[:, :, :].rearrange("p s (a t) -> p s a t", a=2)
        sg = sb("sg", [P, 2, TOK])
        sg2 = sb("sg2", [P, 2, SEQ])
        work = sb("work", [P, 2080])
        probs = work[:, 0:1024].rearrange("p (s t) -> p s t", s=2)
        probs_t = work[:, 1024:2048].rearrange("p (s t) -> p s t", s=2)
        z = work[:, 0:4 * (SEQ + FFN_TAPS - 1)].rearrange("p (s a t) -> p s a t", s=2, a=2)
        stat = sb("stat", [P, 2, 8])
        cos_a = sb("cos_a", [P, SEQ])
        sin_a = sb("sin_a", [P, SEQ])
        cos_b = sb("cos_b", [P, SEQ])
        sin_b = sb("sin_b", [P, SEQ])
        pos_i = sg2[:, 0, :].bitcast(I32)
        silu_c = cols[:, vcol["c"][0]:vcol["c"][0] + KD * 32].rearrange("p (k v) -> p k v", v=32)

        def part(start, n, **dims):
            names = " ".join(dims)
            return area[:, start:start + n].rearrange(f"p ({names}) -> p {names}", **dims)

        def squared(width, k):
            return sq[:, k, :] if width == SEQ else pair_of(sq if k < 4 else kt, k % 4)

        def hid(width, which, j):
            half = FJ * TOK // 2
            return hidr[:, which * half + j * width:which * half + (j + 1) * width]

        tmp = part(0, KD * TOK, k=KD, t=TOK)
        attn = part(0, 8 * SEQ, c=8, t=SEQ)
        u_pad = part(2048, CC * (SEQ + TAPS - 1), c=CC, t=SEQ + TAPS - 1)
        u_end = 2048 + CC * (SEQ + TAPS - 1)
        dwc = part(u_end, CC * SEQ, c=CC, t=SEQ)
        csq = part(u_end + 1024, CC * SEQ, c=CC, t=SEQ)
        oc = part(u_end + 2048, CC * SEQ, c=CC, t=SEQ)
        lat = part(u_end + 3072, 6 * SEQ, c=6, t=SEQ)
        va = part(u_end + 4608, 1024, b=2, t=512)
        vb = part(u_end + 5632, 1024, b=2, t=512)
        hrs = part(10240, 1024, b=2, t=TOK)
        gates = [part(u_end + 3072 + 512 * m, 512, t=512) for m in range(3)] + \
            [pair_of(sq, c) for c in range(4)] + [hrs[:, 0, :]]
        merged = qt
        bt = x[:, 1, :, :]
        mixed = part(0, KD * TOK, k=KD, t=TOK)
        spec = part(4096, 4 * 4 * 256, t=4, g=4, f=256)
        a_in = part(8192, 4 * TOK, g=4, t=TOK)

        ps = ctx.enter_context(nc.psum_tensor("ps", [P, 8, 512], F32))

        tensor_done = sem("tensor_done")
        scalar_done = sem("scalar_done")
        vector_done = sem("vector_done")
        inputs_landed = sem("inputs_landed")
        context_landed = sem("context_landed")
        weights_landed = [sem(f"weights_landed{s}") for s in range(RING)]
        output_stored = sem("output_stored")
        N_IN = 4 * 16

        def col(name, k=0, n=1):
            return cols[:, vcol[name][0] + k:vcol[name][0] + k + n]

        def mat(name):
            return consts[:, ccol[name][0]:ccol[name][0] + ccol[name][1]]

        def bank(g):
            return ps[:, bank_of.get(g, 0), :]

        def as_f32(a):
            return a.bitcast(F32)

        units = len(blocks) // UB
        split_units = [u for u in range(units) if any(q is not None and is_split(q[0]) for q in blocks[u * UB:(u + 1) * UB])]
        split_index = {u: n for n, u in enumerate(split_units)}
        loops = {u: (name, turns, width) for u, name, turns, width in loop_list}

        def unit_step(u):
            for u0, (name, turns, width) in loops.items():
                if u0 <= u < u0 + turns * width:
                    return ("unit", u0 + (u - u0) % width), (u - u0) // width
            return ("unit", u), None

        def rest_step(n):
            for u0, (name, turns, width) in loops.items():
                behind = n - split_index[u0] - turns * TURN_SPLITS
                if 0 <= behind < HEADS_RING:
                    return ("rest", split_index[u0] + TURN_SPLITS + behind)
            return ("rest", n)

        def heads_free(n, i=None, u0=None):
            old = n - HEADS_RING
            if i is None:
                return T.at(*unit_step(split_units[old]))
            if old < split_index[u0]:
                return T.at(("unit", split_units[old + TURN_SPLITS]), i - 1)
            return T.at(("unit", split_units[old]), i)

        def upcoming(state, unit, reach, ahead=HEADS_RING - 1):
            base = sum(u <= unit for u in split_units) - 1
            while state[0] < len(split_units):
                n, u = state[0], split_units[state[0]]
                if not (u <= unit or (n <= base + ahead and u <= unit + reach)):
                    break
                yield n
                state[0] += 1

        block = ctx.enter_context(nc.Block())

        @block.sync
        def _(sp):
            sp.dma_start(cols[:, :], cols_d).then_inc(inputs_landed, 16)
            sp.dma_start(pos_i[:, :], pos_d).then_inc(inputs_landed, 16)

            def load(u, slot):
                sp.dma_start(ring[:, slot, :], stream[u, :, :]).then_inc(weights_landed[slot], 16)

            def slot_read(u):
                if u >= RING:
                    name, turn = unit_step(u - RING)
                    sp.wait_ge(tensor_done, T.at(name, turn))

            u = 0
            while u < units:
                if u == [q[0] for q in loop_list][1]:
                    sp.wait_ge(tensor_done, T.at(((("b1", 1), "at"), "o", 7)))
                    sp.dma_start(x[:, 1, :, :], ctx_d).then_inc(context_landed, 16)
                if u in loops:
                    name, turns, width = loops[u]
                    for s in range(width):
                        slot_read(u + s)
                        load(u + s, (u + s) % RING)
                    with sp.Fori(1, turns) as i:
                        for s in range(width):
                            sp.wait_ge(tensor_done, T.at(("unit", u + s - RING), i) if s >= RING else
                                       T.at(("unit", u + s - RING + width), i - 1))
                            src = stream[bass.ds(i * width + (u + s), 1), :, :]
                            sp.dma_start(ring[:, (u + s) % RING, :], src.rearrange("a p n -> (a p) n"))\
                              .then_inc(weights_landed[(u + s) % RING], 16)
                    u += turns * width
                else:
                    slot_read(u)
                    load(u, u % RING)
                    if u == 1:
                        sp.dma_start(consts[:, :], consts_d).then_inc(inputs_landed, 16)
                        sp.dma_start(x[:, 0, :, :], x_d).then_inc(inputs_landed, 16)
                    u += 1
            sp.wait_ge(vector_done, V.at("final"))
            sp.dma_start(out_d, tmp[:, :, 0:SEQ]).then_inc(output_stored, 16)
            sp.wait_ge(output_stored, 16)

        @block.tensor
        def _(pe):
            cur = [0]
            nbank = [0]
            tenant = {}
            turn = [RING, 0]

            def take_bank(g, i=None):
                b = nbank[0] % BANKS
                nbank[0] += 1
                old = tenant.get(b)
                if i is None and old is not None:
                    wait_read(old)
                new_banks[g] = b
                tenant[b] = g
                return ps[:, b, :]

            def wait_read(g, turn=None):
                if A.has(("read", g)):
                    pe.wait_ge(scalar_done, A.at(("read", g), turn))
                if V.has(("read", g)):
                    pe.wait_ge(vector_done, V.at(("read", g), turn))

            def weights(name, k, n, width=1, i=None):
                while blocks[cur[0]] is None:
                    cur[0] += 1
                b = cur[0]
                assert blocks[b] == (name, k, n), (blocks[b], name, k, n)
                u = b // UB
                slot, at = u % RING, b % UB
                split = is_split(name)
                if at == 0 and split:
                    s = split_index[u]
                    if i is None:
                        pe.wait_ge(vector_done, V.at(rest_step(s)))
                    elif s - turn[1] < HEADS_RING:
                        pe.wait_ge(vector_done, V.at(("rest", s + TURN_SPLITS), i - 1))
                    else:
                        pe.wait_ge(vector_done, V.at(("rest", s), i))
                elif at == 0:
                    lands = 16 * (u // RING + 1)
                    pe.wait_ge(weights_landed[slot], lands if i is None else lands + 16 * (turn[0] // RING) * i)
                cur[0] += width
                T.unit = u
                e = b + width
                last = e % UB == 0 or all(q is None for q in blocks[e:e + UB - e % UB])
                where = slice(at * P, (at + width) * P)
                w = (heads[:, split_index[u] % HEADS_RING, where], rests[:, slot, where]) if split else \
                    ring[:, slot, where]
                return w, ("unit", u) if last else None

            def product(out, lhsT, rhs, first, last, done=None, unit=None):
                if isinstance(lhsT, tuple):
                    nc.tensor.matmul(out, lhsT[0], rhs[0], start=first, stop=False)
                    nc.tensor.matmul(out, lhsT[0], rhs[1], start=False, stop=False)
                    ins = nc.tensor.matmul(out, lhsT[1], rhs[0], start=False, stop=last)
                else:
                    ins = nc.tensor.matmul(out, lhsT, rhs, start=first, stop=last)
                if unit is not None:
                    T.found[unit] = (T.n + 1, T.loop, T.unit)
                if done is not None or unit is not None:
                    ins.then_inc(tensor_done, T.mark(done))

            def linear(out, name, ks, n, act, done=None, ready=None, i=None):
                ks = range(ks) if isinstance(ks, int) else ks
                for k in ks:
                    if ready is not None:
                        ready(k)
                    w, unit = weights(name, k, n, i=i)
                    product(out, w, act(k), k == ks[0], k == ks[-1], done if k == ks[-1] else None, unit)

            def linear_pair(outs, name, order, n, act, dones, ready=None, i=None):
                for at, (e, k) in enumerate(order):
                    if ready is not None:
                        ready(k)
                    mine = [b for b, (f, _) in enumerate(order) if f == e]
                    w, unit = weights(name, k, n + e, i=i)
                    product(outs[e], w, act(k), at == mine[0], at == mine[-1],
                            dones[e] if at == mine[-1] else None, unit)

            def h_of(k, t=slice(0, TOK)):
                return hr[:, 0, k, t], hr[:, 1, k, t]

            def once(fn):
                seen = set()

                def ready(k):
                    if k not in seen:
                        seen.add(k)
                        fn(k)
                return ready

            def mean_square(p, T_, k):
                if k == 0:
                    for q in last_cols:
                        wait_read(q)
                    last_cols[:] = [(p, "ms")]
                    new_banks[(p, "ms")] = COLS_BANK
                pe.wait_ge(scalar_done, A.at((p, "sq", k)))
                product(ps[:, COLS_BANK, 0:T_], mat("ones"), squared(T_, k), k == 0, k == KD - 1,
                        (p, "ms") if k == KD - 1 else None)

            def norm(p, T_, done=0):
                for k in range(done, KD):
                    mean_square(p, T_, k)
                return once(lambda k: pe.wait_ge(vector_done, V.at((p, "h", k))))

            def behind(p, T_):
                return lambda m: mean_square(p, T_, m - 2)

            def mod_rows(name, g, half=None, i=None, before=None):
                if half != 1:
                    for q in before or last_mod:
                        pe.wait_ge(scalar_done, A.at(("read", (q, "rows")), None if before is None else i - 1))
                for k in range(KD) if half is None else range(half * KD // 2, (half + 1) * KD // 2):
                    for r in range(2):
                        w, unit = weights(name, k, g * KD + 4 * r, 4, i)
                        t = 32 * (2 * (k % 2) + r)
                        done = ((name, g), "rows") if k == KD - 1 and r == 1 else None
                        product(ps[t:t + 32, ROWS_BANK, :], silu_c[:, k, :], w, k < 2, k >= KD - 2, done, unit)

            def mod_cols(name, g, i=None, before=None):
                n = 2 * NVEC[int(name[3]) - 1]
                if before is None:
                    for q in last_cols:
                        wait_read(q)
                else:
                    pe.wait_ge(vector_done, V.at(("read", (before[0], "cols")), i - 1))
                last_cols[:] = [((name, g), "cols")]
                pe.wait_ge(scalar_done, A.at(("read", ((name, g), "rows")), i))
                for q in range(4):
                    product(ps[:, COLS_BANK, q * n:(q + 1) * n], rows[:, q * P:(q + 1) * P], mat(f"pick{name[3]}"),
                            True, True, ((name, g), "cols") if q == 3 else None)
                last_mod[:] = [(name, g)]

            last_mod, last_cols, pending = [], [], []

            def hook(*group):
                if pending:
                    mod_cols(*pending.pop())
                if group:
                    mod_rows(*group)
                    pending.append(group)

            def ffn(p, up, down, T_, ready, guest=None, after_down=None):
                shared = T_ == SEQ
                kinds = ("up",) if shared else ("gate", "up")
                hx = lambda k: h_of(k, slice(0, T_))

                def pair(j, outs, i=None):
                    if shared:
                        outs = (outs[0][:, 0:SEQ], outs[0][:, SEQ:TOK])
                    linear_pair(outs, up, up_order(T_), 2 * j, hx,
                                (None if shared else (p, "gate", j), (p, "up", j)),
                                ready if j == 0 else None, i)

                for lo, hi in hidden_ranges(T_):
                    while blocks[cur[0]] is None:
                        cur[0] += 1
                    b0 = cur[0]
                    turns = (hi - lo) // PAIRS
                    names = [(p, kind, lo + j) for j in range(PAIRS) for kind in kinds]
                    for n in range(BANKS):
                        take_bank(names[n] if n < len(names) else (p, "spare", lo, n))
                    for n, g in enumerate(names):
                        b = (nbank[0] + n) % BANKS
                        new_banks[g] = b
                        tenant[b] = g
                    turn[:] = [loops[b0 // UB][2], split_index[b0 // UB]]
                    g0 = guest_groups(lo)
                    if guest:
                        hook()
                    for e in range(HEADS_RING):
                        pe.wait_ge(vector_done, V.at(rest_step(turn[1] + e)))
                    with T.turns(pe, (p, "up", lo), turns) as i:
                        for n, g in enumerate(names):
                            same = n - BANKS
                            if same >= 0:
                                wait_read(names[same], i)
                            else:
                                held = [m for m in range(len(names)) if m % BANKS == n % BANKS][-1]
                                wait_read(names[held], i - 1)
                            if g[1] == "up":
                                j = g[2]
                                outs = [ps[:, new_banks[(p, kind, j)], :] for kind in kinds]
                                pair(j, outs, i)
                                if guest and j - lo in (1, 2):
                                    mod_rows(guest, g0, j - lo - 1, i, [(guest, g0)])
                                if guest and j - lo == 3:
                                    mod_cols(guest, g0, i, [(guest, g0)])
                    cur[0] = b0 + turns * turn[0] * UB
                    T.unit = cur[0] // UB - 1
                    for j in range(lo + turns * PAIRS, hi):
                        pair(j, [take_bank((p, kind, j)) for kind in kinds])
                    hd = lambda k: (hid(T_, 0, k - lo), hid(T_, 1, k - lo))
                    outs = [take_bank((p, "down", lo, m))[:, 0:T_] for m in range(2)]
                    linear_pair(outs, down, late(range(lo, hi)), 0, hd, [(p, "down", lo, m) for m in range(2)],
                                once(lambda k: pe.wait_ge(vector_done, V.at(*hid_step(p, k, lo, hi)))))
                    for m in range(2, KD):
                        out = take_bank((p, "down", lo, m))
                        linear(out[:, 0:T_], down, range(lo, hi), m, hd, (p, "down", lo, m))
                        if hi == FJ:
                            after_down(m)

            def head_norm(p, pairs, head, rot, tile, between=lambda c: None):
                for c in range(pairs):
                    out = take_bank((p, "hms", c))
                    pe.wait_ge(scalar_done, A.at((p, "hsq", c)))
                    product(out, mat(head), pair_of(sq, c), True, True, (p, "hms", c))
                    if c >= 1:
                        between(c - 1)
                        rotate(p, c - 1, rot, tile)
                between(pairs - 1)
                rotate(p, pairs - 1, rot, tile)

            def rotate(p, c, rot, tile):
                out = take_bank((p, "rot", c))
                pe.wait_ge(vector_done, V.at((p, "hn", c)))
                product(out, mat(rot), pair_of(tile, c), True, True, (p, "rot", c))

            def attention(p, tasks, scores, values, ready, between=lambda t: None):
                ready()
                for t in range(tasks + 3):
                    if t < tasks:
                        out = take_bank((p, "s", t))
                        scores(t, out)
                    if 2 <= t < tasks + 2:
                        s = t - 2
                        out = take_bank((p, "pt", s))
                        pe.wait_ge(vector_done, V.at((p, "p", s)))
                        order = transposed_order(p)
                        for b in range(4):
                            ins = nc.tensor.transpose(out[:, order[b] * P:(order[b] + 1) * P],
                                                      probs[:, s % 2, b * P:(b + 1) * P], mat("ident"))
                        ins.then_inc(tensor_done, T.mark((p, "pt", s)))
                    if t >= 3:
                        s = t - 3
                        pe.wait_ge(scalar_done, A.at((p, "ptc", s)))
                        values(s)
                    if t < tasks:
                        between(t)

            pe.wait_ge(inputs_landed, N_IN)
            pe.wait_ge(scalar_done, A.at("silu c"))
            hook("mod1_0", 0)
            hook("mod1_0", 1)
            hook()
            for l in range(DEPTH):
                p = ("b1", l)
                guests = MIXER_MODS[l]
                ready = norm((*p, "mix"), SEQ, 0 if l == 0 else KD - 2)
                hx = lambda k: h_of(k, slice(0, SEQ))
                for c in range(3):
                    out = take_bank((p, "lat", c))
                    linear(out[:, 0:SEQ], f"lat_{l}", KD, 2 * c, hx, None, ready)
                    linear(out[:, SEQ:TOK], f"lat_{l}", KD, 2 * c + 1, hx, (p, "lat", c))
                hook(*guests[0])
                out = take_bank((p, "latms"))
                for k in range(5):
                    pe.wait_ge(scalar_done, A.at((p, "latsq", k // 2)))
                    q = k < 3
                    product(out[:, 0:SEQ] if q else out[:, SEQ:TOK], mat("ones"),
                            sq[:, k, :], k in (0, 3), k in (2, 4), (p, "latms") if k == 4 else None)
                for c in range(4):
                    out = take_bank((p, "uq", c))
                    for e in range(2):
                        linear(out[:, e * SEQ:(e + 1) * SEQ], f"uq_{l}", 3, 2 * c + e,
                               lambda k: lat[:, k, :], (p, "uq", c) if e else None,
                               (lambda k: pe.wait_ge(vector_done, V.at((p, "latn", k)))) if c == e == 0 else None)
                for c in range(4):
                    out = take_bank((p, "uk", c))
                    for e in range(2):
                        linear(out[:, e * SEQ:(e + 1) * SEQ], f"uk_{l}", 2, 2 * c + e,
                               lambda k: lat[:, 3 + k, :], (p, "uk", c) if e else None,
                               (lambda k: pe.wait_ge(vector_done, V.at((p, "latn", 3 + k)))) if c == e == 0 else None)
                outs = [take_bank((p, "va", b)) for b in range(2)]
                for k in range(2):
                    w, unit = weights(f"uv_{l}", k, 0, 4)
                    for b in range(2):
                        product(outs[b], lat[:, 3 + k, b * P:(b + 1) * P], w, k == 0, k == 1,
                                (p, "va", b) if k == 1 else None, unit if b == 1 else None)
                hook(*guests[1])

                def pair_behind(what, name):
                    def do(c):
                        out = take_bank((p, what, c))
                        linear(out[:, 0:SEQ], name, KD, 2 * c, hx)
                        linear(out[:, SEQ:TOK], name, KD, 2 * c + 1, hx, (p, what, c))
                    return do

                head_norm((p, "qa"), 4, "head_a", "rot_a", qt, pair_behind("qkb", f"qkb_{l}"))
                head_norm((p, "ka"), 4, "head_a", "rot_a", kt, pair_behind("conv", f"conv_{l}"))
                outs = [take_bank((p, "vb", b)) for b in range(2)]
                for k in range(KD):
                    w, unit = weights(f"vb_{l}", k, 0, 4)
                    for b in range(2):
                        product(outs[b], h_of(k, slice(b * P, (b + 1) * P)), w, k == 0, k == KD - 1,
                                (p, "vb", b) if k == KD - 1 else None, unit if b == 1 else None)
                hook(*guests[2])

                def early_gates(m):
                    out = take_bank((p, "g01", m))
                    linear(out[:, 0:SEQ], f"gate0_{l}", KD, m, hx)
                    linear(out[:, SEQ:TOK], f"gate1_{l}", KD, m, hx, (p, "g01", m))

                for guest in guests[3:]:
                    hook(*guest)
                head_norm((p, "qkb"), 4, "head_b", "rot_b", bt, lambda c: early_gates(c) if c < 3 else None)

                def scores(t, out):
                    for b in range(2):
                        if t < HEADS:
                            q, k = qt[:, t, b * P:(b + 1) * P], kt[:, t, :]
                        else:
                            c, r = (t - HEADS) // 2, 64 * (t % 2)
                            q, k = bt[r:r + 64, c, b * P:(b + 1) * P], bt[r:r + 64, 4 + c, :]
                        product(out[:, b * SEQ:(b + 1) * SEQ], q, k, True, True, ((p, "at"), "s", t) if b else None)

                held = [None]

                def values(s):
                    r = 64 * (s % 2)
                    if s % 2 == 0:
                        held[0] = take_bank(((p, "at"), "o", s // 2))
                    v, hh = (va, s) if s < HEADS else (vb, s - HEADS)
                    if s == 0:
                        pe.wait_ge(scalar_done, A.at(("read", (p, "vb", 1))))
                    for b in range(2):
                        product(held[0][r:r + 64, 0:SEQ], v[:, b, hh * 64:(hh + 1) * 64],
                                probs_t[:, s % 2, b * SEQ:(b + 1) * SEQ], b == 0, b == 1,
                                ((p, "at"), "o", s // 2) if b and s % 2 else (((p, "at"), "ov", s) if b else None))

                attention((p, "at"), 16, scores, values,
                          lambda: pe.wait_ge(vector_done, V.at(((p, "qkb"), "roped", 3))),
                          lambda t: early_gates(3 + t // 3) if t % 3 == 2 else None)
                out = take_bank((p, "lnm"))
                pe.wait_ge(vector_done, V.at((p, "dwc")))
                for k in range(CC):
                    product(out[:, 0:SEQ], mat("ones"), dwc[:, k, :], k == 0, k == CC - 1,
                            (p, "lnm") if k == CC - 1 else None)
                out = take_bank((p, "lnv"))
                pe.wait_ge(scalar_done, A.at((p, "csq")))
                for k in range(CC):
                    product(out[:, 0:SEQ], mat("ones"), csq[:, k, :], k == 0, k == CC - 1,
                            (p, "lnv") if k == CC - 1 else None)
                hook()
                for m in range(KD):
                    out = take_bank((p, "g2c", m))
                    linear(out[:, 0:SEQ], f"gate2_{l}", KD, m, hx, (p, "g2", m))
                    if m == 0:
                        pe.wait_ge(scalar_done, A.at((p, "oc")))
                    linear(out[:, SEQ:TOK], f"pw2_{l}", CC, m, lambda k: oc[:, k, :], (p, "g2c", m))
                    out = take_bank((p, "oab", m))
                    if m == 0:
                        pe.wait_ge(scalar_done, A.at(("read", ((p, "at"), "o", 7))))
                    linear(out[:, 0:SEQ], f"oa_{l}", 4, m, lambda k: attn[:, k, :])
                    linear(out[:, SEQ:TOK], f"ob_{l}", 4, m, lambda k: attn[:, 4 + k, :], (p, "oab", m))
                linear_pair([take_bank((p, "out", m))[:, 0:SEQ] for m in range(2)], f"out_{l}", late(range(KD)), 0,
                            lambda k: merged[:, k, :], [(p, "out", m) for m in range(2)],
                            once(lambda k: pe.wait_ge(vector_done, V.at((p, "merged", k)))))
                for m in range(2, KD):
                    out = take_bank((p, "out", m))
                    linear(out[:, 0:SEQ], f"out_{l}", KD, m, lambda k: merged[:, k, :], (p, "out", m))
                    behind((*p, "ffn"), SEQ)(m)
                ready = norm((*p, "ffn"), SEQ, KD - 2)
                ffn((*p, "ffn"), f"up_{l}", f"down_{l}", SEQ, ready, FFN_MODS[l],
                    behind(("b1", 1, "mix"), SEQ) if l == 0 else behind(("b2", 0, "f1"), TOK))

            for l in range(DEPTH):
                p = ("b2", l)
                ready = norm((*p, "f1"), TOK, KD - 2)
                ffn((*p, "f1"), f"f1up_{l}", f"f1down_{l}", TOK, ready, FFN_MODS[2] if l == 0 else None,
                    behind((*p, "mix"), TOK))
                ready = norm((*p, "mix"), TOK, KD - 2)
                hx = h_of
                if l % 2 == 0:
                    linear_pair([take_bank((p, "a", g)) for g in range(2)], "ain", together(range(KD)), 0, hx,
                                [(p, "a", g) for g in range(2)], ready)
                    for g in range(2, 4):
                        linear(take_bank((p, "a", g)), "ain", KD, g, hx, (p, "a", g))
                    for g in range(4):
                        linear(take_bank((p, "u", g)), "uin", KD, g, hx, (p, "u", g))
                    hook(*MIXER_MODS[2][0])
                    outs = [take_bank((p, "v", b)) for b in range(4)]
                    for k in range(KD):
                        w, unit = weights("vin", k, 0, 4)
                        for b in range(4):
                            product(outs[b], h_of(k, slice(b * P, (b + 1) * P)), w, k == 0, k == KD - 1,
                                    (p, "v", b) if k == KD - 1 else None, unit if b == 3 else None)
                    for guest in MIXER_MODS[2][1:]:
                        hook(*guest)
                    hook()
                    for b in range(4):
                        for q in range(2):
                            out = take_bank((p, "sp", b, q))
                            for e in range(2):
                                g = 2 * q + e
                                if b == 0:
                                    pe.wait_ge(scalar_done, A.at(("read", (p, "a", g))))
                                product(out[:, e * 256:(e + 1) * 256], a_in[:, g, b * P:(b + 1) * P],
                                        mat("dft_c"), True, True, (p, "sp", b, q) if e else None)
                    for g in range(4):
                        out = take_bank((p, "f", g))
                        for s in range(2):
                            for b in range(2):
                                t = 2 * s + b
                                if g == 0:
                                    pe.wait_ge(scalar_done, A.at(("read", (p, "sp", t, 1))))
                                o = out[:, s * SEQ:(s + 1) * SEQ]
                                product(o, spec[:, t, g, 0:128], mat("cos_n")[:, b * 256:(b + 1) * 256],
                                        b == 0, False)
                                product(o, spec[:, t, g, 128:256], mat("nsin_n")[:, b * 256:(b + 1) * 256],
                                        False, b == 1, (p, "f", g) if s and b else None)
                    for g in range(4):
                        out = take_bank((p, "mx", g))
                        if g == 0:
                            pe.wait_ge(vector_done, V.at((p, "vn")))
                        for t in range(4):
                            product(out[:, t * P:(t + 1) * P], vt_of(kt)[:, t, g * P:(g + 1) * P], mat(f"ws{g}"),
                                    True, True, (p, "mx", g) if t == 3 else None)
                    linear_pair([take_bank((p, "out", m)) for m in range(2)], "oab", late(range(KD)), 0,
                                lambda k: mixed[:, k, :], [(p, "out", m) for m in range(2)],
                                once(lambda k: pe.wait_ge(scalar_done, A.at(("read", (p, "f", k)))) if k < 4 else
                                     pe.wait_ge(vector_done, V.at((p, "sgu", k - 4)))))
                    for m in range(2, KD):
                        linear(take_bank((p, "out", m)), "oab", KD, m, lambda k: mixed[:, k, :], (p, "out", m))
                        behind((*p, "f2"), TOK)(m)
                else:
                    for c in range(4):
                        out = take_bank((p, "q", c))
                        linear(out[:, 0:SEQ], "q2", KD, 2 * c, lambda k: h_of(k, slice(0, SEQ)), None, ready)
                        linear(out[:, SEQ:TOK], "q2", KD, 2 * c + 1, lambda k: h_of(k, slice(0, SEQ)), (p, "q", c))
                    for c in range(2):
                        linear(take_bank((p, "k", c)), "k2", KD, c, hx, (p, "k", c))
                    outs = [take_bank((p, "v", b)) for b in range(4)]
                    for k in range(KD):
                        w, unit = weights("v2", k, 0, 2)
                        for b in range(4):
                            product(outs[b][:, 0:256], h_of(k, slice(b * P, (b + 1) * P)), w, k == 0, k == KD - 1,
                                    (p, "v", b) if k == KD - 1 else None, unit if b == 3 else None)
                    head_norm((p, "q"), 4, "ones", "rot_b", qt)
                    head_norm((p, "k"), 2, "ones", "rot_b", kt)
                    held = [None]

                    def scores(t, out):
                        hh, b = divmod(t, 2)
                        product(out, qt[:, hh, b * P:(b + 1) * P], pair_of(kt, hh // 4), True, True,
                                ((p, "at"), "s", t))

                    def values(s):
                        hh, b = divmod(s, 2)
                        if b == 0:
                            held[0] = take_bank(((p, "at"), "o", hh))
                        for c in range(4):
                            product(held[0][:, b * P:(b + 1) * P], v2_of(va)[:, c, (hh // 4) * P:(hh // 4 + 1) * P],
                                    probs_t[:, s % 2, c * P:(c + 1) * P], c == 0, c == 3,
                                    (((p, "at"), "o", hh) if b else ((p, "at"), "ov", s)) if c == 3 else None)

                    def both():
                        pe.wait_ge(vector_done, V.at(((p, "k"), "roped", 1)))
                        pe.wait_ge(scalar_done, A.at(("read", (p, "v", 3))))

                    attention((p, "at"), 16, scores, values, both)
                    linear_pair([take_bank((p, "out", m))[:, 0:SEQ] for m in range(2)], "o2", late(range(KD)), 0,
                                lambda k: attn[:, k, :], [(p, "out", m) for m in range(2)],
                                once(lambda k: pe.wait_ge(scalar_done, A.at(("read", ((p, "at"), "o", k))))))
                    for m in range(2, KD):
                        out = take_bank((p, "out", m))
                        linear(out[:, 0:SEQ], "o2", KD, m, lambda k: attn[:, k, :], (p, "out", m))
                        behind((*p, "f2"), SEQ)(m)
                T_ = TOK if l == 0 else SEQ
                ready = norm((*p, "f2"), T_, KD - 2)
                ffn((*p, "f2"), f"f2up_{l}", f"f2down_{l}", T_, ready, None,
                    behind(("b2", 1, "f1"), TOK) if l == 0 else behind("fin", SEQ))
            norm("fin", SEQ, KD - 2)

        @block.scalar
        def _(act):
            def own(i=None):
                if A.n:
                    act.wait_ge(scalar_done, A.so_far(i))

            state = [0]

            def after(S, name, turn=None):
                if turn is None and A.loop is None:
                    for n in upcoming(state, S.unit_of(name), 5):
                        split(n)
                    A.unit = max(A.unit, S.unit_of(name))
                return S.at(name, turn)

            def prepare(p):
                for n in upcoming(state, T.unit_of((p, "ms")), RING - 1, HEADS_RING):
                    split(n)

            def in_turn(u0, j, i, lo):
                first = split_index[u0] + (j - lo + 2) * PAIR_UNITS
                for n in range(first, first + PAIR_UNITS):
                    split(n, i, u0)

            def before_loop(u0):
                while state[0] < split_index[u0] + HEADS_RING:
                    split(state[0])
                    state[0] += 1

            def past_loop(u0):
                name, turns, width = loops[u0]
                state[0] = split_index[u0] + turns * TURN_SPLITS + HEADS_RING
                A.unit = u0 + turns * width - 1

            def rest_pair(j):
                for n in range(state[0], min(state[0] + PAIR_UNITS, len(split_units))):
                    split(n)
                    state[0] += 1

            def split(n, i=None, u0=None):
                u = split_units[n]
                lands = 16 * (u // RING + 1)
                act.wait_ge(weights_landed[u % RING], lands if i is None else lands + 16 * (loops[u0][2] // RING) * i)
                if n >= HEADS_RING:
                    act.wait_ge(tensor_done, heads_free(n, i, u0))
                nc.scalar.activation(heads[:, n % HEADS_RING, :], ring[:, u % RING, :], ACT.Copy)\
                  .then_inc(scalar_done, A.mark(("heads", n)))

            def norm(p, T_, halves, updated, shift):
                for k in range(KD):
                    if k == KD - 2 and shift is not None:
                        prepare(p)
                    if updated is not None:
                        act.wait_ge(vector_done, after(V, updated(k)))
                    nc.scalar.activation(squared(T_, k).rearrange("p (v t) -> p v t", v=T_ // SEQ),
                                         x[:, 0:T_ // SEQ, k, :], ACT.Square)\
                      .then_inc(scalar_done, A.mark((p, "sq", k)))
                act.wait_ge(tensor_done, after(T, (p, "ms")))
                nc.scalar.activation(rs[:, 0:T_], bank((p, "ms"))[:, 0:T_], ACT.Sqrt, bias=col("eps"), scale=1.0 / D)\
                  .then_inc(scalar_done, A.mark(("read", (p, "ms"))))
                if shift is None:
                    return
                for k in range(KD):
                    act.wait_ge(vector_done, after(V, (p, "hn", k)))
                    for v in range(halves):
                        t = slice(v * SEQ, (v + 1) * SEQ)
                        nc.scalar.activation(hr[:, 0, k, t], tmp[:, k, t], ACT.Identity, bias=shift(k, v))\
                          .then_inc(scalar_done, A.mark((p, "hh", k) if v == halves - 1 else None))

            def copy_pair(dst, g, read=True):
                act.wait_ge(tensor_done, after(T, g))
                nc.scalar.activation(dst, bank(g), ACT.Copy)\
                  .then_inc(scalar_done, A.mark(("read", g) if read else None))

            def squares(p, pairs, tile, from_bank=None):
                for c in range(pairs):
                    if from_bank is not None:
                        copy_pair(pair_of(tile, c), from_bank(c))
                    own()
                    nc.scalar.activation(pair_of(sq, c), pair_of(tile, c), ACT.Square)\
                      .then_inc(scalar_done, A.mark((p, "hsq", c)))

            def roots(p, pairs, scale=1.0, between=None):
                for c in range(pairs):
                    if between is not None and c >= 2:
                        between(c - 2)
                    act.wait_ge(tensor_done, after(T, (p, "hms", c)))
                    if c >= 2:
                        act.wait_ge(vector_done, after(V, (p, "hn", c - 2)))
                    nc.scalar.activation(hrs[:, c % 2, :], bank((p, "hms", c)), ACT.Sqrt, bias=col("eps"),
                                         scale=scale)\
                      .then_inc(scalar_done, A.mark(("read", (p, "hms", c))))

            def softmax(p, t, J, scale):
                act.wait_ge(vector_done, after(V, (p, "nm", t)))
                W = 512 // J
                for b in range(J):
                    nc.scalar.activation(probs[:, t % 2, b * W:(b + 1) * W], probs[:, t % 2, b * W:(b + 1) * W],
                                         ACT.Exp, bias=stat[:, t % 2, b:b + 1], scale=scale,
                                         accum_out=stat[:, t % 2, 2 + b:3 + b])\
                      .then_inc(scalar_done, A.mark((p, "e", t) if b == J - 1 else None))

            def attention(p, tasks, J, scale, out_of, between=lambda t: None):
                for t in range(tasks + 2):
                    if t < tasks:
                        softmax(p, t, J, scale(t))
                    if t >= 1 and t - 1 < tasks:
                        s = t - 1
                        act.wait_ge(tensor_done, after(T, (p, "pt", s)))
                        if s >= 2:
                            act.wait_ge(tensor_done, after(T, out_step(p, s - 2)))
                        nc.scalar.activation(probs_t[:, s % 2, :], bank((p, "pt", s)), ACT.Copy)\
                          .then_inc(scalar_done, A.mark((p, "ptc", s)))
                        A.found[("read", (p, "pt", s))] = A.found[(p, "ptc", s)]
                    if t >= 2 and (t - 2) % 2 == 1:
                        c = (t - 2) // 2
                        act.wait_ge(tensor_done, after(T, (p, "o", c)))
                        nc.scalar.activation(out_of(c), bank((p, "o", c))[:, 0:SEQ], ACT.Copy)\
                          .then_inc(scalar_done, A.mark(("read", (p, "o", c))))
                    if t < tasks:
                        between(t)

            def ffn1(p, l, guest):
                w0, b0 = vcol[f"ffn_w_{l}"][0], vcol[f"ffn_b_{l}"][0]

                def c(at, j, i):
                    return cols[:, at + j:at + j + 1] if i is None else cols[:, bass.ds(i * PAIRS + (at + j), 1)]

                def pair(j, i=None):
                    act.wait_ge(tensor_done, after(T, (p, "up", j), i))
                    act.wait_ge(vector_done, buffer_free(V, p, j, i))
                    s = j % 2
                    for ab in range(2):
                        nc.scalar.activation(zc[:, s, ab, :], two(bank((p, "up", j)))[:, ab, :], ACT.Identity,
                                             scale=c(w0 + (2 * 2 + ab) * FJ, j, i), bias=c(b0 + ab * FJ, j, i))\
                          .then_inc(scalar_done, A.mark())
                    nc.scalar.activation(z[:, s, :, FFN_TAPS - 1:], two(bank((p, "up", j))), ACT.Copy)\
                      .then_inc(scalar_done, A.mark((p, "z", j)))
                    A.found[("read", (p, "up", j))] = A.found[(p, "z", j)]

                def finish(j, i=None):
                    s = j % 2
                    act.wait_ge(vector_done, after(V, (p, "cv", j), i))
                    nc.scalar.activation(zc[:, s, 0, :], zc[:, s, 0, :], ACT.Silu)\
                      .then_inc(scalar_done, A.mark((p, "si", j)))
                    hidden_heads(p, j, SEQ, 0, i)

                each_pair(p, SEQ, pair, finish, guest)

            def hidden_heads(p, j, T_, lo, i):
                act.wait_ge(vector_done, after(V, (p, "gated", j), i))
                nc.scalar.activation(hid_at(hidr, T_, 0, j - lo, i), sg[:, (j - lo) % 2, 0:T_], ACT.Copy)\
                  .then_inc(scalar_done, A.mark((p, "hidh", j)))

            def each_pair(p, T_, begin, finish, guest):
                for lo, hi in hidden_ranges(T_):
                    turns = (hi - lo) // PAIRS
                    u0 = next(loop_units)
                    g0 = guest_groups(lo)
                    if guest:
                        cols_before[:] = [(guest, g0)]
                    before_loop(u0)
                    with A.turns(act, (p, "up", lo), turns) as i:
                        for j in range(lo, lo + PAIRS):
                            begin(j, i)
                            in_turn(u0, j, i, lo)
                            finish(j, i)
                            if guest and j - lo == 2:
                                mod_rows(guest, g0, i)
                    past_loop(u0)
                    for j in range(lo + turns * PAIRS, hi):
                        begin(j)
                        rest_pair(j)
                        finish(j)

            loop_units = iter([q[0] for q in loop_list])

            def ffn2_(p, T_, guest=None):
                los = [lo for lo, hi in hidden_ranges(T_)]

                def gate(j, i=None):
                    lo = max(q for q in los if q <= j)
                    g = (p, "up", j) if T_ == SEQ else (p, "gate", j)
                    act.wait_ge(tensor_done, after(T, g, i))
                    if i is not None or j - lo >= 2:
                        act.wait_ge(vector_done, buffer_free(V, p, j, i, lo))
                    nc.scalar.activation(sg[:, (j - lo) % 2, 0:T_], bank(g)[:, 0:T_], ACT.Silu)\
                      .then_inc(scalar_done, A.mark((p, "si", j)))
                    A.found[("read", g)] = A.found[(p, "si", j)]

                each_pair(p, T_, gate, lambda j, i=None: hidden_heads(p, j, T_, max(q for q in los if q <= j), i), guest)

            def mod_rows(name, g, i=None):
                act.wait_ge(tensor_done, after(T, ((name, g), "rows"), i))
                if cols_before:
                    act.wait_ge(tensor_done, after(T, (cols_before[0], "cols"), None if i is None else i - 1))
                nc.scalar.activation(rows[:, :], ps[:, ROWS_BANK, :], ACT.Copy)\
                  .then_inc(scalar_done, A.mark(("read", ((name, g), "rows"))))
                cols_before[:] = [(name, g)]

            cols_before = []

            act.wait_ge(inputs_landed, N_IN)
            nc.scalar.activation(silu_c, silu_c, ACT.Silu)\
              .then_inc(scalar_done, A.mark("silu c"))
            mod_rows("mod1_0", 0)
            mod_rows("mod1_0", 1)
            for n, t in enumerate((cos_a, sin_a, cos_b, sin_b)):
                act.wait_ge(vector_done, after(V, ("angle", n)))
                nc.scalar.activation(t[:, :], t[:, :], ACT.Sin).then_inc(scalar_done, A.mark(("table", n)))
            for l in range(DEPTH):
                p = ("b1", l)
                norm((*p, "mix"), SEQ, 1, None if l == 0 else lambda k: x_step(("b1", l - 1, "ffn"), "down", 0, k),
                     lambda k, v: mods_sb[:, l, k:k + 1])
                for c in range(3):
                    copy_pair(lat[:, 2 * c:2 * c + 2, :].rearrange("p a t -> p (a t)"), (p, "lat", c))
                    own()
                    nc.scalar.activation(sq[:, 2 * c:2 * c + 2, :], lat[:, 2 * c:2 * c + 2, :], ACT.Square)\
                      .then_inc(scalar_done, A.mark((p, "latsq", c)))
                guests = MIXER_MODS[l]
                act.wait_ge(tensor_done, after(T, (p, "latms")))
                for k, rank in enumerate((Q_RANK, KV_RANK)):
                    nc.scalar.activation(rs[:, k * SEQ:(k + 1) * SEQ], bank((p, "latms"))[:, k * SEQ:(k + 1) * SEQ],
                                         ACT.Sqrt, bias=col("eps"), scale=1.0 / rank)\
                      .then_inc(scalar_done, A.mark(("read", (p, "latms")) if k else None))
                mod_rows(*guests[0])
                squares((p, "qa"), 4, qt, lambda c: (p, "uq", c))
                for c in range(4):
                    act.wait_ge(tensor_done, after(T, (p, "uk", c)))
                    nc.scalar.activation(kt[0:64, 2 * c:2 * c + 2, :], two(bank((p, "uk", c)))[0:64], ACT.Copy)\
                      .then_inc(scalar_done, A.mark(("read", (p, "uk", c))))
                for b in range(2):
                    copy_pair(va[:, b, :], (p, "va", b))
                shared = lat[64:96, 5:6, :].to_broadcast([32, HEADS, SEQ])
                nc.scalar.activation(kt[64:96, :, :], shared, ACT.Copy).then_inc(scalar_done, A.mark())
                mod_rows(*guests[1])
                roots((p, "qa"), 4)
                squares((p, "ka"), 4, kt)
                for c in range(4):
                    copy_pair(pair_of(bt, c), (p, "qkb", c))

                def glu(c):
                    act.wait_ge(tensor_done, after(T, (p, "conv", c)))
                    if c >= 2:
                        act.wait_ge(vector_done, after(V, ("read", (p, "conv", c - 2))))
                    nc.scalar.activation(sg2[:, c % 2, :], bank((p, "conv", c))[:, SEQ:TOK], ACT.Sigmoid)\
                      .then_inc(scalar_done, A.mark((p, "glu", c)))

                roots((p, "ka"), 4, between=glu)
                glu(2)
                glu(3)
                squares((p, "qkb"), 4, bt)
                for b in range(2):
                    copy_pair(vb[:, b, :], (p, "vb", b))
                for guest in guests[2:]:
                    mod_rows(*guest)

                def early_gates(m):
                    act.wait_ge(tensor_done, after(T, (p, "g01", m)))
                    nc.scalar.activation(gates[m], bank((p, "g01", m)), ACT.Sigmoid)\
                      .then_inc(scalar_done, A.mark(("read", (p, "g01", m))))

                roots((p, "qkb"), 4)
                for m in range(3):
                    early_gates(m)
                attention((p, "at"), 16, 2, lambda t: (NOPE + ROPE_A) ** -0.5 if t < HEADS else 64 ** -0.5,
                          lambda c: attn[:, c, :], lambda t: early_gates(3 + t // 3) if t % 3 == 2 else None)
                act.wait_ge(vector_done, after(V, (p, "cen")))
                nc.scalar.activation(csq[:, :, :], dwc[:, :, :], ACT.Square).then_inc(scalar_done, A.mark((p, "csq")))
                act.wait_ge(tensor_done, after(T, (p, "lnv")))
                nc.scalar.activation(rs[:, 0:SEQ], bank((p, "lnv"))[:, 0:SEQ], ACT.Sqrt, bias=col("eps"),
                                     scale=1.0 / CONV_CH)\
                  .then_inc(scalar_done, A.mark(("read", (p, "lnv"))))
                act.wait_ge(vector_done, after(V, (p, "lnn")))
                for c in range(CC):
                    nc.scalar.activation(oc[:, c, :], dwc[:, c, :], ACT.Silu, bias=col(f"ln_b_{l}", c),
                                         scale=col(f"ln_g_{l}", c))\
                      .then_inc(scalar_done, A.mark((p, "oc") if c == CC - 1 else None))
                for m in range(KD):
                    if m >= 2:
                        act.wait_ge(vector_done, after(V, (p, "merged", m - 2)))
                    act.wait_ge(tensor_done, after(T, (p, "g2c", m)))
                    nc.scalar.activation(sg2[:, m % 2, :], bank((p, "g2c", m))[:, 0:SEQ], ACT.Sigmoid)\
                      .then_inc(scalar_done, A.mark((p, "sg2", m)))
                norm((*p, "ffn"), SEQ, 1, lambda k: x_step(p, "out", k), lambda k, v: mods_sb[:, l, 3 * KD + k:3 * KD + k + 1])
                ffn1((*p, "ffn"), l, FFN_MODS[l])
            for l in range(DEPTH):
                p = ("b2", l)

                def shift(n):
                    return lambda k, v: mods_sb[:, l, (n * KD + k) * 2 + v:(n * KD + k) * 2 + v + 1]

                before = ("b1", 1, "ffn") if l == 0 else ("b2", 0, "f2")
                if l == 0:
                    act.wait_ge(context_landed, 16)
                norm((*p, "f1"), TOK, 2, lambda k: x_step(before, "down", l * (FJ // 2), k), shift(0))
                ffn2_((*p, "f1"), TOK, FFN_MODS[2] if l == 0 else None)
                norm((*p, "mix"), TOK, 2, lambda k: x_step((*p, "f1"), "down", FJ // 2, k), shift(3))
                if l % 2 == 0:
                    for g in range(4):
                        copy_pair(a_in[:, g, :], (p, "a", g))
                    for g in range(4):
                        act.wait_ge(tensor_done, after(T, (p, "u", g)))
                        nc.scalar.activation(pair_of(qt, g), bank((p, "u", g)), ACT.Gelu_apprx_tanh)\
                          .then_inc(scalar_done, A.mark(("read", (p, "u", g))))
                    mod_rows(*MIXER_MODS[2][0])
                    for b in range(4):
                        act.wait_ge(tensor_done, after(T, (p, "v", b)))
                        nc.scalar.activation(vt_of(kt)[:, b, :], bank((p, "v", b)), ACT.Gelu_apprx_tanh)\
                          .then_inc(scalar_done, A.mark(("read", (p, "v", b))))
                    for guest in MIXER_MODS[2][1:]:
                        mod_rows(*guest)
                    for b in range(4):
                        for q in range(2):
                            copy_pair(spec[:, b, 2 * q:2 * q + 2, :].rearrange("p a f -> p (a f)"), (p, "sp", b, q))
                    act.wait_ge(vector_done, after(V, (p, "vss")))
                    nc.scalar.activation(rs[:, 0:16], rs[:, 0:16], ACT.Sqrt, bias=col("eps"), scale=1.0 / P)\
                      .then_inc(scalar_done, A.mark((p, "vrt")))
                    for g in range(4):
                        copy_pair(mixed[:, g, :], (p, "f", g))
                else:
                    squares((p, "q"), 4, qt, lambda c: (p, "q", c))
                    for c in range(2):
                        copy_pair(pair_of(kt, c), (p, "k", c))
                    for b in range(4):
                        act.wait_ge(tensor_done, after(T, (p, "v", b)))
                        nc.scalar.activation(v2_of(va)[:, b, :], bank((p, "v", b))[:, 0:256], ACT.Copy)\
                          .then_inc(scalar_done, A.mark(("read", (p, "v", b))))
                    roots((p, "q"), 4, 1.0 / P)
                    squares((p, "k"), 2, kt)
                    roots((p, "k"), 2, 1.0 / P)
                    attention((p, "at"), 16, 1, lambda t: 128 ** -0.5, lambda c: attn[:, c, :])
                T_ = TOK if l == 0 else SEQ
                norm((*p, "f2"), T_, T_ // SEQ, lambda k: x_step(p, "out", k), shift(6))
                ffn2_((*p, "f2"), T_)
            norm("fin", SEQ, 1, lambda k: x_step(("b2", 1, "f2"), "down", 0, k), None)

        @block.vector
        def _(dve):
            def own(i=None):
                if V.n:
                    dve.wait_ge(vector_done, V.so_far(i))

            def step(ins, name=None, i=None):
                ins.then_inc(vector_done, V.mark(name))
                own(i)

            state = [0]

            def after(S, name, turn=None):
                if turn is None and V.loop is None:
                    for n in upcoming(state, S.unit_of(name), 5):
                        split(n)
                    V.unit = max(V.unit, S.unit_of(name))
                return S.at(name, turn)

            def prepare(p):
                for n in upcoming(state, T.unit_of((p, "ms")), RING - 1, HEADS_RING):
                    split(n)

            def in_turn(u0, j, i, lo):
                first = split_index[u0] + (j - lo + 2) * PAIR_UNITS
                for n in range(first, first + PAIR_UNITS):
                    split(n, i, u0)

            def before_loop(u0):
                while state[0] < split_index[u0] + HEADS_RING:
                    split(state[0])
                    state[0] += 1

            def past_loop(u0):
                name, turns, width = loops[u0]
                state[0] = split_index[u0] + turns * TURN_SPLITS + HEADS_RING
                V.unit = u0 + turns * width - 1

            def rest_pair(j):
                for n in range(state[0], min(state[0] + PAIR_UNITS, len(split_units))):
                    split(n)
                    state[0] += 1

            def split(n, i=None, u0=None):
                u = split_units[n]
                dve.wait_ge(scalar_done, after(A, ("heads", n) if i is not None else heads_step(n), i))
                nc.vector.tensor_tensor(rests[:, u % RING, :], ring[:, u % RING, :],
                                        as_f32(heads[:, n % HEADS_RING, :]), ALU.subtract)\
                  .then_inc(vector_done, V.mark(("rest", n)))

            def heads_step(n):
                return ("heads", n)

            def mod_cols(name, g, i=None):
                nv = NVEC[int(name[3]) - 1]
                l = int(name[5])
                b0 = vcol[f"b_{name}"][0]
                dve.wait_ge(tensor_done, after(T, ((name, g), "cols"), i))
                if i is None:
                    at = g * KD * nv
                    out, bias = mods_sb[:, l, at:at + KD * nv], cols[:, b0 + at:b0 + at + KD * nv]
                else:
                    at = i * (KD * nv) + g * KD * nv
                    out, bias = mods_sb[:, l, bass.ds(at, KD * nv)], cols[:, bass.ds(at + b0, KD * nv)]
                src = ps[:, COLS_BANK, 0:KD * nv].rearrange("p (q r v) -> p r q v", q=4, r=2)
                step(nc.vector.tensor_tensor(out.rearrange("p (r q v) -> p r q v", q=4, r=2), src,
                                             bias.rearrange("p (r q v) -> p r q v", q=4, r=2), ALU.add),
                     ("read", ((name, g), "cols")), i)

            pending = []

            def hook(*group):
                if pending:
                    mod_cols(*pending.pop())
                if group:
                    pending.append(group)

            def adapt(l, slot, scale_at, gains, v, nv):
                sc = mods_sb[:, l, scale_at * KD * nv:(scale_at + 1) * KD * nv].rearrange("p (k v) -> p k v", v=nv)
                step(nc.vector.scalar_tensor_tensor(out=amod[:, slot, :, v], in0=sc[:, :, v], scalar=1.0, in1=gains,
                                                    op0=ALU.add, op1=ALU.mult))

            def norm(p, T_, slot, shift, gain=None):
                if gain is None:
                    prepare(p)
                dve.wait_ge(scalar_done, after(A, ("read", (p, "ms"))))
                step(nc.vector.reciprocal(rs[:, 0:T_], rs[:, 0:T_]))
                halves = [slice(v * SEQ, (v + 1) * SEQ) for v in range(T_ // SEQ)]
                for k in range(KD + 1):
                    if k < KD:
                        for v, t in enumerate(halves):
                            g = gain(k) if gain else amod[:, slot, k, v:v + 1]
                            name = ("final" if k == KD - 1 else None) if gain else \
                                ((p, "hn", k) if v == len(halves) - 1 else None)
                            nc.vector.scalar_tensor_tensor(out=tmp[:, k, t], in0=x[:, v, k, :], scalar=g, in1=rs[:, t],
                                                           op0=ALU.mult, op1=ALU.mult)\
                              .then_inc(vector_done, V.mark(name))
                    if k >= 1 and gain is None:
                        dve.wait_ge(scalar_done, after(A, (p, "hh", k - 1)))
                        for v, t in enumerate(halves):
                            nc.vector.scalar_tensor_tensor(out=hr[:, 1, k - 1, t], in0=tmp[:, k - 1, t],
                                                           scalar=shift(k - 1, v), in1=as_f32(hr[:, 0, k - 1, t]),
                                                           op0=ALU.add, op1=ALU.subtract)\
                              .then_inc(vector_done, V.mark((p, "h", k - 1) if v == len(halves) - 1 else None))

            def update(p, what, T_, gate):
                for m in range(KD):
                    dve.wait_ge(tensor_done, after(T, (p, *what, m)))
                    for v in range(T_ // SEQ):
                        t = slice(v * SEQ, (v + 1) * SEQ)
                        last = v == T_ // SEQ - 1
                        nc.vector.scalar_tensor_tensor(out=x[:, v, m, :], in0=bank((p, *what, m))[:, t],
                                                       scalar=gate(m, v), in1=x[:, v, m, :],
                                                       op0=ALU.mult, op1=ALU.add)\
                          .then_inc(vector_done, V.mark(("read", (p, *what, m)) if last else None))
                own()

            def head_norm(p, pairs, tile, gain, cos, sin, between=lambda e: None):
                for c in range(pairs + 1):
                    if c < pairs:
                        b = hrs[:, c % 2, :]
                        dve.wait_ge(scalar_done, after(A, ("read", (p, "hms", c))))
                        step(nc.vector.reciprocal(b, b))
                        step(nc.vector.scalar_tensor_tensor(out=pair_of(tile, c), in0=pair_of(tile, c),
                                                            scalar=gain(c), in1=b, op0=ALU.mult, op1=ALU.mult),
                             (p, "hn", c))
                    if c >= 1:
                        e = c - 1
                        dve.wait_ge(tensor_done, after(T, (p, "rot", e)))
                        a, b2 = rt[:, 0, :], rt[:, 1, :]
                        tp = pair_of(tile, e)
                        shaped = two if cos(e).shape[1] == SEQ else (lambda q: q)
                        wide = (lambda q: q.rearrange("p (a t) -> p a t", a=1).to_broadcast([P, 2, SEQ])) \
                            if cos(e).shape[1] == SEQ else (lambda q: q)
                        step(nc.vector.tensor_tensor(shaped(b2), shaped(bank((p, "rot", e))), wide(sin(e)), ALU.mult),
                             ("read", (p, "rot", e)))
                        step(nc.vector.tensor_tensor(shaped(a), shaped(tp), wide(cos(e)), ALU.mult))
                        step(nc.vector.tensor_tensor(tp, a, b2, ALU.add), (p, "roped", e))
                        between(e)

            def attention(p, tasks, J, scale, masked, between=None):
                W = 512 // J

                def first(t):
                    dve.wait_ge(tensor_done, after(T, (p, "s", t)))
                    if t >= 2:
                        dve.wait_ge(tensor_done, after(T, (p, "pt", t - 2)))
                    pr = probs[:, t % 2, :]
                    if masked:
                        step(nc.vector.tensor_tensor(pr, bank((p, "s", t)), mat("mask"), ALU.add), ("read", (p, "s", t)))
                    else:
                        step(nc.vector.tensor_copy(pr, bank((p, "s", t))), ("read", (p, "s", t)))
                    st = stat[:, t % 2, :]
                    step(nc.vector.tensor_reduce(st[:, 4:4 + J], pr.rearrange("p (j w) -> p j w", w=W), AX.X, ALU.max))
                    step(nc.vector.tensor_scalar(st[:, 0:J], st[:, 4:4 + J], -scale(t), None, ALU.mult), (p, "nm", t))

                def second(t):
                    dve.wait_ge(scalar_done, after(A, (p, "e", t)))
                    st = stat[:, t % 2, :]
                    step(nc.vector.reciprocal(st[:, 6:6 + J], st[:, 2:2 + J]))
                    for b in range(J):
                        o = probs[:, t % 2, b * W:(b + 1) * W]
                        step(nc.vector.tensor_scalar(o, o, st[:, 6 + b:7 + b], None, ALU.mult),
                             (p, "p", t) if b == J - 1 else None)

                for t in range(tasks + 1):
                    if t < tasks:
                        first(t)
                    if t >= 1:
                        second(t - 1)
                    if t < tasks and between is not None:
                        between(t)

            def each_pair(p, T_, begin, finish, guest, gate):
                for lo, hi in hidden_ranges(T_):
                    turns = (hi - lo) // PAIRS
                    u0 = next(loop_units)
                    g0 = guest_groups(lo)
                    before_loop(u0)
                    with V.turns(dve, (p, "up", lo), turns) as i:
                        for j in range(lo, lo + PAIRS):
                            begin(j, i)
                            first = split_index[u0] + (j - lo + 2) * PAIR_UNITS
                            split(first, i, u0)
                            finish(j, i)
                            split(first + 1, i, u0)
                            hidden_rests(p, j, T_, lo, i)
                            if guest and j - lo == 3:
                                mod_cols(guest, g0, i)
                    past_loop(u0)
                    for j in range(lo + turns * PAIRS, hi):
                        begin(j)
                        rest_pair(j)
                        finish(j)
                        hidden_rests(p, j, T_, lo, None)
                    update(p, ("down", lo), T_, gate)

            loop_units = iter([q[0] for q in loop_list])

            def hidden_rests(p, j, T_, lo, i):
                dve.wait_ge(scalar_done, after(A, (p, "hidh", j), i))
                step(nc.vector.tensor_tensor(hid_at(hidr, T_, 1, j - lo, i), sg[:, (j - lo) % 2, 0:T_],
                                             as_f32(hid_at(hidr, T_, 0, j - lo, i)), ALU.subtract), (p, "hid", j), i)

            def ffn1(p, l, guest, gate):
                w0 = vcol[f"ffn_w_{l}"][0]

                def pair(j, i=None):
                    s = j % 2
                    dve.wait_ge(scalar_done, after(A, (p, "z", j), i))
                    for tap in (1, 0):
                        for ab in range(2):
                            at = w0 + (tap * 2 + ab) * FJ + j
                            w = cols[:, at:at + 1] if i is None else cols[:, bass.ds(i * PAIRS + at, 1)]
                            nc.vector.scalar_tensor_tensor(out=zc[:, s, ab, :], in0=z[:, s, ab, tap:tap + SEQ],
                                                           scalar=w, in1=zc[:, s, ab, :], op0=ALU.mult, op1=ALU.add)\
                              .then_inc(vector_done, V.mark((p, "cv", j) if (tap, ab) == (0, 1) else None))
                        own(i)

                def join(j, i=None):
                    dve.wait_ge(scalar_done, after(A, (p, "si", j), i))
                    step(nc.vector.tensor_tensor(sg[:, j % 2, 0:SEQ], zc[:, j % 2, 0, :], zc[:, j % 2, 1, :], ALU.mult),
                         (p, "gated", j), i)

                step(nc.vector.memset(z[:, :, :, 0:FFN_TAPS - 1], 0.0))
                each_pair(p, SEQ, pair, join, guest, gate)

            def ffn2_(p, T_, gate, guest=None):
                los = [lo for lo, hi in hidden_ranges(T_)]

                def join(j, i=None):
                    lo = max(q for q in los if q <= j)
                    g = (p, "up", j)
                    dve.wait_ge(tensor_done, after(T, g, i))
                    dve.wait_ge(scalar_done, after(A, (p, "si", j), i))
                    up = bank(g)[:, SEQ:TOK] if T_ == SEQ else bank(g)
                    s_ = sg[:, (j - lo) % 2, 0:T_]
                    step(nc.vector.tensor_tensor(s_, s_, up, ALU.mult), (p, "gated", j), i)
                    V.found[("read", g)] = V.found[(p, "gated", j)]

                each_pair(p, T_, join, lambda j, i=None: None, guest, gate)

            dve.wait_ge(inputs_landed, N_IN)
            step(nc.vector.tensor_copy(rs[:, 0:SEQ], pos_i[:, :]))
            for n, (t, f, quarter) in enumerate(((cos_a, "inv_freq_a", 1), (sin_a, "inv_freq_a", 0),
                                                 (cos_b, "inv_freq_b", 1), (sin_b, "inv_freq_b", 0))):
                ang, k = rt[:, 0, 0:SEQ], rt[:, 1, 0:SEQ]
                step(nc.vector.tensor_scalar(ang, rs[:, 0:SEQ], col(f), None, ALU.mult))
                step(nc.vector.tensor_scalar(k, ang, 1.0 / (2.0 * np.pi), 0.25 * quarter, ALU.mult, ALU.add))
                step(nc.vector.tensor_scalar(k, k, 12582912.0, None, ALU.add))
                step(nc.vector.tensor_scalar(k, k, 12582912.0, None, ALU.subtract))
                for part_ in TWO_PI:
                    step(nc.vector.scalar_tensor_tensor(out=ang, in0=k, scalar=-part_, in1=ang,
                                                        op0=ALU.mult, op1=ALU.add))
                if quarter:
                    step(nc.vector.tensor_scalar(ang, ang, np.pi / 2, None, ALU.add))
                step(nc.vector.tensor_scalar(t[:, :], ang, 3.1415925, -3.1415925, ALU.min, ALU.max), ("angle", n))
            step(nc.vector.memset(kt[96:128, :, :], 0.0), "kt zero")
            hook("mod1_0", 0)
            hook("mod1_0", 1)
            hook()
            for l in range(DEPTH):
                p = ("b1", l)
                guests = MIXER_MODS[l]
                adapt(l, 0, 1, col(f"g_mix1_{l}", 0, KD), 0, 1)
                norm((*p, "mix"), SEQ, 0, lambda k, v: mods_sb[:, l, k:k + 1])
                dve.wait_ge(scalar_done, after(A, ("read", (p, "latms"))))
                step(nc.vector.reciprocal(rs[:, :], rs[:, :]))
                for k in range(5):
                    g = col(f"g_qlat_{l}", k) if k < 3 else col(f"g_kvlat_{l}", k - 3)
                    r = rs[:, 0:SEQ] if k < 3 else rs[:, SEQ:TOK]
                    step(nc.vector.scalar_tensor_tensor(out=lat[:, k, :], in0=lat[:, k, :], scalar=g, in1=r,
                                                        op0=ALU.mult, op1=ALU.mult), (p, "latn", k))
                hook(*guests[0])
                if l == 0:
                    dve.wait_ge(scalar_done, after(A, ("table", 3)))
                hook(*guests[1])
                head_norm((p, "qa"), 4, qt, lambda c: col(f"g_qa_{l}"), lambda e: cos_a[:, :], lambda e: sin_a[:, :])
                step(nc.vector.memset(u_pad[:, :, 0:TAPS - 1], 0.0))

                def glu(c):
                    dve.wait_ge(scalar_done, after(A, (p, "glu", c)))
                    step(nc.vector.tensor_tensor(u_pad[:, c, TAPS - 1:], bank((p, "conv", c))[:, 0:SEQ],
                                                 sg2[:, c % 2, :], ALU.mult), ("read", (p, "conv", c)))

                head_norm((p, "ka"), 4, kt, lambda c: col(f"g_ka_{l}"), lambda e: cos_a[:, :], lambda e: sin_a[:, :],
                          glu)
                for guest in guests[2:]:
                    hook(*guest)
                head_norm((p, "qkb"), 4, bt, lambda c: col(f"g_qb_{l}" if c < 2 else f"g_kb_{l}"),
                          lambda e: cos_b[:, :], lambda e: sin_b[:, :])

                def taps(t):
                    for tap in range(2 * t, min(2 * t + 2, TAPS)):
                        for c in range(CC):
                            w = col(f"conv_w_{l}", tap * CC + c)
                            name = (p, "dwc") if tap == TAPS - 1 and c == CC - 1 else None
                            if tap == 0:
                                nc.vector.tensor_scalar(dwc[:, c, :], u_pad[:, c, 0:SEQ], w, col(f"conv_b_{l}", c),
                                                        ALU.mult, ALU.add).then_inc(vector_done, V.mark(name))
                            else:
                                nc.vector.scalar_tensor_tensor(out=dwc[:, c, :], in0=u_pad[:, c, tap:tap + SEQ],
                                                               scalar=w, in1=dwc[:, c, :], op0=ALU.mult, op1=ALU.add)\
                                  .then_inc(vector_done, V.mark(name))
                        own()

                attention((p, "at"), 16, 2, lambda t: (NOPE + ROPE_A) ** -0.5 if t < HEADS else 64 ** -0.5, True, taps)
                dve.wait_ge(tensor_done, after(T, (p, "lnm")))

                def spread(a):
                    return a.rearrange("p (a t) -> p a t", a=1).to_broadcast([P, CC, SEQ])

                step(nc.vector.scalar_tensor_tensor(out=dwc[:, :, :], in0=spread(bank((p, "lnm"))[:, 0:SEQ]),
                                                    scalar=-1.0 / CONV_CH, in1=dwc[:, :, :], op0=ALU.mult, op1=ALU.add),
                     (p, "cen"))
                V.found[("read", (p, "lnm"))] = V.found[(p, "cen")]
                dve.wait_ge(scalar_done, after(A, ("read", (p, "lnv"))))
                step(nc.vector.reciprocal(rs[:, 0:SEQ], rs[:, 0:SEQ]))
                step(nc.vector.tensor_tensor(dwc[:, :, :], dwc[:, :, :], spread(rs[:, 0:SEQ]), ALU.mult), (p, "lnn"))
                hook()
                for m in range(KD):
                    a, b = rt[:, 0, :], rt[:, 1, 0:SEQ]
                    dve.wait_ge(tensor_done, after(T, (p, "g2c", m)))
                    dve.wait_ge(scalar_done, after(A, (p, "sg2", m)))
                    step(nc.vector.scalar_tensor_tensor(out=b, in0=bank((p, "g2c", m))[:, SEQ:TOK],
                                                        scalar=col(f"pw2_b_{l}", m), in1=sg2[:, m % 2, :],
                                                        op0=ALU.add, op1=ALU.mult), ("read", (p, "g2c", m)))
                    dve.wait_ge(tensor_done, after(T, (p, "oab", m)))
                    step(nc.vector.tensor_tensor(a, bank((p, "oab", m)), gates[m], ALU.mult),
                         ("read", (p, "oab", m)))
                    step(nc.vector.tensor_tensor(b, b, a[:, 0:SEQ], ALU.add))
                    step(nc.vector.tensor_tensor(merged[:, m, :], b, a[:, SEQ:TOK], ALU.add), (p, "merged", m))
                update(p, ("out",), SEQ, lambda m, v: mods_sb[:, l, 2 * KD + m:2 * KD + m + 1])
                adapt(l, 1, 4, col(f"g_ffn1_{l}", 0, KD), 0, 1)
                norm((*p, "ffn"), SEQ, 1, lambda k, v: mods_sb[:, l, 3 * KD + k:3 * KD + k + 1])
                ffn1((*p, "ffn"), l, FFN_MODS[l], lambda m, v: mods_sb[:, l, 5 * KD + m:5 * KD + m + 1])
                own()
            for l in range(DEPTH):
                p = ("b2", l)
                for n in range(3):
                    for v in range(2):
                        adapt(l, n, 3 * n + 1, col(f"g2_{l}", n * KD, KD), v, 2)
                for n in (2, 8):
                    g = mods_sb[:, l, n * KD * 2:(n + 1) * KD * 2]
                    step(nc.vector.tensor_scalar(g, g, 0.5, None, ALU.mult))

                if l == 0:
                    dve.wait_ge(context_landed, 16)

                def gate(n):
                    return lambda m, v: mods_sb[:, l, (n * KD + m) * 2 + v:(n * KD + m) * 2 + v + 1]

                norm((*p, "f1"), TOK, 0, gate(0))
                ffn2_((*p, "f1"), TOK, gate(2), FFN_MODS[2] if l == 0 else None)
                norm((*p, "mix"), TOK, 1, gate(3))
                if l % 2 == 0:
                    vt = vt_of(kt)
                    hook(*MIXER_MODS[2][0])
                    for guest in MIXER_MODS[2][1:]:
                        hook(*guest)
                    hook()
                    for b in range(4):
                        dve.wait_ge(scalar_done, after(A, ("read", (p, "v", b))))
                        step(nc.vector.tensor_tensor(vt_of(sq)[:, b, :], vt[:, b, :], vt[:, b, :], ALU.mult))
                        step(nc.vector.tensor_reduce(rs[:, 4 * b:4 * b + 4],
                                                     vt_of(sq)[:, b, :].rearrange("p (g d) -> p g d", g=4),
                                                     AX.X, ALU.add), (p, "vss") if b == 3 else None)
                    dve.wait_ge(scalar_done, after(A, (p, "vrt")))
                    step(nc.vector.reciprocal(rs[:, 0:16], rs[:, 0:16]))
                    for b in range(4):
                        for g in range(4):
                            o = vt[:, b, g * P:(g + 1) * P]
                            step(nc.vector.scalar_tensor_tensor(out=o, in0=o, scalar=rs[:, 4 * b + g:4 * b + g + 1],
                                                                in1=mat("g_v")[:, g * P:(g + 1) * P],
                                                                op0=ALU.mult, op1=ALU.mult),
                                 (p, "vn") if b == g == 3 else None)
                    for g in range(4):
                        dve.wait_ge(tensor_done, after(T, (p, "mx", g)))
                        bs = mat("b_s")[:, g * P:(g + 1) * P].rearrange("p (a t) -> p a t", a=1)\
                            .to_broadcast([P, 4, P])
                        o = rt[:, 0, :]
                        step(nc.vector.tensor_tensor(o.rearrange("p (a t) -> p a t", a=4),
                                                     bank((p, "mx", g)).rearrange("p (a t) -> p a t", a=4),
                                                     bs, ALU.add), ("read", (p, "mx", g)))
                        step(nc.vector.tensor_tensor(mixed[:, 4 + g, :], o, pair_of(qt, g), ALU.mult), (p, "sgu", g))
                else:
                    head_norm((p, "q"), 4, qt, lambda c: col("gq2"), lambda e: mat("cos_c")[:, 0:SEQ],
                              lambda e: mat("sin_c")[:, 0:SEQ])
                    head_norm((p, "k"), 2, kt, lambda c: col("gk2"), lambda e: mat("cos_c"), lambda e: mat("sin_c"))
                    attention((p, "at"), 16, 1, lambda t: 128 ** -0.5, False)
                T_ = TOK if l == 0 else SEQ
                update(p, ("out",), T_, gate(5))
                norm((*p, "f2"), T_, 2, gate(6))
                ffn2_((*p, "f2"), T_, gate(8))
                own()
            norm("fin", SEQ, None, None, lambda k: col("g_final", k))

    found = {"T": T.found, "A": A.found, "V": V.found}
    if found == known:
        assert not T.guessed + A.guessed + V.guessed
    return found, new_banks


def two(a):
    return a.rearrange("p (a t) -> p a t", a=2)


def pair_of(tile, c):
    return tile[:, 2 * c:2 * c + 2, :].rearrange("p a t -> p (a t)")


def vt_of(tile):
    return tile[:, :, :].rearrange("p (b e) t -> p b (e t)", b=4)


def v2_of(tile):
    return tile[:, :, :].rearrange("p e (b t) -> p (e b) t", b=2)


def transposed_order(p):
    return (0, 2, 1, 3) if p[0][0] == "b1" else (0, 1, 2, 3)


def out_step(p, s):
    return (p, "o", s // 2) if s % 2 else (p, "ov", s)


def x_step(p, *what):
    return ("read", (p, *what))


def hid_step(p, k, lo, hi):
    turns = (hi - lo) // PAIRS
    if k - lo < turns * PAIRS:
        return (p, "hid", lo + (k - lo) % PAIRS), (k - lo) // PAIRS
    return (p, "hid", k), None


def hid_at(hidr, width, which, j, i):
    at = which * FJ * TOK // 2 + j * width
    if i is None:
        return hidr[:, at:at + width]
    return hidr[:, bass.ds(i * (PAIRS * width) + at, width)]


def buffer_free(V, p, j, i, lo=0):
    if i is None:
        turns = (j - lo) // PAIRS
        if j - 2 - lo < turns * PAIRS:
            return V.at((p, "hid", lo + (j - 2 - lo) % PAIRS), (j - 2 - lo) // PAIRS)
        return V.at((p, "hid", j - 2))
    if j - lo >= 2:
        return V.at((p, "hid", j - 2), i)
    return V.at((p, "hid", j + PAIRS - 2), i - 1)


def _columns(a):
    return np.asarray(a).reshape(-1, P).T


def _constants():
    m = {}
    m["ones"] = np.ones((P, P))
    a = np.zeros((P, P))
    a[0:64, 0:64] = 1.0 / 64
    a[64:96, 64:96] = 1.0 / 32
    m["head_a"] = a
    b = np.zeros((P, P))
    b[0:64, 0:64] = b[64:128, 64:128] = 1.0 / 64
    m["head_b"] = b

    def rot(starts, half):
        r = np.zeros((P, P))
        for s in starts:
            for i in range(half):
                r[s + half + i, s + i] = -1.0
                r[s + i, s + half + i] = 1.0
        return r

    m["rot_a"] = rot((64,), 16)
    m["rot_b"] = rot((0, 64), 32)
    m["ident"] = np.eye(P)

    def dft(n):
        a = 2 * np.pi * (np.outer(np.arange(n), np.arange(n)) % n) / n
        return np.cos(a) / np.sqrt(n), np.sin(a) / np.sqrt(n)

    c, s = dft(P)
    m["dft_c"] = np.concatenate([c, s], 1)
    c, s = dft(SEQ)
    m["cos_n"] = np.concatenate([c[0:P], c[P:]], 1)
    m["nsin_n"] = -np.concatenate([s[0:P], s[P:]], 1)
    inv = THETA ** (-np.arange(0, 64, 2, dtype=np.float32) / np.float32(64))
    row = np.repeat(np.arange(SEQ // GRID_W), GRID_W).astype(np.float32)
    colm = np.tile(np.arange(GRID_W), SEQ // GRID_W).astype(np.float32)
    ang = np.concatenate([np.tile((row[:, None] * inv).T, (2, 1)), np.tile((colm[:, None] * inv).T, (2, 1))], 0)
    m["cos_c"] = np.concatenate([np.cos(ang), np.ones((P, SEQ))], 1)
    m["sin_c"] = np.concatenate([np.sin(ang), np.zeros((P, SEQ))], 1)
    mask = np.zeros((P, 2, SEQ))
    for q in range(2):
        mask[:, q, :] = np.where(np.arange(SEQ)[None] <= (q * P + np.arange(P))[:, None], 0.0, MASKED)
    m["mask"] = mask.reshape(P, 2 * SEQ)
    pick1, pick2 = np.zeros((P, 2)), np.zeros((P, 4))
    for k in range(2):
        for r in range(2):
            t = 32 * (2 * k + r)
            pick1[t, r] = 1.0
            pick2[t + 1, 2 * r] = pick2[t + 2, 2 * r + 1] = 1.0
    m["pick1"], m["pick2"] = pick1, pick2
    return {k: v.astype(np.float32) for k, v in m.items()}


def _pack(w):
    f = np.float32
    mats = {}
    o = np.cumsum([0, Q_RANK, KV_RANK, ROPE_A, 512, 512, 512, 512, 512, D, D, D])
    for l in range(DEPTH):
        mats[f"mod1_{l}"] = w["w_mod"][l]
        mats[f"mod2_{l}"] = w["w_mod_2"][l]
        wi = w["w_in"][l]
        rope = np.zeros((D, P), f)
        rope[:, 64:96] = wi[:, o[2]:o[3]]
        mats[f"lat_{l}"] = np.concatenate([wi[:, o[0]:o[2]], rope], 1)
        uq = np.zeros((Q_RANK, HEADS, P), f)
        uq[:, :, 0:96] = w["w_uq"][l].reshape(Q_RANK, HEADS, 96)
        mats[f"uq_{l}"] = uq.reshape(Q_RANK, HEADS * P)
        kv = w["w_ukv"][l].reshape(KV_RANK, HEADS, P)
        uk = np.zeros((KV_RANK, HEADS, P), f)
        uk[:, :, 0:64] = kv[:, :, 0:64]
        mats[f"uk_{l}"] = uk.reshape(KV_RANK, HEADS * P)
        mats[f"uv_{l}"] = kv[:, :, 64:128].reshape(KV_RANK, 512)
        mats[f"qkb_{l}"] = wi[:, o[3]:o[5]]
        mats[f"vb_{l}"] = wi[:, o[5]:o[6]]
        mats[f"conv_{l}"] = wi[:, o[6]:o[8]].reshape(D, 2, CC, P).transpose(0, 2, 1, 3).reshape(D, D)
        for n in range(3):
            mats[f"gate{n}_{l}"] = wi[:, o[8 + n]:o[9 + n]]
        mats[f"pw2_{l}"] = w["w_conv_pw2"][l]
        mats[f"oa_{l}"] = w["w_mla_o"][l]
        mats[f"ob_{l}"] = w["w_moba_o"][l]
        mats[f"out_{l}"] = w["w_out"][l]
        mats[f"up_{l}"] = w["w_up"][l].reshape(D, 2, FJ, P).transpose(0, 2, 1, 3).reshape(D, 2 * D_FF)
        mats[f"down_{l}"] = w["w_down"][l]
        for n in (1, 2):
            gu = np.zeros((D, 2, D_FF), f)
            gu[:, :, 0:D_FF_2] = w[f"w_ffn{n}_gu_2"][l].reshape(D, 2, D_FF_2)
            mats[f"f{n}up_{l}"] = gu.reshape(D, 2, FJ, P).transpose(0, 2, 1, 3).reshape(D, 2 * D_FF)
            dn = np.zeros((D_FF, D), f)
            dn[0:D_FF_2] = w[f"w_ffn{n}_down_2"][l]
            mats[f"f{n}down_{l}"] = dn
    wab = w["w_in_ab_2"][0]
    mats["ain"], mats["uin"], mats["vin"] = wab[:, 0:512], wab[:, 512:1024], wab[:, 1024:1536]
    mats["oab"] = w["w_out_ab_2"][0]
    qkv = w["w_qkv_2"][0]
    mats["q2"], mats["k2"], mats["v2"] = qkv[:, 0:1024], qkv[:, 1024:1280], qkv[:, 1280:1536]
    mats["o2"] = w["w_o_2"][0]

    blocks, _ = weight_blocks()
    stream = np.zeros((len(blocks) // UB, P, UB, P), f)
    for b, q in enumerate(blocks):
        if q is not None:
            name, k, n = q
            stream[b // UB, :, b % UB, :] = mats[name][k * P:(k + 1) * P, n * P:(n + 1) * P]

    vcol, vcols = vector_columns()
    cols = np.zeros((P, vcols), f)

    def put(name, a):
        s, n = vcol[name]
        cols[:, s:s + n] = a

    inv_a = (1.0 / (THETA ** (np.arange(0, 32, 2, dtype=f) / f(32)))).astype(f)
    inv_b = (1.0 / (THETA ** (np.arange(0, 64, 2, dtype=f) / f(64)))).astype(f)
    a = np.zeros((P, 1), f)
    a[64:96, 0] = np.tile(inv_a, 2)
    put("inv_freq_a", a)
    put("inv_freq_b", np.tile(inv_b, 4)[:, None])
    c = np.zeros((P, KD, 32), f)
    for n, a in enumerate((w["c"][0], w["c_2"][0], w["c_ctx_2"])):
        c[:, :, n] = _columns(a)
    put("c", c.reshape(P, KD * 32))
    put("eps", f(EPS))
    put("g_final", _columns(w["g_final_2"]))
    put("gq2", w["g_q_2"][0][:, None])
    put("gk2", w["g_k_2"][0][:, None])
    for l in range(DEPTH):
        put(f"b_mod1_{l}", _columns(w["b_mod"][l]))
        put(f"b_mod2_{l}", np.repeat(_columns(w["b_mod_2"][l]), 2, axis=1))
        put(f"g_mix1_{l}", _columns(w["mix_norm_g"][l]))
        put(f"g_ffn1_{l}", _columns(w["ffn_norm_g"][l]))
        put(f"g_qlat_{l}", _columns(w["mla_q_norm_g"][l]))
        put(f"g_kvlat_{l}", _columns(w["mla_kv_norm_g"][l]))
        for n, (a, b) in (("qa", ("mla_qn_nope_g", "mla_qn_rope_g")), ("ka", ("mla_kn_nope_g", "mla_kn_rope_g"))):
            g = np.zeros((P, 1), f)
            g[0:64, 0], g[64:96, 0] = w[a][l], w[b][l]
            put(f"g_{n}_{l}", g)
        put(f"g_qb_{l}", np.tile(w["moba_qn_g"][l], 2)[:, None])
        put(f"g_kb_{l}", np.tile(w["moba_kn_g"][l], 2)[:, None])
        put(f"conv_w_{l}", _columns(w["conv_dw_w"][l].reshape(-1)))
        put(f"conv_b_{l}", _columns(w["conv_dw_b"][l]))
        put(f"ln_g_{l}", _columns(w["conv_ln_g"][l]))
        put(f"ln_b_{l}", _columns(w["conv_ln_b"][l]))
        put(f"pw2_b_{l}", _columns(w["b_conv_pw2"][l]))
        put(f"ffn_w_{l}", _columns(w["ffn_dw_w"][l].reshape(-1)))
        put(f"ffn_b_{l}", _columns(w["ffn_dw_b"][l]))
        put(f"g2_{l}", np.concatenate([_columns(w[n][l]) for n in ("g_ffn1_2", "g_mix_2", "g_ffn2_2")], 1))

    ccol, ccols = const_columns()
    consts = np.zeros((P, ccols), f)
    made = _constants()
    for g in range(4):
        made[f"ws{g}"] = w["w_s_2"][0, g].T
    made["g_v"] = np.broadcast_to(w["g_v_2"][0].reshape(1, 512), (P, 512))
    made["b_s"] = np.broadcast_to(w["b_s_2"][0].reshape(1, 512), (P, 512))
    for name, (s, n) in ccol.items():
        consts[:, s:s + n] = made[name]
    return stream.reshape(-1, P, UB * P), cols, consts


def kernel(**inputs):
    import concourse.bacc as bacc
    from concourse.bass_utils import run_bass_kernel_spmd

    w = {k: np.asarray(v) for k, v in inputs.items()}
    stream, cols, consts = _pack(w)
    arrays = {
        "stream": stream, "columns": cols, "constants": consts,
        "x_in": np.ascontiguousarray(w["x"][0].T.reshape(KD, P, SEQ).transpose(1, 0, 2)),
        "ctx_in": np.ascontiguousarray(w["ctx_2"][0].T.reshape(KD, P, SEQ).transpose(1, 0, 2)),
        "positions_in": np.ascontiguousarray(np.broadcast_to(w["positions"].astype(np.int32), (P, SEQ))),
    }

    def program(known, banks):
        nc = bacc.Bacc("TRN2", target_bir_lowering=False, num_devices=1, dynamic_dma_scratch_size=1024)
        args = [nc.dram_tensor(k, a.shape, mybir.dt.from_np(a.dtype), kind="ExternalInput").ap()
                for k, a in arrays.items()]
        out = nc.dram_tensor("out", (P, KD, SEQ), F32, kind="ExternalOutput").ap()
        return nc, build(nc, *args, out, known, banks)

    found = ({}, {})
    while True:
        before = found
        nc, found = program(*before)
        if found == before:
            break
    r = run_bass_kernel_spmd(nc, [arrays], core_ids=[0])
    y = r.results[0]["out"]
    return y.transpose(2, 1, 0).reshape(1, SEQ, D)
```
